# Optimizing a Trainium2 kernel written in Bass

```python
import math
import jax
import jax.numpy as jnp
from jax import lax
import numpy as np

D_MODEL = 1024
BATCH = 1
SEQ = 256
DEPTH = 2

MEM_LEN = 256
EPS = 1e-6
MIX_WIDTH = D_MODEL
GROUP_WIDTH = MIX_WIDTH // 4

GLA_HEADS = 4
GLA_DV = GROUP_WIDTH // GLA_HEADS
GLA_DK = GLA_DV // 2
GLA_RANK = 16
GLA_TAU = 16.0
GLA_CHUNK = 64

POOL_WINDOWS = (2, 4, 8, 16)
POOL_GROUPS = len(POOL_WINDOWS)
POOL_CG = GROUP_WIDTH // POOL_GROUPS

DSA_HEADS = 4
DSA_DH = GROUP_WIDTH // DSA_HEADS
IDX_HEADS = 8
IDX_DIM = 32
DSA_TOPK_MAX = 256
DSA_QBLOCK = 128

SGU_GROUPS = 4
SGU_CHUNK = 128
SGU_CG = GROUP_WIDTH // SGU_GROUPS

REL_BUCKETS = 32
REL_MAX_DIST = 128

XA_HEADS = 4
XA_DH = 64

D_FF = 2816
N_EXPERTS = 8
TOP_K = 2
D_FF_EXPERT = 3584

IN_SPLITS = (
    GLA_HEADS * GLA_DK, GLA_HEADS * GLA_DK, GROUP_WIDTH, GROUP_WIDTH, GLA_RANK,
    GROUP_WIDTH,
    GROUP_WIDTH, GROUP_WIDTH, GROUP_WIDTH, IDX_HEADS * IDX_DIM, IDX_DIM, IDX_HEADS,
    2 * GROUP_WIDTH,
)
IN_WIDTH = sum(IN_SPLITS)

kernel_name = 'hybrid_parallel_group_block'

F32 = jnp.float32

def rmsnorm(x, g):
    xf = x.astype(F32)
    y = xf * lax.rsqrt(jnp.mean(xf * xf, axis=-1, keepdims=True) + EPS)
    return (y * g.astype(F32)).astype(x.dtype)

def split_cols(z, sizes):
    outs, off = [], 0
    for s in sizes:
        outs.append(z[..., off:off + s])
        off += s
    return outs

def rel_bucket(dist):
    n = jnp.maximum(dist, 0)
    max_exact = REL_BUCKETS // 2
    nf = jnp.maximum(n, 1).astype(F32)
    large = max_exact + (jnp.log(nf / max_exact) / math.log(REL_MAX_DIST / max_exact)
                         * (REL_BUCKETS - max_exact)).astype(jnp.int32)
    large = jnp.minimum(large, REL_BUCKETS - 1)
    return jnp.where(n < max_exact, n, large)

def gla_mixer(q, k, v, g_out, a_low, wa2, ba, norm_g):
    B, T, _ = q.shape
    C = GLA_CHUNK
    N = T // C
    logit = (a_low @ wa2 + ba).astype(F32)
    log_a = jax.nn.log_sigmoid(logit) / GLA_TAU

    def heads(t, d):
        return t.reshape(B, N, C, GLA_HEADS, d).transpose(0, 3, 1, 2, 4).astype(F32)

    qh = heads(q, GLA_DK) * (GLA_DK ** -0.5)
    kh = heads(k, GLA_DK)
    vh = heads(v, GLA_DV)
    b = jnp.cumsum(heads(log_a, GLA_DK), axis=3)
    q_t = qh * jnp.exp(b)
    k_t = kh * jnp.exp(-b)
    causal = jnp.tril(jnp.ones((C, C), dtype=bool))
    att = jnp.where(causal, jnp.einsum('bhnik,bhnjk->bhnij', q_t, k_t), 0.0)
    o_intra = jnp.einsum('bhnij,bhnjv->bhniv', att, vh)
    b_last = b[:, :, :, -1:, :]
    chunk_kv = jnp.einsum('bhnck,bhncv->bhnkv', kh * jnp.exp(b_last - b), vh)
    decay = jnp.exp(b_last[:, :, :, 0, :])

    def step(S, inp):
        dec_n, kv_n = inp
        return S * dec_n[..., None] + kv_n, S

    S0 = jnp.zeros((B, GLA_HEADS, GLA_DK, GLA_DV), F32)
    _, S_start = lax.scan(step, S0, (jnp.moveaxis(decay, 2, 0), jnp.moveaxis(chunk_kv, 2, 0)))
    S_start = jnp.moveaxis(S_start, 0, 2)
    o = o_intra + jnp.einsum('bhnck,bhnkv->bhncv', q_t, S_start)
    o = o * lax.rsqrt(jnp.mean(o * o, axis=-1, keepdims=True) + EPS)
    o = o.transpose(0, 2, 3, 1, 4).reshape(B, T, GLA_HEADS * GLA_DV) * norm_g.astype(F32)
    return (o * jax.nn.silu(g_out.astype(F32))).astype(q.dtype)

def pool_mixer(u, w, b, scale):
    B, T, _ = u.shape
    uf = u.astype(F32)
    csum = jnp.concatenate([jnp.zeros((B, 1, GROUP_WIDTH), F32), jnp.cumsum(uf, axis=1)], axis=1)
    tpos = jnp.arange(T)
    outs = []
    for gi, win in enumerate(POOL_WINDOWS):
        c = csum[:, :, gi * POOL_CG:(gi + 1) * POOL_CG]
        hi = c[:, 1:]
        lo = jnp.pad(c[:, :T + 1 - win], ((0, 0), (win - 1, 0), (0, 0)))
        cnt = jnp.minimum(tpos + 1, win).astype(F32)[None, :, None]
        outs.append((hi - lo) / cnt - uf[:, :, gi * POOL_CG:(gi + 1) * POOL_CG])
    p = jnp.stack(outs, axis=2)
    y = jnp.einsum('btgc,gcd->btgd', p, w.astype(F32)) + b.astype(F32)
    return (y.reshape(B, T, GROUP_WIDTH) * scale.astype(F32)).astype(u.dtype)

def dsa_mixer(q, k, v, qi, ki, wi, rel_bias):
    B, T, _ = q.shape
    topk = min(DSA_TOPK_MAX, T // 4)
    n_blk = T // DSA_QBLOCK
    qh = q.reshape(B, T, DSA_HEADS, DSA_DH)
    kh = k.reshape(B, T, DSA_HEADS, DSA_DH)
    vh = v.reshape(B, T, DSA_HEADS, DSA_DH)
    qih = qi.reshape(B, T, IDX_HEADS, IDX_DIM)
    kif = ki.astype(F32)
    w_idx = wi.astype(F32) * (IDX_HEADS ** -0.5)
    spos = jnp.arange(T)
    gather = jax.vmap(lambda arr, idx: arr[idx])

    def block(blk):
        t0 = blk * DSA_QBLOCK
        tpos = t0 + jnp.arange(DSA_QBLOCK)
        q_b = lax.dynamic_slice_in_dim(qh, t0, DSA_QBLOCK, axis=1).astype(F32)
        qi_b = lax.dynamic_slice_in_dim(qih, t0, DSA_QBLOCK, axis=1).astype(F32)
        w_b = lax.dynamic_slice_in_dim(w_idx, t0, DSA_QBLOCK, axis=1)
        dots = jnp.einsum('bqhd,bsd->bqsh', qi_b, kif) * (IDX_DIM ** -0.5)
        score = jnp.einsum('bqsh,bqh->bqs', jax.nn.relu(dots), w_b)
        visible = spos[None, :] <= tpos[:, None]
        score = jnp.where(visible[None], score, -jnp.inf)
        _, sel = lax.top_k(score, topk)
        k_sel = gather(kh, sel).astype(F32)
        v_sel = gather(vh, sel).astype(F32)
        dist = tpos[None, :, None] - sel
        bias = rel_bias[rel_bucket(dist)].astype(F32)
        logits = jnp.einsum('bqhd,bqkhd->bqkh', q_b, k_sel) * (DSA_DH ** -0.5) + bias
        logits = jnp.where((dist >= 0)[..., None], logits, -jnp.inf)
        p = jax.nn.softmax(logits, axis=2)
        return jnp.einsum('bqkh,bqkhd->bqhd', p, v_sel).astype(q.dtype)

    out = lax.map(block, jnp.arange(n_blk))
    return out.transpose(1, 0, 2, 3, 4).reshape(B, T, DSA_HEADS * DSA_DH)

def sgu_mixer(zuv, ln_g, ln_b, w_s, b_s):
    B, T, _ = zuv.shape
    z = jax.nn.gelu(zuv.astype(F32))
    u, v = z[..., :GROUP_WIDTH], z[..., GROUP_WIDTH:]
    mu = jnp.mean(v, axis=-1, keepdims=True)
    var = jnp.mean(jnp.square(v - mu), axis=-1, keepdims=True)
    vn = (v - mu) * lax.rsqrt(var + EPS) * ln_g.astype(F32) + ln_b.astype(F32)
    vn = vn.reshape(B, T // SGU_CHUNK, SGU_CHUNK, SGU_GROUPS, SGU_CG)
    ws = w_s.astype(F32) * jnp.tril(jnp.ones((SGU_CHUNK, SGU_CHUNK), F32))
    mixed = jnp.einsum('gts,bnsgc->bntgc', ws, vn) + b_s.astype(F32).T[None, None, :, :, None]
    return (u * mixed.reshape(B, T, GROUP_WIDTH)).astype(zuv.dtype)

def hybrid_mixer(hn, w_in, gla_wa2, gla_ba, gla_norm, pool_w, pool_b, pool_scale,
                 sgu_ln_g, sgu_ln_b, sgu_w, sgu_b, w_out, rel_bias):
    z = hn @ w_in
    (a_q, a_k, a_v, a_g, a_lr, b_u, c_q, c_k, c_v, c_qi, c_ki, c_wi, d_uv) = split_cols(z, IN_SPLITS)
    o_a = gla_mixer(a_q, a_k, a_v, a_g, a_lr, gla_wa2, gla_ba, gla_norm)
    o_b = pool_mixer(b_u, pool_w, pool_b, pool_scale)
    o_c = dsa_mixer(c_q, c_k, c_v, c_qi, c_ki, c_wi, rel_bias)
    o_d = sgu_mixer(d_uv, sgu_ln_g, sgu_ln_b, sgu_w, sgu_b)
    return jnp.concatenate([o_a, o_b, o_c, o_d], axis=-1) @ w_out

def cross_attn(hn, mem, norm_mem, wq, wkv, wo):
    B, T, _ = hn.shape
    q = (hn @ wq).reshape(B, T, XA_HEADS, XA_DH).astype(F32)
    kv = rmsnorm(mem, norm_mem) @ wkv
    M = mem.shape[1]
    k = kv[..., :XA_HEADS * XA_DH].reshape(B, M, XA_HEADS, XA_DH).astype(F32)
    v = kv[..., XA_HEADS * XA_DH:].reshape(B, M, XA_HEADS, XA_DH).astype(F32)
    p = jax.nn.softmax(jnp.einsum('bthd,bmhd->bhtm', q, k) * (XA_DH ** -0.5), axis=-1)
    o = jnp.einsum('bhtm,bmhd->bthd', p, v).reshape(B, T, XA_HEADS * XA_DH).astype(hn.dtype)
    return o @ wo

def swiglu(h, w1, w3, w2):
    return (jax.nn.silu(h @ w1) * (h @ w3)) @ w2

def moe_swiglu(h, router, w1, w3, w2):
    logits = (h @ router).astype(F32)
    top_v, top_i = lax.top_k(logits, TOP_K)
    gates = jax.nn.softmax(top_v, axis=-1)
    dense_gate = jnp.sum(jax.nn.one_hot(top_i, N_EXPERTS, dtype=F32) * gates[..., None], axis=-2)
    y = jnp.zeros(h.shape, F32)
    for e in range(N_EXPERTS):
        y = y + swiglu(h, w1[e], w3[e], w2[e]).astype(F32) * dense_gate[..., e:e + 1]
    return y.astype(h.dtype)

def setup_inputs(seed: int = 0) -> dict:
    key = jax.random.key(seed)
    ks = jax.random.split(key, 30)
    n_dense = (DEPTH + 1) // 2
    n_moe = DEPTH // 2

    def nrm(k, shape, fan_in):
        return jax.random.normal(k, shape, F32) * (fan_in ** -0.5)

    def gain(k, shape):
        return 1.0 + 0.05 * jax.random.normal(k, shape, F32)

    def small(k, shape):
        return 0.02 * jax.random.normal(k, shape, F32)

    return {
        'x': jax.random.normal(ks[0], (BATCH, SEQ, D_MODEL), F32),
        'mem': jax.random.normal(ks[1], (BATCH, MEM_LEN, D_MODEL), F32),
        'rel_bias': 0.5 * jax.random.normal(ks[2], (REL_BUCKETS, DSA_HEADS), F32),
        'final_norm': gain(ks[3], (D_MODEL,)),
        'norm_mix': gain(ks[4], (DEPTH, D_MODEL)),
        'w_in': nrm(ks[5], (DEPTH, D_MODEL, IN_WIDTH), D_MODEL),
        'gla_wa2': nrm(ks[6], (DEPTH, GLA_RANK, GLA_HEADS * GLA_DK), GLA_RANK),
        'gla_ba': small(ks[7], (DEPTH, GLA_HEADS * GLA_DK)),
        'gla_norm': gain(ks[8], (DEPTH, GROUP_WIDTH)),
        'pool_w': nrm(ks[9], (DEPTH, POOL_GROUPS, POOL_CG, POOL_CG), POOL_CG),
        'pool_b': small(ks[10], (DEPTH, POOL_GROUPS, POOL_CG)),
        'pool_scale': gain(ks[11], (DEPTH, GROUP_WIDTH)),
        'sgu_ln_g': gain(ks[12], (DEPTH, GROUP_WIDTH)),
        'sgu_ln_b': small(ks[13], (DEPTH, GROUP_WIDTH)),
        'sgu_w': nrm(ks[14], (DEPTH, SGU_GROUPS, SGU_CHUNK, SGU_CHUNK), SGU_CHUNK),
        'sgu_b': gain(ks[15], (DEPTH, SGU_GROUPS, SGU_CHUNK)),
        'w_out': nrm(ks[16], (DEPTH, MIX_WIDTH, D_MODEL), MIX_WIDTH),
        'norm_xa': gain(ks[17], (DEPTH, D_MODEL)),
        'norm_mem': gain(ks[18], (DEPTH, D_MODEL)),
        'xa_wq': nrm(ks[19], (DEPTH, D_MODEL, XA_HEADS * XA_DH), D_MODEL),
        'xa_wkv': nrm(ks[20], (DEPTH, D_MODEL, 2 * XA_HEADS * XA_DH), D_MODEL),
        'xa_wo': nrm(ks[21], (DEPTH, XA_HEADS * XA_DH, D_MODEL), XA_HEADS * XA_DH),
        'norm_ffn': gain(ks[22], (DEPTH, D_MODEL)),
        'ffn_w1': nrm(ks[23], (n_dense, D_MODEL, D_FF), D_MODEL),
        'ffn_w3': nrm(ks[24], (n_dense, D_MODEL, D_FF), D_MODEL),
        'ffn_w2': nrm(ks[25], (n_dense, D_FF, D_MODEL), D_FF),
        'router': nrm(ks[26], (n_moe, D_MODEL, N_EXPERTS), D_MODEL),
        'moe_w1': nrm(ks[27], (n_moe, N_EXPERTS, D_MODEL, D_FF_EXPERT), D_MODEL),
        'moe_w3': nrm(ks[28], (n_moe, N_EXPERTS, D_MODEL, D_FF_EXPERT), D_MODEL),
        'moe_w2': nrm(ks[29], (n_moe, N_EXPERTS, D_FF_EXPERT, D_MODEL), D_FF_EXPERT),
    }

def reference(x, mem, rel_bias, final_norm, norm_mix, w_in, gla_wa2, gla_ba, gla_norm,
              pool_w, pool_b, pool_scale, sgu_ln_g, sgu_ln_b, sgu_w, sgu_b, w_out,
              norm_xa, norm_mem, xa_wq, xa_wkv, xa_wo, norm_ffn,
              ffn_w1, ffn_w3, ffn_w2, router, moe_w1, moe_w3, moe_w2):
    h = x
    for i in range(DEPTH):
        h = h + hybrid_mixer(rmsnorm(h, norm_mix[i]), w_in[i], gla_wa2[i], gla_ba[i], gla_norm[i],
                             pool_w[i], pool_b[i], pool_scale[i], sgu_ln_g[i], sgu_ln_b[i],
                             sgu_w[i], sgu_b[i], w_out[i], rel_bias)
        h = h + cross_attn(rmsnorm(h, norm_xa[i]), mem, norm_mem[i], xa_wq[i], xa_wkv[i], xa_wo[i])
        hn = rmsnorm(h, norm_ffn[i])
        j = i // 2
        if i % 2 == 0:
            h = h + swiglu(hn, ffn_w1[j], ffn_w3[j], ffn_w2[j])
        else:
            h = h + moe_swiglu(hn, router[j], moe_w1[j], moe_w3[j], moe_w2[j])
    return rmsnorm(h, final_norm)


_drawn_inputs = setup_inputs


def setup_inputs(seed=0):
    import zlib

    import numpy as np

    out = dict(_drawn_inputs(seed))
    spreads = {}
    factors = {'gla_ba': 3.495, 'sgu_ln_b': 2.947, 'norm_xa': 3.422, 'norm_mem': 2.668}
    for name, (base, spread) in spreads.items():
        noise = np.random.default_rng([zlib.crc32(name.encode()), seed]).standard_normal(out[name].shape)
        drawn = base * np.exp(spread * noise) if base else spread * noise
        out[name] = jnp.asarray(drawn.astype(out[name].dtype))
    for name, factor in factors.items():
        out[name] = (out[name] * factor).astype(out[name].dtype)
    return out
```

```python
import math
from contextlib import ExitStack

import numpy as np

import concourse.bass as bass
from concourse import mybir

P = 128
F32 = mybir.dt.float32
I32 = mybir.dt.int32
U8 = mybir.dt.uint8
ALU = mybir.AluOpType
ACT = mybir.ActivationFunctionType
AX = mybir.AxisListType.X

SEQ, D, DEPTH, MEM = 256, 1024, 2, 256
TT = SEQ // P
KT = D // P
GW = 256
EPS = 1e-6
HEADS = 4
GLA_DK, GLA_DV, GLA_RANK, CHUNK = 32, 64, 16, 64
IDX_HEADS, IDX_DIM, TOPK = 8, 32, 64
DH = 64
WINDOWS = (2, 4, 8, 16)
PAD = 16
N_EXP, FE, FF = 8, 3584, 2816
BUCKETS, MAX_DIST = 32, 128
IN_W = 2616
RING = 7
LAYER_TURNS = 5
JOB_TURNS = 3
FC = 512
NCH = FE // FC
MAX_JOBS = N_EXP + 3
FFN_TILES = (4, 3, 3, 3, 3, 3, 3)
NEG, MARK, HALF = -3.0e38, -3.4e38, -3.2e38

C_AQ, C_AV, C_AG, C_LR, C_BU = 0, 256, 512, 768, 784
C_CQ, C_CK, C_CV, C_QI, C_KI, C_WI, C_UV = 1040, 1296, 1552, 1808, 2064, 2096, 2104
IN_UNITS = ((C_QI, C_UV), (0, 512), (C_AG, C_BU), (C_CQ, C_CV), (C_CV, C_QI), (C_BU, C_CQ), (C_UV, IN_W))
U_QI, U_A, U_AG, U_CQ, U_CV, U_BU, U_UV = range(7)
U_WKV, U_WOUT, U_WQ, U_WO = 0, 1, 5, 6
WOUT_ORDER = (1, 0, 3, 2)

R_MIX, R_XA, R_MEM, R_FFN, R_BA, R_PB, R_PS, R_SB, N_ROWS = 0, 8, 16, 24, 32, 33, 35, 37, 41

CONST = {}
_at = 0
for _name, _w in (("ident", P), ("vis", 256), ("reset", 256), ("bd", 256), ("tril", P), ("inv", 512),
                  ("before", P), ("ones", P), ("iota", P), ("eidx", 8), ("erev", 8)):
    CONST[_name] = (_at, _at + _w)
    _at += _w
CONST_W = _at


def shape_constants():
    c = np.zeros((P, CONST_W), np.float32)
    r = np.arange(P)
    s = np.arange(256)

    def put(name, v):
        c[:, CONST[name][0]:CONST[name][1]] = v

    put("ident", np.eye(P))
    put("vis", np.where(s[None, :] <= P + r[:, None], 0.0, NEG))
    put("reset", np.where(s % CHUNK == 0, 0.0, 1.0)[None, :])
    put("bd", (r[:, None] // GLA_DK == s[None, :] // GLA_DV))
    put("tril", r[None, :] <= r[:, None])
    inv = np.zeros((P, 2, 256), np.float32)
    for g, w in enumerate(WINDOWS):
        inv[64 * (g % 2):64 * (g % 2) + 64, g // 2, :] = 1.0 / np.minimum(s + 1, w).astype(np.float32)
    put("inv", inv.reshape(P, 512))
    put("before", r[:, None] < r[None, :])
    put("ones", 1.0)
    put("iota", r[None, :])
    put("eidx", np.arange(8)[None, :])
    put("erev", 8 - np.arange(8)[None, :])
    gla = ((r[:, None] <= r[None, :]) & (r[:, None] // CHUNK == r[None, :] // CHUNK)).astype(np.int32)
    gla = np.ascontiguousarray(np.tile(gla[:, None, :], (1, HEADS, 1)).reshape(P, HEADS * P)).astype(np.float32)
    n = np.maximum(255 - np.arange(384), 0)
    exact = BUCKETS // 2
    nf = np.maximum(n, 1).astype(np.float32)
    large = exact + (np.log(nf / np.float32(exact)) / np.float32(math.log(MAX_DIST / exact))
                     * np.float32(BUCKETS - exact)).astype(np.int32)
    bucket = np.where(n < exact, n, np.minimum(large, BUCKETS - 1))
    onehot = (np.arange(BUCKETS)[:, None] == bucket[None, :]).astype(np.float32)
    flip = np.ascontiguousarray(np.eye(P, dtype=np.float32)[::-1])
    return c, gla, onehot, flip


def build(nc, A, out):
    ctx = ExitStack()
    with ctx:
        def sb(name, shape, dt=F32):
            return ctx.enter_context(nc.sbuf_tensor(name, shape, dt))

        def sem(name):
            return ctx.enter_context(nc.semaphore(name))

        ring = sb("ring", [P, RING, 4096])
        cst = sb("cst", [P, CONST_W])
        gmask = sb("gmask", [P, HEADS * P], U8)
        h = sb("h", [P, TT, D])
        xnT = sb("xnT", [P, KT, SEQ])
        mixT = xnT
        memT = sb("memT", [P, KT, MEM])
        bias = sb("bias", [P, HEADS, 256])
        r2 = sb("r2", [P, 2048])
        bc = sb("bc", [P, 3, GW])
        wsT = sb("wsT", [P, 4, P])
        pwbd = sb("pwbd", [P, 2, P])
        wa2 = sb("wa2", [GLA_RANK, P])
        prow = sb("prow", [N_ROWS, P])
        pcol = sb("pcol", [P, N_ROWS])
        routw = sb("routw", [P, KT, N_EXP])
        qidx = sb("qidx", [P, 1024])
        qT = sb("qT", [P, 2, SEQ])
        kT = sb("kT", [P, 2, SEQ])
        cv = sb("cv", [P, TT, GW])
        av = sb("av", [P, TT, GW])
        sg = sb("sg", [P, TT, GW])
        uvg = sb("uvg", [P, TT, 512])
        wis = sb("wis", [P, TT, IDX_HEADS])
        score = sb("score", [P, 2, 256])
        m8 = sb("m8", [P, 8])
        gla = sb("gla", [P, 1024])
        glab = sb("glab", [P, 512])
        kdec = sb("kdec", [P, 512])
        Sst = sb("Sst", [P, 3, GW])
        bu = sb("bu", [P, 2, PAD + SEQ])
        pw1 = sb("pw1", [P, 2, PAD + SEQ])
        pw2 = sb("pw2", [P, 2, PAD + SEQ])
        tick = sb("tick", [P, 2])
        zeros = sb("zeros", [P, GW])
        kxT = sb("kxT", [P, 2, MEM])
        vx = sb("vx", [P, 2, GW])
        st = sb("st", [P, 96])
        tabi = sb("tabi", [1, 16], I32)
        jobt = sb("jobt", [P, TT, 2, MAX_JOBS + 1])

        def cc(name, a=0, b=None):
            lo, hi = CONST[name]
            return cst[:, lo + a:hi if b is None else lo + b]

        ident = cc("ident")
        ps = [ctx.enter_context(nc.psum_tensor(f"bank{i}", [P, 512], F32)) for i in range(8)]

        def v3(t, a, b, x):
            return t[:, a:b].rearrange("p (x y) -> p x y", x=x)

        def xT(kt):
            return ps[kt // 2][:, 256 * (kt % 2):256 * (kt % 2) + 256]

        xr = v3(r2, 0, 2048, 2)
        rel = v3(r2, 0, 2048, 8)
        qbd = r2[:, 0:1024].rearrange("p (t h i) -> p t h i", t=2, h=4)
        attT = r2[:, 1024:2048].rearrange("p (t n) -> p t n", t=2)
        qiT = v3(qidx, 0, 512, 2)
        kiT = qidx[:, 512:768]
        lrT = qidx[0:GLA_RANK, 768:1024]
        aqT, akT, eb, enb = (gla[:, 256 * i:256 * i + 256] for i in range(4))
        la, bs = glab[:, 0:256], glab[:, 256:512]
        kdT, kdr = kdec[:, 0:256], v3(kdec, 256, 512, 2)
        lgm = [v3(r2, 1024, 1536, 4), v3(gla, 0, 1024, 4)]
        prb = [v3(r2, 1536, 2048, 4), v3(r2, 0, 1024, 4)]
        pT_mix = [v3(glab, 0, 512, 4), v3(qidx, 0, 1024, 8)]
        prx = [v3(r2, 0, 1024, 4), v3(r2, 1024, 2048, 4)]
        pT_x = [v3(qidx, 0, 1024, 8), v3(gla, 0, 1024, 8)]
        oc = v3(Sst[:, :, :].rearrange("p a b -> p (a b)"), 0, 512, 2)
        wsr = uvg[:, 0, :].rearrange("p (g s) -> p g s", g=4)
        osq = v3(kdec, 0, 512, 2)
        vn = uvg[:, :, 256:512]
        oxT = kT
        f_sil, f_act = v3(glab, 0, 512, 2), v3(kdec, 0, 512, 2)
        memf = memT[:, :, :].rearrange("p k m -> p (k m)")
        xnf = xnT[:, :, :].rearrange("p k m -> p (k m)")
        j_sil, j_act = v3(memf, 0, 1024, 2), v3(memf, 1024, 2048, 2)
        j_actT = xnf[:, 0:1024].rearrange("p (b f s) -> p b f s", b=2, f=4)
        yrow = xnf[:, 1024:2048]
        xg = v3(qidx, 0, 1024, KT)
        hot, hotg = v3(kdec, 0, 256, 2), v3(kdec, 256, 512, 2)
        hotgT = v3(glab, 0, 256, 2)
        fnorm = bias[:, :, :].rearrange("p h x -> p (h x)")
        hank = v3(qidx, 0, 1024, HEADS)

        ss, rs, ms = st[:, 0:2], st[:, 2:4], st[:, 4:6]
        s_mx, s_sum, s_rec = st[:, 8:16], st[:, 16:24], st[:, 24:32]
        s_bn, s_ag, s_vm, s_vr = st[:, 32:44], st[:, 44:48], st[:, 48:50], st[:, 50:52]
        s_og, s_or = st[:, 52:60], st[:, 60:68]
        s_d, s_e, s_g = st[:, 68:70], st[:, 70:72], st[:, 72:76]

        names = """loaded_h loaded_mem loaded_const loaded_par loaded_fnorm bias_rows bias_hank stored v_chain a_chain
            g_chain bias_ps hank_ps bias_done h_upd ss_ready ms_ready rstd_ready xr_ready xT_ps xT_v xT_a
            par_free zeroed wkv_scaled pcol_ps pcol_done wsm_done ws_ps ws_done la_ready ls_ready b_ready
            eb_ready qe_ready r2_zero qbd_done kd_ready att_ps att_done kd_ps kdr_done kv_ps s_ready o_ps osq
            ms_gla r_gla og_done pool_out vms vr vn_done sg_ps od_done pt1_ps pt0_ps pt1_v pt1_a pt0_v pv_ps
            oc_done mt_ps mt_v mt_a xpv_ps ox_done xo_ps xo_done f_h f_s f_a  rlog_ps top_diff top_exp
            sel_ready rank_ps jobs_ready j_h1 j_h3 j_s j_a j_tps j_t j_yps j_yv j_ya j_g j_gps j_gtps j_gv j_ga
            j_gt j_c1 j_cv fin_ms fin_r fin scored dots_ps rel lg p xmx xp xpt_ps xpt_a lg_ps xlg_ps xpt_v""".split()
        S = {n: sem(n) for n in names}
        arrived = [sem(f"arrived{i}") for i in range(RING)]
        slot_free = [sem(f"slot_free{i}") for i in range(RING)]
        GROUPS = ("qi", "ki", "a", "av", "lr", "ag", "logit", "q", "k", "cv", "bu", "uv0", "uv1", "kx", "vx", "y", "xq", "wout", "xout")
        ENDS = {"ki": (U_QI, 0), "av": (U_A, 0), "ag": (U_AG, 0), "k": (U_CQ, 0), "cv": (U_CV, 0), "bu": (U_BU, 0),
                "uv1": (U_UV, 0), "vx": (U_WKV, 1), "xq": (U_WQ, 1), "wout": (U_WOUT + 3, 1), "xout": (U_WO, 1)}
        g_ps = {n: slot_free[ENDS[n][0]] if n in ENDS else sem(f"ps_{n}") for n in GROUPS}
        g_ev = {n: sem(f"ev_{n}") for n in GROUPS if n not in ("logit", "wout", "xout")}

        consts, glam, onehot, flip = A["consts"], A["glam"], A["onehot"], A["flip"]
        rev = nc.dram_tensor("bias_scratch", (HEADS, 384), F32, kind="Internal")
        block = ctx.enter_context(nc.Block())

        def chain(eng, s):
            n = [0]

            def link(ins):
                n[0] += 1
                ins.then_inc(s, 1)
                eng.wait_ge(s, n[0])

            def restart():
                n[0] = 0
                eng.sem_clear(s)
            return link, restart

        def rows(ap, n):
            return ap.rearrange("(r c) -> r c", c=P)

        @block.sync
        def _(sp):
            sp.dma_start(xr, A["mem"][0].rearrange("(t p) d -> p t d", p=P)).then_inc(S["loaded_mem"], 16)
            sp.dma_start(h[:, :, :], A["x"][0].rearrange("(t p) d -> p t d", p=P)).then_inc(S["loaded_h"], 16)
            sp.dma_start(cst[:, :], consts).then_inc(S["loaded_const"], 16)
            sp.dma_start(uvg[:, 1, :], glam).then_inc(S["loaded_const"], 16)
            sp.dma_start(routw[:, :, :], A["router"][0].rearrange("(k p) e -> p k e", p=P)).then_inc(S["loaded_const"], 16)
            sp.dma_start(gla[0:BUCKETS, 0:384], onehot).then_inc(S["loaded_const"], 16)
            sp.dma_start(kdec[0:BUCKETS, 0:HEADS], A["rel_bias"]).then_inc(S["loaded_const"], 16)
            sp.dma_start(glab[:, 0:P], flip).then_inc(S["loaded_const"], 16)

            with sp.Fori(0, DEPTH) as layer:
                lay = bass.ds(layer, 1)
                L1 = sp.snap(layer + 1)
                turn = [sp.snap(layer * LAYER_TURNS + (t + 1)) for t in range(LAYER_TURNS)]
                sp.wait_ge(S["par_free"], 1)
                sp.wait_ge(S["par_free"], L1)
                for name, row, n in (("norm_mix", R_MIX, 8), ("norm_xa", R_XA, 8), ("norm_mem", R_MEM, 8),
                                     ("norm_ffn", R_FFN, 8), ("gla_ba", R_BA, 1), ("pool_scale", R_PS, 2)):
                    sp.dma_start(prow[row:row + n, :], A[name][lay].rearrange("e (r c) -> (e r) c", c=P))\
                      .then_inc(S["loaded_par"], 16)
                sp.dma_start(prow[R_PB:R_PB + 2, :], A["pool_b"][lay].rearrange("e (r a) c -> (e r) (a c)", a=2))\
                  .then_inc(S["loaded_par"], 16)
                sp.dma_start(prow[R_SB:R_SB + 4, :], A["sgu_b"][lay].rearrange("e g t -> (e g) t"))\
                  .then_inc(S["loaded_par"], 16)
                for i, name in enumerate(("gla_norm", "sgu_ln_g", "sgu_ln_b")):
                    sp.dma_start(bc[:, i, :], A[name][lay].broadcast_to([P, GW])).then_inc(S["loaded_par"], 16)
                sp.dma_start(wa2[:, :], A["gla_wa2"][lay].rearrange("e r c -> (e r) c")).then_inc(S["loaded_par"], 16)
                sp.dma_start(wsr, A["sgu_w"][lay].rearrange("e g t s -> t (e g) s")).then_inc(S["loaded_par"], 16)
                for g in range(4):
                    r0 = 64 * (g % 2)
                    sp.dma_start(pwbd[r0:r0 + 64, g // 2, r0:r0 + 64],
                                 A["pool_w"][lay, g].rearrange("e c d -> (e c) d")).then_inc(S["loaded_par"], 16)

                def unit(t, s, dst, src):
                    sp.wait_ge(slot_free[s], 1)
                    sp.wait_ge(slot_free[s], turn[t])
                    sp.dma_start(dst, src).then_inc(arrived[s], 16)

                for s, (lo, hi) in enumerate(IN_UNITS):
                    unit(0, s, ring[:, s, 0:KT * (hi - lo)].rearrange("p (k c) -> p k c", k=KT),
                         A["w_in"][lay, :, lo:hi].rearrange("e (k p) c -> p (e k) c", p=P))
                unit(1, U_WKV, v3(ring[:, U_WKV, :], 0, 4096, KT),
                     A["xa_wkv"][lay].rearrange("e (k p) c -> p (e k) c", p=P))
                for i, m in enumerate(WOUT_ORDER):
                    unit(1, U_WOUT + i, v3(ring[:, U_WOUT + i, :], 0, 2048, 2),
                         A["w_out"][lay, 256 * m:256 * m + 256, :].rearrange("e (k p) c -> p (e k) c", p=P))
                unit(1, U_WQ, v3(ring[:, U_WQ, :], 0, 2048, KT),
                     A["xa_wq"][lay].rearrange("e (k p) c -> p (e k) c", p=P))
                unit(1, U_WO, v3(ring[:, U_WO, :], 0, 2048, 2),
                     A["xa_wo"][lay].rearrange("e (k p) c -> p (e k) c", p=P))
                with sp.If(layer < 1):
                    f0 = 0
                    for c, n in enumerate(FFN_TILES):
                        for w, name in enumerate(("ffn_w1", "ffn_w3")):
                            u = 3 * c + w
                            unit(2 + u // RING, u % RING, v3(ring[:, u % RING, :], 0, KT * n * P, KT),
                                 A[name][0, :, P * f0:P * (f0 + n)].rearrange("(k p) c -> p k c", p=P))
                        u = 3 * c + 2
                        unit(2 + u // RING, u % RING, v3(ring[:, u % RING, :], 0, n * D, n),
                             A["ffn_w2"][0, P * f0:P * (f0 + n), :].rearrange("(k p) c -> p k c", p=P))
                        f0 += n

            def job_loads(j, e):
                turns = [sp.snap(j * JOB_TURNS + (2 * LAYER_TURNS - 3 + t + 1)) for t in range(JOB_TURNS)]
                ex = bass.ds(e, 1)
                for c in range(NCH):
                    for w, name in enumerate(("moe_w1", "moe_w3")):
                        u = 3 * c + w
                        sp.wait_ge(slot_free[u % RING], 1)
                        sp.wait_ge(slot_free[u % RING], turns[u // RING])
                        sp.dma_start(v3(ring[:, u % RING, :], 0, 4096, KT),
                                     A[name][0, ex, :, FC * c:FC * c + FC].rearrange("e (k p) c -> p (e k) c", p=P))\
                          .then_inc(arrived[u % RING], 16)
                    u = 3 * c + 2
                    sp.wait_ge(slot_free[u % RING], 1)
                    sp.wait_ge(slot_free[u % RING], turns[u // RING])
                    sp.dma_start(v3(ring[:, u % RING, :], 0, 4096, 4),
                                 A["moe_w2"][0, ex, FC * c:FC * c + FC, :].rearrange("e (k p) c -> p (e k) c", p=P))\
                      .then_inc(arrived[u % RING], 16)

            sp.wait_ge(S["par_free"], DEPTH + 1)
            sp.dma_start(fnorm, A["final_norm"].rearrange("(e d) -> e d", e=1).broadcast_to([P, D]))\
              .then_inc(S["loaded_fnorm"], 16)
            with sp.Fori(0, N_EXP) as j:
                job_loads(j, j)
            sp.wait_ge(S["jobs_ready"], 1)
            n_jobs = sp.value_load(tabi[0:1, 0:1], min_val=N_EXP, max_val=MAX_JOBS)
            with sp.If(n_jobs > N_EXP):
                with sp.Fori(N_EXP, n_jobs) as j:
                    e = sp.value_load(tabi[0:1, bass.ds(j - (N_EXP - 1), 1)], min_val=0, max_val=N_EXP - 1)
                    job_loads(j, e)
            sp.wait_ge(S["fin"], 1)
            sp.dma_start(out[0].rearrange("(t p) d -> p t d", p=P), xr).then_inc(S["stored"], 16)
            sp.wait_ge(S["stored"], 16)

        @block.gpsimd
        def _(gp):
            link, restart = chain(gp, S["g_chain"])

            def take_wait():
                link(gp.tensor_tensor(tick[:, 0:1], tick[:, 1:2], tick[:, 1:2], ALU.add))
            link(gp.memset(tick[:, :], 0.0))
            gp.memset(zeros[:, :], 0.0).then_inc(S["zeroed"], 1)
            link(gp.memset(bu[:, :, 0:PAD], 0.0))
            link(gp.memset(pw1[:, :, 0:PAD], 0.0))
            link(gp.memset(pw2[:, :, 0:PAD], 0.0))
            gp.memset(pwbd[:, :, :], 0.0).then_inc(S["par_free"], 1)
            gp.wait_ge(S["zeroed"], 1)
            gp.wait_ge(S["loaded_const"], 96)
            link(gp.tensor_copy(gmask[:, :], uvg[:, 1, :]))
            with gp.Fori(0, DEPTH) as layer:
                L1 = gp.snap(layer + 1)
                first, second = gp.snap(layer * 2 + 1), gp.snap(layer * 2 + 2)
                landed1 = gp.snap(layer * (16 * LAYER_TURNS) + 32)
                restart()
                gp.wait_ge(S["scored"], second)
                take_wait()
                gp.memset(r2[:, :], 0.0).then_inc(S["r2_zero"], 1)
                gp.wait_ge(S["pcol_done"], L1)
                gp.wait_ge(arrived[U_WKV], landed1)
                take_wait()
                for k in range(KT):
                    w = ring[:, U_WKV, 512 * k:512 * k + 512]
                    i = gp.tensor_scalar(w, w, pcol[:, R_MEM + k:R_MEM + k + 1], None, ALU.mult)
                i.then_inc(S["wkv_scaled"], 1)
                gp.wait_ge(g_ev["bu"], L1)
                t1 = slice(PAD, PAD + SEQ)

                def shifted(k):
                    return slice(PAD - k, PAD + SEQ - k)
                inv = v3(cc("inv"), 0, 512, 2)

                def mean_less_self(src, p0, m):
                    link(gp.tensor_tensor(src[p0:p0 + 64, m, t1], src[p0:p0 + 64, m, t1], inv[p0:p0 + 64, m, :],
                                          ALU.mult))
                    return gp.tensor_tensor(bu[p0:p0 + 64, m, t1], src[p0:p0 + 64, m, t1], bu[p0:p0 + 64, m, t1],
                                            ALU.subtract)
                link(gp.tensor_tensor(pw1[:, :, t1], bu[:, :, t1], bu[:, :, shifted(1)], ALU.add))
                link(gp.tensor_tensor(pw2[:, :, t1], pw1[:, :, t1], pw1[:, :, shifted(2)], ALU.add))
                link(mean_less_self(pw1, 0, 0))
                link(mean_less_self(pw2, 64, 0))
                link(gp.tensor_tensor(pw1[:, 1, t1], pw2[:, 1, t1], pw2[:, 1, shifted(4)], ALU.add))
                link(gp.tensor_tensor(pw2[:, 1, t1], pw1[:, 1, t1], pw1[:, 1, shifted(8)], ALU.add))
                link(mean_less_self(pw1, 0, 1))
                mean_less_self(pw2, 64, 1).then_inc(S["pool_out"], 1)
                gp.wait_ge(S["pool_out"], L1)

        @block.scalar
        def _(act):
            link, restart = chain(act, S["a_chain"])

            def norm(src, junk, n, g0):
                link(act.activation(junk, src[:, 0, :], ACT.Square, accum_out=ss[:, 0:1]))
                act.activation(junk, src[:, 1, :], ACT.Square, accum_out=ss[:, 1:2]).then_inc(S["ss_ready"], 1)
                act.wait_ge(S["ms_ready"], n)
                act.activation(rs, ms, ACT.Sqrt).then_inc(S["rstd_ready"], 1)
                act.wait_ge(S["xT_ps"], n)
                dst = memT if g0 is None else xnT
                for kt in range(KT // 2, KT):
                    i = act.activation(dst[:, kt, :], xT(kt), ACT.Copy,
                                       scale=1.0 if g0 is None else pcol[:, g0 + kt:g0 + kt + 1])
                i.then_inc(S["xT_a"], 1)

            act.wait_ge(S["loaded_mem"], 16)
            norm(xr, xnf[:, 0:1024], 1, None)
            act.wait_ge(S["bias_ps"], 1)
            link(act.activation(gla[0:HEADS, 512:896], ps[4][0:HEADS, 0:384], ACT.Copy))
            act.dma_start(rev[:, :], gla[0:HEADS, 512:896]).then_inc(S["bias_rows"], 16)
            act.wait_ge(S["bias_rows"], 16)
            act.dma_start(hank, bass.AP(rev, 0, [[1, P], [384, HEADS], [1, 256]])).then_inc(S["bias_hank"], 16)
            act.wait_ge(S["hank_ps"], 1)
            for i2 in range(2):
                i = act.activation(bias[:, 2 * i2:2 * i2 + 2, :], v3(ps[5 + i2], 0, 512, 2), ACT.Copy)
            i.then_inc(S["bias_done"], 1)
            act.wait_ge(S["loaded_h"], 16)

            with act.Fori(0, DEPTH) as layer:
                L1 = act.snap(layer + 1)
                first, second = act.snap(layer * 2 + 1), act.snap(layer * 2 + 2)
                ended = [act.snap(layer * LAYER_TURNS + (t + 2)) for t in range(2)]

                def group(name):
                    act.wait_ge(g_ps[name], ended[ENDS[name][1]] if name in ENDS else L1)
                nv = [act.snap(layer * 3 + (u + 2)) for u in range(3)]
                hv = [act.snap(layer * 3 + (u + 1)) for u in range(3)]
                restart()

                def out_of(name, dst, src, func=ACT.Copy):
                    group(name)
                    act.activation(dst, src, func).then_inc(g_ev[name], 1)

                act.wait_ge(S["pcol_ps"], L1)
                act.activation(pcol[:, :], ps[7][:, 0:N_ROWS], ACT.Copy).then_inc(S["pcol_done"], 1)
                act.wait_ge(S["pcol_done"], L1)
                act.wait_ge(S["ws_ps"], L1)
                act.activation(wsT[:, :, :], v3(ps[6], 0, 512, 4), ACT.Copy).then_inc(S["ws_done"], 1)
                act.wait_ge(S["h_upd"], hv[0])
                norm(h, r2[:, 0:1024], nv[0], R_MIX)
                group("ki")
                for q in range(4):
                    act.activation(kiT[32 * q:32 * q + 32, :], ps[5][0:32, 0:256], ACT.Copy)
                act.activation(wis[:, :, :], v3(ps[5], 256, 272, 2), ACT.Copy,
                               scale=float(IDX_HEADS ** -0.5 * IDX_DIM ** -0.5)).then_inc(g_ev["ki"], 1)
                act.wait_ge(S["dots_ps"], first)
                for b in range(4):
                    i = act.activation(rel[:, b:8:4, :], v3(ps[b], 0, 512, 2), ACT.Relu)
                i.then_inc(S["rel"], 1)
                out_of("a", gla[:, 0:512], ps[6][:, :])
                out_of("av", av[:, :, :], v3(ps[7], 0, 512, 2))
                act.wait_ge(S["dots_ps"], second)
                act.wait_ge(S["scored"], first)
                for b in range(4):
                    i = act.activation(rel[:, b:8:4, 0:P], v3(ps[b], 0, 512, 2)[:, :, 0:P], ACT.Relu)
                i.then_inc(S["rel"], 1)
                out_of("ag", sg[:, :, :], v3(ps[5], 0, 512, 2), ACT.Silu)
                act.wait_ge(S["la_ready"], L1)
                link(act.activation(eb, la, ACT.Abs))
                link(act.activation(enb, eb, ACT.Exp, scale=-1.0))
                act.activation(eb, enb, ACT.Ln, bias=1.0).then_inc(S["ls_ready"], 1)
                act.wait_ge(S["b_ready"], L1)
                act.activation(eb, bs, ACT.Exp, scale=1.0 / 16.0)
                act.activation(enb, bs, ACT.Exp, scale=-1.0 / 16.0).then_inc(S["eb_ready"], 1)
                act.wait_ge(S["qe_ready"], L1)
                act.wait_ge(S["r2_zero"], L1)
                for q in range(4):
                    i = act.activation(qbd[32 * q:32 * q + 32, :, q, :],
                                       aqT[32 * q:32 * q + 32, :].rearrange("p (t i) -> p t i", t=2), ACT.Copy)
                i.then_inc(S["qbd_done"], 1)
                out_of("k", kT[:, :, :], v3(ps[4], 0, 512, 2))
                act.wait_ge(S["kd_ps"], L1)
                act.activation(kdr, v3(ps[2], 0, 256, 2), ACT.Copy).then_inc(S["kdr_done"], 1)
                out_of("bu", bu[:, :, PAD:PAD + SEQ], v3(ps[6], 0, 512, 2))
                out_of("uv0", uvg[:, 0, :], ps[7][:, :], ACT.Gelu_apprx_tanh)
                out_of("uv1", uvg[:, 1, :], ps[4][:, :], ACT.Gelu_apprx_tanh)
                act.wait_ge(S["vms"], L1)
                act.activation(s_vr, s_vm, ACT.Sqrt).then_inc(S["vr"], 1)
                out_of("kx", kxT[:, :, :], v3(ps[5], 0, 512, 2))
                act.wait_ge(S["o_ps"], L1)
                for t in range(TT):
                    i = act.activation(osq[:, t, :], ps[t][:, 0:256], ACT.Square)
                i.then_inc(S["osq"], 1)
                act.wait_ge(S["ms_gla"], L1)
                act.activation(s_or, s_og, ACT.Sqrt).then_inc(S["r_gla"], 1)
                for t in (1, 0):
                    act.wait_ge(S["lg"], first if t else second)
                    for hh in range(HEADS):
                        k = 4 * t + hh
                        i = act.activation(prb[t][:, hh, :], lgm[t][:, hh, :], ACT.Exp, bias=s_mx[:, k:k + 1],
                                           accum_out=s_sum[:, k:k + 1])
                    i.then_inc(S["p"], 1)
                act.wait_ge(S["pt1_ps"], L1)
                act.activation(pT_mix[1][:, 4:8, :], v3(ps[1], 0, 512, 4), ACT.Copy).then_inc(S["pt1_a"], 1)
                act.wait_ge(S["mt_ps"], L1)
                act.activation(mixT[:, 6:8, :], v3(ps[6], 0, 512, 2), ACT.Copy).then_inc(S["mt_a"], 1)

                act.wait_ge(S["h_upd"], hv[1])
                norm(h, r2[:, 0:1024], nv[1], R_XA)
                out_of("xq", qT[:, :, :], v3(ps[4], 0, 512, 2))
                for t in range(TT):
                    act.wait_ge(S["xmx"], second if t else first)
                    for hh in range(HEADS):
                        k = 4 * t + hh
                        c0 = 256 * (hh // 2)
                        i = act.activation(prx[t][:, hh, :], ps[2 * t + hh % 2][:, c0:c0 + 256], ACT.Exp,
                                           bias=s_mx[:, k:k + 1], scale=float(DH ** -0.5), accum_out=s_sum[:, k:k + 1])
                    i.then_inc(S["xp"], 1)
                for t in range(TT):
                    act.wait_ge(S["xpt_ps"], second if t else first)
                    act.activation(pT_x[t][:, 4:8, :], v3(ps[5 + 2 * t], 0, 512, 4), ACT.Copy)\
                       .then_inc(S["xpt_a"], 1)

                act.wait_ge(S["h_upd"], hv[2])
                norm(h, r2[:, 0:1024], nv[2], R_FFN)
                with act.If(layer < 1):
                    for f in range(FF // P):
                        act.wait_ge(S["f_h"], f + 1)
                        act.activation(f_sil[:, f % 2, :], ps[f % 2][:, 0:256], ACT.Silu).then_inc(S["f_s"], 1)

            act.wait_ge(S["top_diff"], 1)
            act.activation(s_e, s_d, ACT.Exp).then_inc(S["top_exp"], 1)
            act.wait_ge(S["jobs_ready"], 1)
            n_jobs = act.value_load(tabi[0:1, 0:1], min_val=N_EXP, max_val=MAX_JOBS)

            def gather_out(n):
                act.wait_ge(S["j_gps"], n)
                for kt in range(4, 8):
                    i = act.activation(xg[:, kt, :], ps[3][:, P * (kt - 4):P * (kt - 3)], ACT.Copy,
                                       scale=pcol[:, R_FFN + kt:R_FFN + kt + 1])
                i.then_inc(S["j_ga"], 1)

            def transposed(c, n):
                act.wait_ge(S["j_tps"], n)
                act.activation(j_actT[:, c % 2, :, :], v3(ps[4], 0, 512, 4), ACT.Copy).then_inc(S["j_t"], 1)

            gather_out(1)
            with act.Fori(0, n_jobs) as j:
                cn = [act.snap(j * NCH + (c + 1)) for c in range(NCH)]
                j1, j2 = act.snap(j + 1), act.snap(j + 2)
                for c in range(NCH):
                    act.wait_ge(S["j_h1"], cn[c])
                    act.activation(j_sil[:, c % 2, :], ps[2 * (c % 2)][:, :], ACT.Silu).then_inc(S["j_s"], 1)
                    if c:
                        transposed(c - 1, cn[c - 1])
                gather_out(j2)
                transposed(NCH - 1, cn[NCH - 1])
                act.wait_ge(S["j_yps"], j1)
                act.activation(yrow[:, 512:1024], ps[7][:, :], ACT.Copy).then_inc(S["j_ya"], 1)
            act.wait_ge(S["fin_ms"], 1)
            act.activation(rs, ms, ACT.Sqrt).then_inc(S["fin_r"], 1)

        @block.vector
        def _(dve):
            link, restart = chain(dve, S["v_chain"])
            mult, add, sub, amax, amin = ALU.mult, ALU.add, ALU.subtract, ALU.max, ALU.min

            def inverse_mean(dst, src, n):
                link(dve.tensor_scalar(dst, src, 1.0 / n, EPS, mult, add))
                return dve.reciprocal(dst, dst)

            def norm(src, n, g0):
                dve.wait_ge(S["ss_ready"], n)
                inverse_mean(ms, ss, D).then_inc(S["ms_ready"], 1)
                dve.wait_ge(S["rstd_ready"], n)
                for t in range(TT):
                    i = dve.tensor_scalar(xr[:, t, :], src[:, t, :], rs[:, t:t + 1], None, mult)
                i.then_inc(S["xr_ready"], 1)
                dve.wait_ge(S["xT_ps"], n)
                dst = memT if g0 is None else xnT
                for kt in range(KT // 2):
                    i = dve.tensor_scalar(dst[:, kt, :], xT(kt),
                                          1.0 if g0 is None else pcol[:, g0 + kt:g0 + kt + 1], None, mult)
                i.then_inc(S["xT_v"], 1)

            def add_rows(banks):
                for k, b in enumerate(banks):
                    dst = h[:, k // 2, 512 * (k % 2):512 * (k % 2) + 512]
                    i = dve.tensor_tensor(dst, dst, ps[b][:, :], add)
                return i

            dve.wait_ge(S["loaded_h"], 16)
            dve.sem_inc(S["h_upd"], 1)
            dve.wait_ge(S["loaded_mem"], 16)
            norm(xr, 1, None)

            with dve.Fori(0, DEPTH) as layer:
                L1 = dve.snap(layer + 1)
                first, second = dve.snap(layer * 2 + 1), dve.snap(layer * 2 + 2)
                ended = [dve.snap(layer * LAYER_TURNS + (t + 2)) for t in range(2)]

                def group(name):
                    dve.wait_ge(g_ps[name], ended[ENDS[name][1]] if name in ENDS else L1)
                nv = [dve.snap(layer * 3 + (u + 2)) for u in range(3)]
                par = dve.snap(layer * 272 + 272)
                restart()

                def out_of(name, dst, src):
                    group(name)
                    dve.tensor_copy(dst, src).then_inc(g_ev[name], 1)

                dve.wait_ge(S["loaded_const"], 96)
                dve.wait_ge(S["loaded_par"], par)
                for g in range(4):
                    i = dve.tensor_tensor(wsr[:, g, :], wsr[:, g, :], cc("tril"), mult)
                i.then_inc(S["wsm_done"], 1)
                dve.wait_ge(S["pcol_done"], L1)
                norm(h, nv[0], R_MIX)
                out_of("qi", qiT, v3(ps[4], 0, 512, 2))
                dve.wait_ge(g_ev["ki"], L1)

                def score_and_take(t, n):
                    sc = score[:, t, 0:n]
                    vis = cc("vis", 256 - n)
                    dve.wait_ge(S["rel"], first if t else second)
                    for hh in range(IDX_HEADS):
                        i = dve.scalar_tensor_tensor(sc, rel[:, hh, 0:n], wis[:, t, hh:hh + 1], vis if hh == 0 else sc,
                                                     mult, add)
                        if hh < IDX_HEADS - 1:
                            link(i)
                    link(i)
                    dve.memset(st[:, 95:96], 0.0).then_inc(S["scored"], 1)
                    for _ in range(TOPK // 8):
                        link(dve.max(m8[:, :], sc))
                        link(dve.match_replace(sc, m8[:, :], sc, MARK))
                    link(dve.tensor_scalar(sc, sc, HALF, -1.0e30, ALU.is_gt, mult))
                    link(dve.tensor_tensor(sc, sc, vis, add))

                score_and_take(1, 256)
                score_and_take(0, P)

                out_of("lr", lrT, ps[4][0:GLA_RANK, 0:256])
                group("logit")
                dve.tensor_scalar(la, ps[6][:, 0:256], pcol[:, R_BA:R_BA + 1], None, add).then_inc(S["la_ready"], 1)
                dve.wait_ge(S["ls_ready"], L1)
                link(dve.scalar_tensor_tensor(la, la, 0.0, eb, amin, sub))
                dve.tensor_tensor_scan(bs, cc("reset"), la, 0.0, mult, add).then_inc(S["b_ready"], 1)
                dve.wait_ge(S["eb_ready"], L1)
                dve.scalar_tensor_tensor(aqT, aqT, float(GLA_DK ** -0.5), eb, mult, mult).then_inc(S["qe_ready"], 1)
                link(dve.tensor_tensor(akT, akT, enb, mult))
                last = v3(eb, 0, 256, 4)[:, :, CHUNK - 1:CHUNK]
                dve.tensor_tensor(v3(kdT, 0, 256, 4), v3(akT, 0, 256, 4), last.broadcast_to([P, 4, CHUNK]), mult)\
                   .then_inc(S["kd_ready"], 1)
                out_of("q", qT[:, :, :], v3(ps[7], 0, 512, 2))
                out_of("cv", cv[:, :, :], v3(ps[5], 0, 512, 2))
                dve.wait_ge(S["att_ps"], L1)
                dve.wait_ge(S["r2_zero"], L1)
                dve.wait_ge(g_ev["ag"], L1)
                for t in range(TT):
                    link(dve.tensor_tensor(sg[:, t, :], sg[:, t, :], bc[:, 0, :], mult))
                for t in range(TT):
                    i = dve.copy_predicated(attT[:, t, :], gmask[:, :], ps[t][:, :])
                i.then_inc(S["att_done"], 1)
                for t in range(TT):
                    dve.wait_ge(g_ev[f"uv{t}"], L1)
                    link(dve.bn_stats(s_bn[:, 6 * t:6 * t + 6], uvg[:, t, 256:512]))
                    link(dve.bn_aggr(s_ag[:, 2 * t:2 * t + 2], s_bn[:, 6 * t:6 * t + 6]))
                inverse_mean(s_vm, s_ag[:, 1:4:2], 1).then_inc(S["vms"], 1)
                dve.wait_ge(S["kv_ps"], L1)
                kv = (ps[3][:, 0:256], ps[2][:, 256:512], ps[3][:, 256:512])
                for n in range(3):
                    link(dve.tensor_tensor(Sst[:, n, :], kv[n], cc("bd"), mult))
                for n in (1, 2):
                    e = CHUNK * (n + 1) - 1
                    i = dve.scalar_tensor_tensor(Sst[:, n, :], Sst[:, n - 1, :], eb[:, e:e + 1], Sst[:, n, :], mult, add)
                    if n == 1:
                        link(i)
                i.then_inc(S["s_ready"], 1)
                dve.wait_ge(S["vr"], L1)
                for t in range(TT):
                    link(dve.tensor_scalar(vn[:, t, :], vn[:, t, :], s_ag[:, 2 * t:2 * t + 1], s_vr[:, t:t + 1],
                                           sub, mult))
                    link(dve.tensor_tensor(vn[:, t, :], vn[:, t, :], bc[:, 1, :], mult))
                    i = dve.tensor_tensor(vn[:, t, :], vn[:, t, :], bc[:, 2, :], add)
                i.then_inc(S["vn_done"], 1)
                out_of("vx", vx[:, :, :], v3(ps[6], 0, 512, 2))
                dve.wait_ge(S["osq"], L1)
                link(dve.tensor_reduce(s_og, osq.rearrange("p t (h v) -> p (t h) v", h=HEADS), AX, add))
                inverse_mean(s_og, s_og, GLA_DV).then_inc(S["ms_gla"], 1)
                dve.wait_ge(S["r_gla"], L1)
                for t in range(TT):
                    i = dve.tensor_tensor(v3(sg[:, t, :], 0, 256, 4), v3(sg[:, t, :], 0, 256, 4),
                                          s_or[:, 4 * t:4 * t + 4].unsqueeze(2).broadcast_to([P, 4, GLA_DV]), mult)
                    link(i)
                for t in range(TT):
                    i = dve.tensor_tensor(sg[:, t, :], sg[:, t, :], ps[t][:, 0:256], mult)
                i.then_inc(S["og_done"], 1)
                dve.wait_ge(S["sg_ps"], L1)
                for t in range(TT):
                    for g in range(4):
                        dst = uvg[:, t, 64 * g:64 * g + 64]
                        i = dve.scalar_tensor_tensor(dst, ps[2 + t][:, 64 * g:64 * g + 64],
                                                     pcol[:, R_SB + g:R_SB + g + 1], dst, add, mult)
                i.then_inc(S["od_done"], 1)
                group("y")
                for m in range(2):
                    i = dve.tensor_scalar(mixT[:, 2 + m, :], ps[7][:, 256 * m:256 * m + 256],
                                          pcol[:, R_PB + m:R_PB + m + 1], pcol[:, R_PS + m:R_PS + m + 1], add, mult)
                i.then_inc(g_ev["y"], 1)
                dve.wait_ge(S["bias_done"], 1)
                for t, n in ((1, 256), (0, P)):
                    link(dve.tensor_tensor(lgm[t], bias[:, :, 256 - n:256],
                                           score[:, t, 0:n].unsqueeze(1).broadcast_to([P, HEADS, n]), add))
                    dve.wait_ge(S["lg_ps"], first if t else second)
                    for b in range(2):
                        bank = ps[4 + b if t else 6 + b]
                        link(dve.scalar_tensor_tensor(lgm[t][:, b:4:2, :], v3(bank, 0, 2 * n, 2), float(DH ** -0.5),
                                                      lgm[t][:, b:4:2, :], mult, add))
                    link(dve.tensor_reduce(s_mx[:, 4 * t:4 * t + 4], lgm[t], AX, amax))
                    dve.tensor_scalar(s_mx[:, 4 * t:4 * t + 4], s_mx[:, 4 * t:4 * t + 4], -1.0, None, mult)\
                       .then_inc(S["lg"], 1)
                dve.wait_ge(S["pt1_ps"], L1)
                dve.tensor_copy(pT_mix[1][:, 0:4, :], v3(ps[0], 0, 512, 4)).then_inc(S["pt1_v"], 1)
                dve.wait_ge(S["pt0_ps"], L1)
                dve.tensor_copy(pT_mix[0], v3(ps[2], 0, 512, 4)).then_inc(S["pt0_v"], 1)
                dve.wait_ge(S["p"], second)
                link(dve.reciprocal(s_rec, s_sum))
                dve.wait_ge(S["pv_ps"], L1)
                for t in range(TT):
                    i = dve.tensor_tensor(v3(oc[:, t, :], 0, 256, 4), v3(ps[3], 256 * t, 256 * t + 256, 4),
                                          s_rec[:, 4 * t:4 * t + 4].unsqueeze(2).broadcast_to([P, 4, DH]), mult)
                i.then_inc(S["oc_done"], 1)
                dve.wait_ge(S["mt_ps"], L1)
                dve.tensor_copy(mixT[:, 0:2, :], v3(ps[4], 0, 512, 2))
                dve.tensor_copy(mixT[:, 4:6, :], v3(ps[5], 0, 512, 2)).then_inc(S["mt_v"], 1)
                group("wout")
                add_rows((0, 1, 2, 3)).then_inc(S["h_upd"], 1)
                dve.wait_ge(S["h_upd"], nv[0])
                dve.sem_inc(S["par_free"], 1)

                norm(h, nv[1], R_XA)
                for t in range(TT):
                    dve.wait_ge(S["xlg_ps"], second if t else first)
                    for b in range(2):
                        link(dve.tensor_reduce(s_mx[:, 4 * t + b:4 * t + 4:2], v3(ps[2 * t + b], 0, 512, 2), AX, amax))
                    dve.tensor_scalar(s_mx[:, 4 * t:4 * t + 4], s_mx[:, 4 * t:4 * t + 4], -float(DH ** -0.5), None, mult)\
                       .then_inc(S["xmx"], 1)
                for t in range(TT):
                    dve.wait_ge(S["xpt_ps"], second if t else first)
                    dve.tensor_copy(pT_x[t][:, 0:4, :], v3(ps[4 + 2 * t], 0, 512, 4)).then_inc(S["xpt_v"], 1)
                dve.wait_ge(S["xp"], second)
                link(dve.reciprocal(s_rec, s_sum))
                dve.wait_ge(S["xpv_ps"], L1)
                for t in range(TT):
                    i = dve.tensor_tensor(v3(oc[:, t, :], 0, 256, 4), v3(ps[2 * t], 0, 256, 4),
                                          s_rec[:, 4 * t:4 * t + 4].unsqueeze(2).broadcast_to([P, 4, DH]), mult)
                i.then_inc(S["ox_done"], 1)
                dve.wait_ge(S["xo_ps"], L1)
                dve.tensor_copy(oxT[:, :, :], v3(ps[1], 0, 512, 2)).then_inc(S["xo_done"], 1)
                group("xout")
                add_rows((4, 5, 6, 7)).then_inc(S["h_upd"], 1)
                dve.wait_ge(S["h_upd"], nv[1])

                norm(h, nv[2], R_FFN)
                with dve.If(layer < 1):
                    for f in range(FF // P):
                        dve.wait_ge(S["f_s"], f + 1)
                        dve.tensor_tensor(f_act[:, f % 2, :], f_sil[:, f % 2, :], ps[f % 2][:, 256:512], mult)\
                           .then_inc(S["f_a"], 1)
                    dve.wait_ge(slot_free[RING - 1], LAYER_TURNS + 1)
                    add_rows((4, 5, 6, 7)).then_inc(S["h_upd"], 1)
                    dve.wait_ge(S["h_upd"], 4)

            restart()
            scf = score[:, :, :].rearrange("p a b -> p (a b)")

            def r3(i):
                return v3(scf, 16 * i, 16 * i + 16, 2)
            lg, eq, k1, lg2, k2, sel, gate, pos, tmp = (r3(i) for i in range(9))
            best = [scf[:, 160 + 2 * i:162 + 2 * i] for i in range(4)]

            def rep(v):
                return v.unsqueeze(2).broadcast_to([P, TT, N_EXP])

            def per_tile(v):
                return v.unsqueeze(1).broadcast_to([P, TT, N_EXP])
            dve.wait_ge(S["rlog_ps"], 1)
            link(dve.tensor_copy(lg, v3(ps[4], 0, 16, 2)))

            def first_best(src, top, first, hot1):
                link(dve.tensor_reduce(top, src, AX, amax))
                link(dve.tensor_tensor(eq, src, rep(top), ALU.is_equal))
                link(dve.tensor_tensor(eq, eq, per_tile(cc("erev")), mult))
                link(dve.tensor_reduce(first, eq, AX, amax))
                link(dve.tensor_tensor(hot1, eq, rep(first), ALU.is_equal))
            first_best(lg, best[0], best[1], k1)
            link(dve.scalar_tensor_tensor(lg2, k1, NEG, lg, mult, add))
            first_best(lg2, best[2], best[3], k2)
            dve.tensor_tensor(s_d, best[2], best[0], sub).then_inc(S["top_diff"], 1)
            dve.tensor_tensor(sel, k1, k2, add).then_inc(S["sel_ready"], 1)
            dve.wait_ge(S["top_exp"], 1)
            link(dve.tensor_scalar(s_g[:, 0:2], s_e, 1.0, None, add))
            link(dve.reciprocal(s_g[:, 0:2], s_g[:, 0:2]))
            link(dve.tensor_tensor(s_g[:, 2:4], s_e, s_g[:, 0:2], mult))
            link(dve.tensor_tensor(k1, k1, rep(s_g[:, 0:2]), mult))
            link(dve.tensor_tensor(k2, k2, rep(s_g[:, 2:4]), mult))
            link(dve.tensor_tensor(gate, k1, k2, add))
            dve.wait_ge(S["sel_ready"], 1)
            dve.wait_ge(S["rank_ps"], 1)
            link(dve.scalar_tensor_tensor(pos, sel, 1000.0, v3(ps[5], 0, 16, 2), mult, add))
            link(dve.tensor_scalar(pos, pos, 1000.0, None, sub))
            link(dve.memset(jobt[:, :, 0, MAX_JOBS:], -1.0))
            link(dve.memset(jobt[:, :, 1, MAX_JOBS:], 0.0))
            link(dve.tensor_copy(jobt[:, :, 0, 0:N_EXP], pos))
            link(dve.tensor_copy(jobt[:, :, 1, 0:N_EXP], gate))
            over, upto, pick, one = (scf[:, 192 + 8 * i:200 + 8 * i] for i in range(4))
            cnt = scf[:, 224:230]
            link(dve.tensor_scalar(over, ps[5][:, 16:24], float(P), None, ALU.is_gt))
            link(dve.tensor_tensor_scan(upto, cc("ones", 0, 8), over, 0.0, mult, add))
            for x in range(MAX_JOBS - N_EXP):
                link(dve.scalar_tensor_tensor(pick, upto, float(x + 1), over, ALU.is_equal, mult))
                for k, src in ((0, pos), (1, gate)):
                    link(dve.tensor_tensor(tmp, src, per_tile(pick), mult))
                    link(dve.tensor_reduce(cnt[:, 0:2], tmp, AX, add))
                    link(dve.tensor_scalar(jobt[:, :, k, N_EXP + x:N_EXP + x + 1], cnt[:, 0:2].unsqueeze(2),
                                           float(-P if k == 0 else 0), None, add))
                link(dve.tensor_tensor(one, pick, cc("eidx"), mult))
                link(dve.tensor_reduce(cnt[:, 3 + x:4 + x], one, AX, add))
            link(dve.tensor_scalar(cnt[:, 2:3], upto[:, 7:8], float(N_EXP), None, add))
            dve.tensor_copy(tabi[0:1, 0:4], cnt[0:1, 2:6]).then_inc(S["jobs_ready"], 1)
            dve.wait_ge(S["jobs_ready"], 1)
            n_jobs = dve.value_load(tabi[0:1, 0:1], min_val=N_EXP, max_val=MAX_JOBS)

            def slots_of(dst, j, gated):
                for t in range(TT):
                    i = dve.tensor_scalar(dst[:, t, :], cc("iota"), jobt[:, t, 0, bass.ds(j, 1)],
                                          jobt[:, t, 1, bass.ds(j, 1)] if gated else None,
                                          ALU.is_equal, mult if gated else ALU.bypass)
                return i

            def gather_out(n):
                dve.wait_ge(S["j_gps"], n)
                for kt in range(4):
                    i = dve.tensor_scalar(xg[:, kt, :], ps[2][:, P * kt:P * kt + P],
                                          pcol[:, R_FFN + kt:R_FFN + kt + 1], None, mult)
                i.then_inc(S["j_gv"], 1)

            slots_of(hot, 0, False).then_inc(S["j_g"], 1)
            gather_out(1)
            with dve.Fori(0, n_jobs) as j:
                cn = [dve.snap(j * NCH + (c + 1)) for c in range(NCH)]
                j1, j2 = dve.snap(j + 1), dve.snap(j + 2)
                dve.wait_ge(S["j_h1"], cn[0])
                slots_of(hotg, j, True)
                slots_of(hot, j1, False).then_inc(S["j_g"], 1)
                for c in range(NCH):
                    dve.wait_ge(S["j_s"], cn[c])
                    dve.wait_ge(S["j_h3"], cn[c])
                    dve.tensor_tensor(j_act[:, c % 2, :], j_sil[:, c % 2, :], ps[2 * (c % 2) + 1][:, :], mult)\
                       .then_inc(S["j_a"], 1)
                gather_out(j2)
                dve.wait_ge(S["j_gtps"], j1)
                dve.tensor_copy(hotgT, v3(ps[5], 0, 256, 2)).then_inc(S["j_gt"], 1)
                dve.wait_ge(S["j_yps"], j1)
                dve.tensor_copy(yrow[:, 0:512], ps[6][:, :]).then_inc(S["j_yv"], 1)
                dve.wait_ge(S["j_c1"], j1)
                add_rows((4, 5, 2, 3)).then_inc(S["j_cv"], 1)
                dve.wait_ge(S["j_cv"], j1)

            restart()
            for t in range(TT):
                link(dve.tensor_tensor_reduce(out=xr[:, t, :], in0=h[:, t, :], in1=h[:, t, :], scale=1.0, scalar=0.0,
                                              op0=mult, op1=add, accum_out=ss[:, t:t + 1]))
            inverse_mean(ms, ss, D).then_inc(S["fin_ms"], 1)
            dve.wait_ge(S["fin_r"], 1)
            dve.wait_ge(S["loaded_fnorm"], 16)
            for t in range(TT):
                i = dve.scalar_tensor_tensor(xr[:, t, :], h[:, t, :], rs[:, t:t + 1], fnorm, mult, mult)
            i.then_inc(S["fin"], 1)

        @block.tensor
        def _(pe):
            mm = pe.matmul

            def transposes(n):
                pe.wait_ge(S["xr_ready"], n)
                for kt in range(KT):
                    for t in range(TT):
                        c0 = 256 * (kt % 2) + P * t
                        i = pe.transpose(ps[kt // 2][:, c0:c0 + P], xr[:, t, P * kt:P * kt + P], ident)
                i.then_inc(S["xT_ps"], 1)
                pe.wait_ge(S["xT_v"], n)
                pe.wait_ge(S["xT_a"], n)

            def on_features(dst, w, src=xnT):
                for k in range(KT):
                    i = mm(dst, w[:, k, :], src[:, k, :], start=k == 0, stop=k == KT - 1)
                return i

            def on_tokens(dst, w, t, src=xnT):
                for k in range(KT):
                    i = mm(dst, src[:, k, P * t:P * t + P], w[:, k, :], start=k == 0, stop=k == KT - 1)
                return i

            pe.wait_ge(S["loaded_const"], 96)
            for s in range(RING):
                pe.sem_inc(slot_free[s], 1)
            transposes(1)
            mm(ps[4][0:HEADS, 0:384], kdec[0:BUCKETS, 0:HEADS], gla[0:BUCKETS, 0:384], start=True, stop=True)\
                .then_inc(S["bias_ps"], 1)
            pe.wait_ge(S["bias_hank"], 16)
            for i2 in range(2):
                i = mm(ps[5 + i2][:, :], glab[:, 0:P], hank[:, 2 * i2:2 * i2 + 2, :], start=True, stop=True)
            i.then_inc(S["hank_ps"], 1)
            pe.wait_ge(S["bias_done"], 1)

            with pe.Fori(0, DEPTH) as layer:
                L1 = pe.snap(layer + 1)
                first, second = pe.snap(layer * 2 + 1), pe.snap(layer * 2 + 2)
                nv = [pe.snap(layer * 3 + (u + 2)) for u in range(3)]
                par = pe.snap(layer * 272 + 272)
                landed = [pe.snap(layer * (16 * LAYER_TURNS) + 16 * (t + 1)) for t in range(LAYER_TURNS)]

                def w_in(u):
                    lo, hi = IN_UNITS[u]
                    return v3(ring[:, u, :], 0, KT * (hi - lo), KT)

                pe.wait_ge(S["loaded_par"], par)
                pe.wait_ge(S["wsm_done"], L1)
                for g in range(4):
                    i = pe.transpose(ps[6][:, P * g:P * g + P], wsr[:, g, :], ident)
                i.then_inc(S["ws_ps"], 1)
                pe.transpose(ps[7][:, 0:N_ROWS], prow[:, :], ident[0:N_ROWS, 0:N_ROWS]).then_inc(S["pcol_ps"], 1)
                transposes(nv[0])

                pe.wait_ge(S["pcol_done"], L1)
                pe.wait_ge(arrived[U_QI], landed[0])
                w = w_in(U_QI)
                for m in range(2):
                    i = on_features(ps[4][:, 256 * m:256 * m + 256], w[:, :, P * m:P * m + P])
                i.then_inc(g_ps["qi"], 1)
                on_features(ps[5][0:32, 0:256], w[:, :, 256:288])
                for t in range(TT):
                    i = on_tokens(ps[5][:, 256 + 8 * t:264 + 8 * t], w[:, :, 288:296], t)
                i.then_inc(g_ps["ki"], 1)

                def dots(t, n):
                    for hh in range(IDX_HEADS):
                        r0 = 32 * (hh % 4)
                        c0 = 256 * (hh // 4)
                        i = mm(ps[hh % 4][:, c0:c0 + n], qiT[r0:r0 + 32, hh // 4, P * t:P * t + P],
                               kiT[r0:r0 + 32, 0:n], start=True, stop=True, tile_position=(r0, 0))
                    return i
                pe.wait_ge(g_ev["qi"], L1)
                pe.wait_ge(g_ev["ki"], L1)
                dots(1, 256).then_inc(S["dots_ps"], 1)

                pe.wait_ge(arrived[U_A], landed[0])
                pe.wait_ge(S["ws_done"], L1)
                w = w_in(U_A)
                for m in range(2):
                    i = on_features(ps[6][:, 256 * m:256 * m + 256], w[:, :, P * m:P * m + P])
                i.then_inc(g_ps["a"], 1)
                for t in range(TT):
                    i = on_tokens(ps[7][:, 256 * t:256 * t + 256], w[:, :, 256:512], t)
                i.then_inc(g_ps["av"], 1)
                pe.wait_ge(S["rel"], first)
                dots(0, P).then_inc(S["dots_ps"], 1)
                pe.wait_ge(arrived[U_AG], landed[0])
                w = w_in(U_AG)
                on_features(ps[4][0:GLA_RANK, 0:256], w[:, :, 256:272]).then_inc(g_ps["lr"], 1)
                for t in range(TT):
                    i = on_tokens(ps[5][:, 256 * t:256 * t + 256], w[:, :, 0:256], t)
                i.then_inc(g_ps["ag"], 1)
                pe.wait_ge(g_ev["a"], L1)
                pe.wait_ge(g_ev["lr"], L1)
                mm(ps[6][:, 0:256], wa2[:, :], lrT, start=True, stop=True).then_inc(g_ps["logit"], 1)

                pe.wait_ge(arrived[U_CQ], landed[0])
                pe.wait_ge(g_ev["av"], L1)
                w = w_in(U_CQ)
                for m in range(2):
                    i = on_features(ps[7][:, 256 * m:256 * m + 256], w[:, :, P * m:P * m + P])
                i.then_inc(g_ps["q"], 1)
                for m in range(2):
                    i = on_features(ps[4][:, 256 * m:256 * m + 256], w[:, :, 256 + P * m:384 + P * m])
                i.then_inc(g_ps["k"], 1)
                pe.wait_ge(arrived[U_CV], landed[0])
                pe.wait_ge(g_ev["ag"], L1)
                for t in range(TT):
                    i = on_tokens(ps[5][:, 256 * t:256 * t + 256], w_in(U_CV), t)
                i.then_inc(g_ps["cv"], 1)

                pe.wait_ge(S["qbd_done"], L1)
                pe.wait_ge(S["kd_ready"], L1)
                pe.wait_ge(S["rel"], second)
                for t in range(TT):
                    i = mm(ps[t][:, :], akT[:, P * t:P * t + P], qbd[:, t, :, :], start=True, stop=True)
                i.then_inc(S["att_ps"], 1)
                for t in range(TT):
                    i = pe.transpose(ps[2][:, P * t:P * t + P], kdT[:, P * t:P * t + P], ident)
                i.then_inc(S["kd_ps"], 1)

                pe.wait_ge(arrived[U_BU], landed[0])
                pe.wait_ge(S["la_ready"], L1)
                w = w_in(U_BU)
                for m in range(2):
                    i = on_features(ps[6][:, 256 * m:256 * m + 256], w[:, :, P * m:P * m + P])
                i.then_inc(g_ps["bu"], 1)
                pe.wait_ge(arrived[U_UV], landed[0])
                pe.wait_ge(g_ev["q"], L1)
                on_tokens(ps[7][:, :], w_in(U_UV), 0).then_inc(g_ps["uv0"], 1)
                pe.wait_ge(g_ev["k"], L1)
                on_tokens(ps[4][:, :], w_in(U_UV), 1).then_inc(g_ps["uv1"], 1)

                pe.wait_ge(S["kdr_done"], L1)
                mm(ps[3][:, 0:256], kdr[0:64, 0, :], av[0:64, 0, :], start=True, stop=True)
                mm(ps[3][:, 256:512], kdr[0:64, 1, :], av[0:64, 1, :], start=True, stop=True)
                mm(ps[2][:, 256:512], kdr[64:128, 0, :], av[64:128, 0, :], start=True, stop=True)\
                    .then_inc(S["kv_ps"], 1)

                pe.wait_ge(arrived[U_WKV], landed[1])
                pe.wait_ge(g_ev["cv"], L1)
                pe.wait_ge(g_ev["bu"], L1)
                pe.wait_ge(S["wkv_scaled"], L1)
                w = v3(ring[:, U_WKV, :], 0, 4096, KT)
                for m in range(2):
                    i = on_features(ps[5][:, 256 * m:256 * m + 256], w[:, :, P * m:P * m + P], memT)
                i.then_inc(g_ps["kx"], 1)
                for t in range(2):
                    i = on_tokens(ps[6][:, 256 * t:256 * t + 256], w[:, :, 256:512], t, memT)
                i.then_inc(g_ps["vx"], 1)

                pe.wait_ge(S["att_done"], L1)
                pe.wait_ge(S["zeroed"], 1)
                pe.wait_ge(S["s_ready"], L1)
                for t in range(TT):
                    for half in range(2):
                        n = 2 * t + half
                        state = zeros[:, :] if n == 0 else Sst[:, n - 1, :]
                        mm(ps[t][64 * half:64 * half + 64, 0:256], aqT[:, CHUNK * n:CHUNK * n + CHUNK], state,
                           start=True, stop=False, skip_group_check=True)
                    for hh in range(HEADS):
                        i = mm(ps[t][:, 64 * hh:64 * hh + 64], attT[:, t, P * hh:P * hh + P],
                               av[:, t, 64 * hh:64 * hh + 64], start=False, stop=True, skip_group_check=True)
                i.then_inc(S["o_ps"], 1)

                pe.wait_ge(S["vn_done"], L1)
                for t in range(TT):
                    for g in range(4):
                        i = mm(ps[2 + t][:, 64 * g:64 * g + 64], wsT[:, g, :], vn[:, t, 64 * g:64 * g + 64],
                               start=True, stop=True)
                i.then_inc(S["sg_ps"], 1)

                pe.wait_ge(S["pool_out"], L1)
                pe.wait_ge(g_ev["uv0"], L1)
                for m in range(2):
                    i = mm(ps[7][:, 256 * m:256 * m + 256], pwbd[:, m, :], bu[:, m, PAD:PAD + SEQ], start=True, stop=True)
                i.then_inc(g_ps["y"], 1)

                def attend(t, n, keys, banks, name):
                    for hh in range(HEADS):
                        r0 = 64 * (hh % 2)
                        c0 = n * (hh // 2)
                        i = mm(ps[banks + hh % 2][:, c0:c0 + n], qT[r0:r0 + 64, hh // 2, P * t:P * t + P],
                               keys[r0:r0 + 64, hh // 2, 0:n], start=True, stop=True)
                    i.then_inc(S[name], 1)

                def values(dst, pT, vals, t, tiles):
                    for hh in range(HEADS):
                        for k in range(tiles):
                            i = mm(dst[:, 64 * hh:64 * hh + 64], pT[:, tiles * hh + k, :],
                                   vals[:, k, 64 * hh:64 * hh + 64], start=k == 0, stop=k == tiles - 1)
                    return i

                pe.wait_ge(g_ev["uv1"], L1)
                pe.wait_ge(g_ev["kx"], L1)
                attend(1, 256, kT, 4, "lg_ps")
                pe.wait_ge(g_ev["vx"], L1)
                pe.wait_ge(g_ev["y"], L1)
                attend(0, P, kT, 6, "lg_ps")
                pe.wait_ge(S["og_done"], L1)
                pe.wait_ge(S["p"], first)
                for hh in range(HEADS):
                    for k in range(2):
                        x = 2 * hh + k
                        i = pe.transpose(ps[x // 4][:, P * (x % 4):P * (x % 4) + P],
                                         prb[1][:, hh, P * k:P * k + P], ident)
                i.then_inc(S["pt1_ps"], 1)
                pe.wait_ge(S["od_done"], L1)
                pe.wait_ge(S["p"], second)
                for hh in range(HEADS):
                    i = pe.transpose(ps[2][:, P * hh:P * hh + P], prb[0][:, hh, :], ident)
                i.then_inc(S["pt0_ps"], 1)

                def transpose_rows(bank, src):
                    for k in range(2):
                        for t in range(TT):
                            c0 = 256 * k + P * t
                            i = pe.transpose(ps[bank][:, c0:c0 + P], src[:, t, P * k:P * k + P], ident)
                    return i
                pe.wait_ge(S["lg"], second)
                transpose_rows(4, sg)
                transpose_rows(6, uvg)
                pe.wait_ge(S["pt1_v"], L1)
                pe.wait_ge(S["pt1_a"], L1)
                values(ps[3][:, 256:512], pT_mix[1], cv, 1, 2)
                pe.wait_ge(S["pt0_v"], L1)
                values(ps[3][:, 0:256], pT_mix[0], cv, 0, 1).then_inc(S["pv_ps"], 1)
                pe.wait_ge(S["oc_done"], L1)
                transpose_rows(5, oc).then_inc(S["mt_ps"], 1)

                pe.wait_ge(S["mt_v"], L1)
                pe.wait_ge(S["mt_a"], L1)
                for i4, m in enumerate(WOUT_ORDER):
                    s = U_WOUT + i4
                    pe.wait_ge(arrived[s], landed[1])
                    w = v3(ring[:, s, :], 0, 2048, 2)
                    for k in range(2):
                        for t in range(TT):
                            for half in range(2):
                                i = mm(ps[2 * t + half][:, :], mixT[:, 2 * m + k, P * t:P * t + P],
                                       w[:, k, 512 * half:512 * half + 512],
                                       start=i4 == 0 and k == 0, stop=i4 == 3 and k == 1)
                    i.then_inc(slot_free[s], 1)

                transposes(nv[1])
                pe.wait_ge(arrived[U_WQ], landed[1])
                w = v3(ring[:, U_WQ, :], 0, 2048, KT)
                for m in range(2):
                    i = on_features(ps[4][:, 256 * m:256 * m + 256], w[:, :, P * m:P * m + P])
                i.then_inc(g_ps["xq"], 1)
                pe.wait_ge(g_ev["xq"], L1)
                for t in range(TT):
                    attend(t, MEM, kxT, 2 * t, "xlg_ps")
                for t in range(TT):
                    pe.wait_ge(S["xp"], second if t else first)
                    for x in range(8):
                        i = pe.transpose(ps[4 + 2 * t + x // 4][:, P * (x % 4):P * (x % 4) + P],
                                         prx[t][:, x // 2, P * (x % 2):P * (x % 2) + P], ident)
                    i.then_inc(S["xpt_ps"], 1)
                for t in range(TT):
                    pe.wait_ge(S["xpt_v"], second if t else first)
                    pe.wait_ge(S["xpt_a"], second if t else first)
                    i = values(ps[2 * t][:, 0:256], pT_x[t], vx, t, 2)
                i.then_inc(S["xpv_ps"], 1)
                pe.wait_ge(S["ox_done"], L1)
                transpose_rows(1, oc).then_inc(S["xo_ps"], 1)
                pe.wait_ge(S["xo_done"], L1)
                pe.wait_ge(arrived[U_WO], landed[1])
                w = v3(ring[:, U_WO, :], 0, 2048, 2)
                for t in range(TT):
                    for half in range(2):
                        for k in range(2):
                            i = mm(ps[4 + 2 * t + half][:, :], oxT[:, k, P * t:P * t + P],
                                   w[:, k, 512 * half:512 * half + 512], start=k == 0, stop=k == 1)
                i.then_inc(g_ps["xout"], 1)

                transposes(nv[2])
                with pe.If(layer < 1):
                    def down(f, slot, k, frees):
                        pe.wait_ge(S["f_a"], f + 1)
                        w2 = ring[:, slot, k * D:k * D + D]
                        for q in range(4):
                            i = mm(ps[4 + q][:, :], f_act[:, f % 2, P * (q // 2):P * (q // 2) + P],
                                   w2[:, 512 * (q % 2):512 * (q % 2) + 512], start=f == 0, stop=f == FF // P - 1)
                            if q < len(frees):
                                i.then_inc(slot_free[frees[q]], 1)
                        return i

                    f = 0
                    before = None
                    for c, n in enumerate(FFN_TILES):
                        u1, u3, u2 = 3 * c, 3 * c + 1, 3 * c + 2
                        for k in range(n):
                            for w, u in enumerate((u1, u3)):
                                if k == 0:
                                    pe.wait_ge(arrived[u % RING], landed[2 + u // RING])
                                wt = v3(ring[:, u % RING, :], 0, KT * n * P, KT)
                                i = on_features(ps[f % 2][:, 256 * w:256 * w + 256], wt[:, :, P * k:P * k + P])
                            i.then_inc(S["f_h"], 1)
                            frees = (u1 % RING, u3 % RING) if k == n - 1 else ()
                            if before is not None:
                                bf, bslot, bk, blast = before
                                i = down(bf, bslot, bk, frees)
                                if blast:
                                    i.then_inc(slot_free[bslot], 1)
                            if k == 0:
                                pe.wait_ge(arrived[u2 % RING], landed[2 + u2 // RING])
                            before = (f, u2 % RING, k, k == n - 1)
                            f += 1
                    down(before[0], before[1], before[2], ()).then_inc(slot_free[before[1]], 1)

            for t in range(TT):
                i = on_tokens(ps[4][:, 8 * t:8 * t + 8], routw, t)
            i.then_inc(S["rlog_ps"], 1)
            pe.wait_ge(S["sel_ready"], 1)
            sel = score[:, :, :].rearrange("p a b -> p (a b)")[:, 80:96]
            before_, ones = cc("before"), cc("ones")
            mm(ps[5][:, 0:8], before_, sel[:, 0:8], start=True, stop=True)
            mm(ps[5][:, 8:16], before_, sel[:, 8:16], start=True, stop=False)
            mm(ps[5][:, 8:16], ones, sel[:, 0:8], start=False, stop=True)
            mm(ps[5][:, 16:24], ones, sel[:, 0:8], start=True, stop=False)
            mm(ps[5][:, 16:24], ones, sel[:, 8:16], start=False, stop=True).then_inc(S["rank_ps"], 1)
            pe.wait_ge(S["jobs_ready"], 1)
            n_jobs = pe.value_load(tabi[0:1, 0:1], min_val=N_EXP, max_val=MAX_JOBS)

            def gather(n):
                pe.wait_ge(S["j_g"], n)
                for kt in range(KT):
                    for t in range(TT):
                        i = mm(ps[2 + kt // 4][:, P * (kt % 4):P * (kt % 4) + P], xr[:, t, P * kt:P * kt + P],
                               hot[:, t, :], start=t == 0, stop=t == TT - 1)
                i.then_inc(S["j_gps"], 1)

            gather(1)
            with pe.Fori(0, n_jobs) as j:
                cn = [pe.snap(j * NCH + (c + 1)) for c in range(NCH)]
                j1, j2 = pe.snap(j + 1), pe.snap(j + 2)
                landed = [pe.snap(j * (16 * JOB_TURNS) + 16 * (2 * LAYER_TURNS - 3 + t + 1)) for t in range(JOB_TURNS)]

                def up(c, w, free=None):
                    u = 3 * c + w
                    pe.wait_ge(arrived[u % RING], landed[u // RING])
                    wt = v3(ring[:, u % RING, :], 0, 4096, KT)
                    for k in range(KT):
                        i = mm(ps[2 * (c % 2) + w][:, :], xg[:, k, :], wt[:, k, :], start=k == 0, stop=k == KT - 1)
                        if k == 0 and free is not None:
                            i.then_inc(slot_free[free % RING], 1)
                    i.then_inc(S["j_h3" if w else "j_h1"], 1)

                def transpose_act(c, free):
                    pe.wait_ge(S["j_a"], cn[c])
                    for f in range(4):
                        i = pe.transpose(ps[4][:, P * f:P * f + P], j_act[:, c % 2, P * f:P * f + P], ident)
                        if f == 0:
                            i.then_inc(slot_free[free % RING], 1)
                    i.then_inc(S["j_tps"], 1)

                def down(c, free):
                    u = 3 * c + 2
                    pe.wait_ge(arrived[u % RING], landed[u // RING])
                    pe.wait_ge(S["j_t"], cn[c])
                    wt = v3(ring[:, u % RING, :], 0, 4096, 4)
                    for f in range(4):
                        for half in range(2):
                            i = mm(ps[6 + half][:, :], j_actT[:, c % 2, f, :], wt[:, f, 512 * half:512 * half + 512],
                                   start=c == 0 and f == 0, stop=c == NCH - 1 and f == 3)
                            if f == 0 and half == 0 and free is not None:
                                i.then_inc(slot_free[free % RING], 1)
                    if c < NCH - 1:
                        i.then_inc(slot_free[u % RING], 1)
                    return i

                pe.wait_ge(S["j_gv"], j1)
                pe.wait_ge(S["j_ga"], j1)
                up(0, 0)
                up(0, 1, free=0)
                for c in range(1, NCH):
                    up(c, 0, free=1 if c == 1 else None)
                    transpose_act(c - 1, free=3 * c)
                    up(c, 1)
                    down(c - 1, free=3 * c + 1)
                gather(j2)
                last = 3 * (NCH - 1)
                pe.wait_ge(S["j_a"], cn[NCH - 1])
                for f in range(4):
                    i = pe.transpose(ps[4][:, P * f:P * f + P], j_act[:, (NCH - 1) % 2, P * f:P * f + P], ident)
                i.then_inc(S["j_tps"], 1)
                for t in range(TT):
                    i = pe.transpose(ps[5][:, P * t:P * t + P], hotg[:, t, :], ident)
                i.then_inc(S["j_gtps"], 1)
                down(NCH - 1, None).then_inc(S["j_yps"], 1)
                pe.wait_ge(S["j_gt"], j1)
                pe.wait_ge(S["j_gv"], j2)
                pe.wait_ge(S["j_ga"], j2)
                for half, ready in ((0, "j_yv"), (1, "j_ya")):
                    pe.wait_ge(S[ready], j1)
                    for t, b in ((0, 4), (1, 2)):
                        i = mm(ps[b + half][:, :], hotgT[:, t, :], yrow[:, 512 * half:512 * half + 512],
                               start=True, stop=True)
                        if (half, t) == (0, 0):
                            i.then_inc(slot_free[(last + 2) % RING], 1)
                i.then_inc(S["j_c1"], 1)
                pe.wait_ge(S["j_cv"], j1)


INPUTS = ("x", "mem", "rel_bias", "final_norm", "norm_mix", "w_in", "gla_wa2", "gla_ba", "gla_norm", "pool_w", "pool_b",
          "pool_scale", "sgu_ln_g", "sgu_ln_b", "sgu_w", "sgu_b", "w_out", "norm_xa", "norm_mem", "xa_wq", "xa_wkv",
          "xa_wo", "norm_ffn", "ffn_w1", "ffn_w3", "ffn_w2", "router", "moe_w1", "moe_w3", "moe_w2")


def kernel(**inputs):
    import numpy as _np
    import concourse.bacc as _bacc
    from concourse import mybir as _mybir
    from concourse.bass_utils import run_bass_kernel_spmd as _run

    nc = _bacc.Bacc("TRN2", target_bir_lowering=False, num_devices=1)
    arrays = {name: _np.ascontiguousarray(inputs[name]) for name in INPUTS}
    for name, value in zip(("consts", "glam", "onehot", "flip"), shape_constants()):
        arrays[name] = value
    aps = {name: nc.dram_tensor(f"in_{name}", a.shape, _mybir.dt.from_np(a.dtype), kind="ExternalInput").ap()
           for name, a in arrays.items()}
    out = nc.dram_tensor("out", arrays["x"].shape, _mybir.dt.from_np(arrays["x"].dtype), kind="ExternalOutput").ap()
    build(nc, aps, out)
    r = _run(nc, [{f"in_{name}": a for name, a in arrays.items()}], core_ids=[0])
    return r.results[0]["out"]
```

```python
import math
from contextlib import ExitStack

import numpy as np

import concourse.bass as bass
from concourse import mybir

P = 128
F32 = mybir.dt.float32
F32R = mybir.dt.float32r
I32 = mybir.dt.int32
U8 = mybir.dt.uint8
ALU = mybir.AluOpType
ACT = mybir.ActivationFunctionType
AX = mybir.AxisListType.X

SEQ, D, DEPTH, MEM = 256, 1024, 2, 256
TT = SEQ // P
KT = D // P
GW = 256
EPS = 1e-6
HEADS = 4
GLA_DK, GLA_DV, GLA_RANK, CHUNK = 32, 64, 16, 64
IDX_HEADS, IDX_DIM, TOPK = 8, 32, 64
DH = 64
WINDOWS = (2, 4, 8, 16)
PAD = 16
N_EXP, FE, FF = 8, 3584, 2816
BUCKETS, MAX_DIST = 32, 128
IN_W = 2616
RING = 7
LAYER_TURNS = 5
JOB_TURNS = 3
FC = 512
NCH = FE // FC
MAX_JOBS = N_EXP + 3
PIECE, NB = 1024, 4
QP = 4096 // PIECE
JOB_UNITS = [(1, 0), (3, 0)] + [x for c in range(1, NCH) for x in ((1, c), (3, c), (2, c - 1))] + [(2, NCH - 1)]
UNIT_OF = {x: u for u, x in enumerate(JOB_UNITS)}
JOB_PIECES = QP * len(JOB_UNITS)


def after(unit):
    return QP * UNIT_OF[unit] + QP - 1 + NB


FFN_TILES = (4, 3, 3, 3, 3, 3, 3)
NEG, MARK, HALF = -3.0e38, -3.4e38, -3.2e38

C_AQ, C_AV, C_AG, C_LR, C_BU = 0, 256, 512, 768, 784
C_CQ, C_CK, C_CV, C_QI, C_KI, C_WI, C_UV = 1040, 1296, 1552, 1808, 2064, 2096, 2104
IN_UNITS = ((C_QI, C_UV), (0, 512), (C_AG, C_BU), (C_CQ, C_CV), (C_CV, C_QI), (C_BU, C_CQ), (C_UV, IN_W))
U_QI, U_A, U_AG, U_CQ, U_CV, U_BU, U_UV = range(7)
U_WKV, U_WOUT, U_WQ, U_WO = 0, 1, 5, 6
WOUT_ORDER = (1, 0, 3, 2)

R_MIX, R_XA, R_MEM, R_FFN, R_BA, R_PB, R_PS, R_SB, N_ROWS = 0, 8, 16, 24, 32, 33, 35, 37, 41

CONST = {}
_at = 0
for _name, _w in (("ident", P), ("vis", 256), ("reset", 256), ("bd", 256), ("tril", P), ("inv", 512),
                  ("before", P), ("ones", P), ("iota", P), ("eidx", 8), ("erev", 8)):
    CONST[_name] = (_at, _at + _w)
    _at += _w
CONST_W = _at


def shape_constants():
    c = np.zeros((P, CONST_W), np.float32)
    r = np.arange(P)
    s = np.arange(256)

    def put(name, v):
        c[:, CONST[name][0]:CONST[name][1]] = v

    put("ident", np.eye(P))
    put("vis", np.where(s[None, :] <= P + r[:, None], 0.0, NEG))
    put("reset", np.where(s % CHUNK == 0, 0.0, 1.0)[None, :])
    put("bd", (r[:, None] // GLA_DK == s[None, :] // GLA_DV))
    put("tril", r[None, :] <= r[:, None])
    inv = np.zeros((P, 2, 256), np.float32)
    for g, w in enumerate(WINDOWS):
        inv[64 * (g % 2):64 * (g % 2) + 64, g // 2, :] = 1.0 / np.minimum(s + 1, w).astype(np.float32)
    put("inv", inv.reshape(P, 512))
    put("before", r[:, None] < r[None, :])
    put("ones", 1.0)
    put("iota", r[None, :])
    put("eidx", np.arange(8)[None, :])
    put("erev", 8 - np.arange(8)[None, :])
    gla = ((r[:, None] <= r[None, :]) & (r[:, None] // CHUNK == r[None, :] // CHUNK)).astype(np.int32)
    gla = np.ascontiguousarray(np.tile(gla[:, None, :], (1, HEADS, 1)).reshape(P, HEADS * P)).astype(np.float32)
    n = np.maximum(255 - np.arange(384), 0)
    exact = BUCKETS // 2
    nf = np.maximum(n, 1).astype(np.float32)
    large = exact + (np.log(nf / np.float32(exact)) / np.float32(math.log(MAX_DIST / exact))
                     * np.float32(BUCKETS - exact)).astype(np.int32)
    bucket = np.where(n < exact, n, np.minimum(large, BUCKETS - 1))
    onehot = (np.arange(BUCKETS)[:, None] == bucket[None, :]).astype(np.float32)
    flip = np.ascontiguousarray(np.eye(P, dtype=np.float32)[::-1])
    return c, gla, onehot, flip


def build(nc, A, out):
    ctx = ExitStack()
    with ctx:
        def sb(name, shape, dt=F32):
            return ctx.enter_context(nc.sbuf_tensor(name, shape, dt))

        def sem(name):
            return ctx.enter_context(nc.semaphore(name))

        ring = sb("ring", [P, RING, 4096])
        cst = sb("cst", [P, CONST_W])
        gmask = sb("gmask", [P, HEADS * P], U8)
        h = sb("h", [P, TT, D])
        base = nc.sbuf_base
        xnT = sb("xnT", [P, KT, SEQ])
        mixT = xnT
        memT = sb("memT", [P, KT, MEM])
        qidx = sb("qidx", [P, 1024])
        qT = sb("qT", [P, 2, SEQ])
        kT = sb("kT", [P, 2, SEQ])
        cv = sb("cv", [P, TT, GW])
        av = sb("av", [P, TT, GW])
        sg = sb("sg", [P, TT, GW])
        gla = sb("gla", [P, 1024])
        glab = sb("glab", [P, 512])
        kdec = sb("kdec", [P, 512])
        Sst = sb("Sst", [P, 3, GW])
        bu = sb("bu", [P, 2, PAD + SEQ])
        pw1 = sb("pw1", [P, 2, PAD + SEQ])
        stretch = nc.sbuf_base - base

        def over(name, shape):
            n = 4 * int(np.prod(shape[1:]))
            assert over.at + n <= stretch
            t = nc.alloc_sbuf_tensor_at(name, shape, F32R, offset=base + over.at, align_bytes=32)
            over.at += n
            return t
        over.at = 0
        w_hi, w_lo = over("w_hi", [P, NB, PIECE]), over("w_lo", [P, NB, PIECE])
        xg_hi, xg_lo = over("xg_hi", [P, KT, P]), over("xg_lo", [P, KT, P])
        at_hi, at_lo = over("at_hi", [P, 4, P]), over("at_lo", [P, 4, P])

        pw2 = sb("pw2", [P, 2, PAD + SEQ])
        uvg = sb("uvg", [P, TT, 512])
        bias = sb("bias", [P, HEADS, 256])
        r2 = sb("r2", [P, 2048])
        bc = sb("bc", [P, 3, GW])
        wsT = sb("wsT", [P, 4, P])
        pwbd = sb("pwbd", [P, 2, P])
        wa2 = sb("wa2", [GLA_RANK, P])
        prow = sb("prow", [N_ROWS, P])
        pcol = sb("pcol", [P, N_ROWS])
        routw = sb("routw", [P, KT, N_EXP])
        wis = sb("wis", [P, TT, IDX_HEADS])
        score = sb("score", [P, 2, 256])
        m8 = sb("m8", [P, 8])
        tick = sb("tick", [P, 2])
        zeros = sb("zeros", [P, GW])
        kxT = sb("kxT", [P, 2, MEM])
        vx = sb("vx", [P, 2, GW])
        st = sb("st", [P, 96])
        tabi = sb("tabi", [1, 16], I32)
        jobt = sb("jobt", [P, TT, 2, MAX_JOBS + 1])

        def cc(name, a=0, b=None):
            lo, hi = CONST[name]
            return cst[:, lo + a:hi if b is None else lo + b]

        ident = cc("ident")
        ps = [ctx.enter_context(nc.psum_tensor(f"bank{i}", [P, 512], F32)) for i in range(8)]

        def v3(t, a, b, x):
            return t[:, a:b].rearrange("p (x y) -> p x y", x=x)

        def xT(kt):
            return ps[kt // 2][:, 256 * (kt % 2):256 * (kt % 2) + 256]

        xr = v3(r2, 0, 2048, 2)
        rel = v3(r2, 0, 2048, 8)
        qbd = r2[:, 0:1024].rearrange("p (t h i) -> p t h i", t=2, h=4)
        attT = r2[:, 1024:2048].rearrange("p (t n) -> p t n", t=2)
        qiT = v3(qidx, 0, 512, 2)
        kiT = qidx[:, 512:768]
        lrT = qidx[0:GLA_RANK, 768:1024]
        aqT, akT, eb, enb = (gla[:, 256 * i:256 * i + 256] for i in range(4))
        la, bs = glab[:, 0:256], glab[:, 256:512]
        kdT, kdr = kdec[:, 0:256], v3(kdec, 256, 512, 2)
        lgm = [v3(r2, 1024, 1536, 4), v3(gla, 0, 1024, 4)]
        prb = [v3(r2, 1536, 2048, 4), v3(r2, 0, 1024, 4)]
        pT_mix = [v3(glab, 0, 512, 4), v3(qidx, 0, 1024, 8)]
        prx = [v3(r2, 0, 1024, 4), v3(r2, 1024, 2048, 4)]
        pT_x = [v3(qidx, 0, 1024, 8), v3(gla, 0, 1024, 8)]
        oc = v3(Sst[:, :, :].rearrange("p a b -> p (a b)"), 0, 512, 2)
        wsr = uvg[:, 0, :].rearrange("p (g s) -> p g s", g=4)
        osq = v3(kdec, 0, 512, 2)
        vn = uvg[:, :, 256:512]
        oxT = kT
        f_sil, f_act = v3(glab, 0, 512, 2), v3(kdec, 0, 512, 2)
        xnf = xnT[:, :, :].rearrange("p k m -> p (k m)")
        j_sil = [t[:, :, :].rearrange("p a b -> p (a b)") for t in (kxT, vx)]
        j_act = pw2[:, :, :].rearrange("p a b -> p (a b)")[:, 0:FC]
        yrow = uvg[:, :, :].rearrange("p a b -> p (a b)")
        hot, hotg, hotgT = (bc[:, i, :].rearrange("p (t s) -> p t s", t=2) for i in range(3))
        fnorm = bias[:, :, :].rearrange("p h x -> p (h x)")
        hank = v3(qidx, 0, 1024, HEADS)

        ss, rs, ms = st[:, 0:2], st[:, 2:4], st[:, 4:6]
        s_mx, s_sum, s_rec = st[:, 8:16], st[:, 16:24], st[:, 24:32]
        s_bn, s_ag, s_vm, s_vr = st[:, 32:44], st[:, 44:48], st[:, 48:50], st[:, 50:52]
        s_og, s_or = st[:, 52:60], st[:, 60:68]
        s_d, s_e, s_g = st[:, 68:70], st[:, 70:72], st[:, 72:76]

        names = """loaded_h loaded_mem loaded_const loaded_par loaded_fnorm bias_rows bias_hank stored v_chain a_chain
            g_chain bias_ps hank_ps bias_done h_upd ss_ready ms_ready rstd_ready xr_ready xT_ps xT_v xT_a
            par_free zeroed wkv_scaled pcol_ps pcol_done wsm_done ws_ps ws_done la_ready ls_ready b_ready
            eb_ready qe_ready r2_zero qbd_done kd_ready att_ps att_done kd_ps kdr_done kv_ps s_ready o_ps osq
            ms_gla r_gla og_done pool_out vms vr vn_done sg_ps od_done pt1_ps pt0_ps pt1_v pt1_a pt0_v pv_ps
            oc_done mt_ps mt_v mt_a xpv_ps ox_done xo_ps xo_done f_h f_s f_a  rlog_ps top_diff top_exp
            sel_ready rank_ps jobs_ready j_h1 j_h3 j_s j_a j_tps j_th j_t j_yps j_yv j_ya j_g j_gps j_gtps j_gh j_gl
            j_gt j_c1 j_cv loaded_nffn hi_ready lo_ready piece_free fin_ms fin_r fin scored dots_ps rel lg p xmx xp xpt_ps xpt_a lg_ps xlg_ps xpt_v""".split()
        S = {n: sem(n) for n in names}
        arrived = [sem(f"arrived{i}") for i in range(RING)]
        slot_free = [sem(f"slot_free{i}") for i in range(RING)]
        GROUPS = ("qi", "ki", "a", "av", "lr", "ag", "logit", "q", "k", "cv", "bu", "uv0", "uv1", "kx", "vx", "y", "xq", "wout", "xout")
        ENDS = {"ki": (U_QI, 0), "av": (U_A, 0), "ag": (U_AG, 0), "k": (U_CQ, 0), "cv": (U_CV, 0), "bu": (U_BU, 0),
                "uv1": (U_UV, 0), "vx": (U_WKV, 1), "xq": (U_WQ, 1), "wout": (U_WOUT + 3, 1), "xout": (U_WO, 1)}
        g_ps = {n: slot_free[ENDS[n][0]] if n in ENDS else sem(f"ps_{n}") for n in GROUPS}
        g_ev = {n: sem(f"ev_{n}") for n in GROUPS if n not in ("logit", "wout", "xout")}

        consts, glam, onehot, flip = A["consts"], A["glam"], A["onehot"], A["flip"]
        rev = nc.dram_tensor("bias_scratch", (HEADS, 384), F32, kind="Internal")
        block = ctx.enter_context(nc.Block())

        def chain(eng, s):
            n = [0]

            def link(ins):
                n[0] += 1
                ins.then_inc(s, 1)
                eng.wait_ge(s, n[0])

            def restart():
                n[0] = 0
                eng.sem_clear(s)
            return link, restart

        def rows(ap, n):
            return ap.rearrange("(r c) -> r c", c=P)

        @block.sync
        def _(sp):
            sp.dma_start(xr, A["mem"][0].rearrange("(t p) d -> p t d", p=P)).then_inc(S["loaded_mem"], 16)
            sp.dma_start(h[:, :, :], A["x"][0].rearrange("(t p) d -> p t d", p=P)).then_inc(S["loaded_h"], 16)
            sp.dma_start(cst[:, :], consts).then_inc(S["loaded_const"], 16)
            sp.dma_start(uvg[:, 1, :], glam).then_inc(S["loaded_const"], 16)
            sp.dma_start(routw[:, :, :], A["router"][0].rearrange("(k p) e -> p k e", p=P)).then_inc(S["loaded_const"], 16)
            sp.dma_start(gla[0:BUCKETS, 0:384], onehot).then_inc(S["loaded_const"], 16)
            sp.dma_start(kdec[0:BUCKETS, 0:HEADS], A["rel_bias"]).then_inc(S["loaded_const"], 16)
            sp.dma_start(glab[:, 0:P], flip).then_inc(S["loaded_const"], 16)

            with sp.Fori(0, DEPTH) as layer:
                lay = bass.ds(layer, 1)
                L1 = sp.snap(layer + 1)
                turn = [sp.snap(layer * LAYER_TURNS + (t + 1)) for t in range(LAYER_TURNS)]
                sp.wait_ge(S["par_free"], 1)
                sp.wait_ge(S["par_free"], L1)
                for name, row, n in (("norm_mix", R_MIX, 8), ("norm_xa", R_XA, 8), ("norm_mem", R_MEM, 8),
                                     ("norm_ffn", R_FFN, 8), ("gla_ba", R_BA, 1), ("pool_scale", R_PS, 2)):
                    sp.dma_start(prow[row:row + n, :], A[name][lay].rearrange("e (r c) -> (e r) c", c=P))\
                      .then_inc(S["loaded_par"], 16)
                sp.dma_start(prow[R_PB:R_PB + 2, :], A["pool_b"][lay].rearrange("e (r a) c -> (e r) (a c)", a=2))\
                  .then_inc(S["loaded_par"], 16)
                sp.dma_start(prow[R_SB:R_SB + 4, :], A["sgu_b"][lay].rearrange("e g t -> (e g) t"))\
                  .then_inc(S["loaded_par"], 16)
                for i, name in enumerate(("gla_norm", "sgu_ln_g", "sgu_ln_b")):
                    sp.dma_start(bc[:, i, :], A[name][lay].broadcast_to([P, GW])).then_inc(S["loaded_par"], 16)
                sp.dma_start(wa2[:, :], A["gla_wa2"][lay].rearrange("e r c -> (e r) c")).then_inc(S["loaded_par"], 16)
                sp.dma_start(wsr, A["sgu_w"][lay].rearrange("e g t s -> t (e g) s")).then_inc(S["loaded_par"], 16)
                for g in range(4):
                    r0 = 64 * (g % 2)
                    sp.dma_start(pwbd[r0:r0 + 64, g // 2, r0:r0 + 64],
                                 A["pool_w"][lay, g].rearrange("e c d -> (e c) d")).then_inc(S["loaded_par"], 16)

                def unit(t, s, dst, src):
                    sp.wait_ge(slot_free[s], 1)
                    sp.wait_ge(slot_free[s], turn[t])
                    sp.dma_start(dst, src).then_inc(arrived[s], 16)

                for s, (lo, hi) in enumerate(IN_UNITS):
                    unit(0, s, ring[:, s, 0:KT * (hi - lo)].rearrange("p (k c) -> p k c", k=KT),
                         A["w_in"][lay, :, lo:hi].rearrange("e (k p) c -> p (e k) c", p=P))
                unit(1, U_WKV, v3(ring[:, U_WKV, :], 0, 4096, KT),
                     A["xa_wkv"][lay].rearrange("e (k p) c -> p (e k) c", p=P))
                for i, m in enumerate(WOUT_ORDER):
                    unit(1, U_WOUT + i, v3(ring[:, U_WOUT + i, :], 0, 2048, 2),
                         A["w_out"][lay, 256 * m:256 * m + 256, :].rearrange("e (k p) c -> p (e k) c", p=P))
                unit(1, U_WQ, v3(ring[:, U_WQ, :], 0, 2048, KT),
                     A["xa_wq"][lay].rearrange("e (k p) c -> p (e k) c", p=P))
                unit(1, U_WO, v3(ring[:, U_WO, :], 0, 2048, 2),
                     A["xa_wo"][lay].rearrange("e (k p) c -> p (e k) c", p=P))
                with sp.If(layer < 1):
                    f0 = 0
                    for c, n in enumerate(FFN_TILES):
                        for w, name in enumerate(("ffn_w1", "ffn_w3")):
                            u = 3 * c + w
                            unit(2 + u // RING, u % RING, v3(ring[:, u % RING, :], 0, KT * n * P, KT),
                                 A[name][0, :, P * f0:P * (f0 + n)].rearrange("(k p) c -> p k c", p=P))
                        u = 3 * c + 2
                        unit(2 + u // RING, u % RING, v3(ring[:, u % RING, :], 0, n * D, n),
                             A["ffn_w2"][0, P * f0:P * (f0 + n), :].rearrange("(k p) c -> p k c", p=P))
                        f0 += n

            def job_loads(j, e):
                turns = [sp.snap(j * JOB_TURNS + (2 * LAYER_TURNS - 3 + t + 1)) for t in range(JOB_TURNS)]
                ex = bass.ds(e, 1)
                for u, (w, c) in enumerate(JOB_UNITS):
                    slot = ring[:, u % RING, :]
                    sp.wait_ge(slot_free[u % RING], 1)
                    sp.wait_ge(slot_free[u % RING], turns[u // RING])
                    if w == 2:
                        dst, src = v3(slot, 0, 4096, 4), A["moe_w2"][0, ex, FC * c:FC * c + FC, :]
                    else:
                        dst, src = v3(slot, 0, 4096, KT), A[f"moe_w{w}"][0, ex, :, FC * c:FC * c + FC]
                    sp.dma_start(dst, src.rearrange("e (k p) c -> p (e k) c", p=P)).then_inc(arrived[u % RING], 16)

            sp.wait_ge(S["par_free"], DEPTH + 1)
            sp.dma_start(fnorm, A["final_norm"].rearrange("(e d) -> e d", e=1).broadcast_to([P, D]))\
              .then_inc(S["loaded_fnorm"], 16)
            sp.dma_start(yrow, A["norm_ffn"][DEPTH - 1:DEPTH, :].broadcast_to([P, D])).then_inc(S["loaded_nffn"], 16)
            with sp.Fori(0, N_EXP) as j:
                job_loads(j, j)
            sp.wait_ge(S["jobs_ready"], 1)
            n_jobs = sp.value_load(tabi[0:1, 0:1], min_val=N_EXP, max_val=MAX_JOBS)
            with sp.If(n_jobs > N_EXP):
                with sp.Fori(N_EXP, n_jobs) as j:
                    e = sp.value_load(tabi[0:1, bass.ds(j - (N_EXP - 1), 1)], min_val=0, max_val=N_EXP - 1)
                    job_loads(j, e)
            sp.wait_ge(S["fin"], 1)
            sp.dma_start(out[0].rearrange("(t p) d -> p t d", p=P), xr).then_inc(S["stored"], 16)
            sp.wait_ge(S["stored"], 16)

        @block.gpsimd
        def _(gp):
            link, restart = chain(gp, S["g_chain"])

            def take_wait():
                link(gp.tensor_tensor(tick[:, 0:1], tick[:, 1:2], tick[:, 1:2], ALU.add))
            link(gp.memset(tick[:, :], 0.0))
            gp.memset(zeros[:, :], 0.0).then_inc(S["zeroed"], 1)
            link(gp.memset(bu[:, :, 0:PAD], 0.0))
            link(gp.memset(pw1[:, :, 0:PAD], 0.0))
            link(gp.memset(pw2[:, :, 0:PAD], 0.0))
            gp.memset(pwbd[:, :, :], 0.0).then_inc(S["par_free"], 1)
            gp.wait_ge(S["zeroed"], 1)
            gp.wait_ge(S["loaded_const"], 96)
            link(gp.tensor_copy(gmask[:, :], uvg[:, 1, :]))
            with gp.Fori(0, DEPTH) as layer:
                L1 = gp.snap(layer + 1)
                first, second = gp.snap(layer * 2 + 1), gp.snap(layer * 2 + 2)
                landed1 = gp.snap(layer * (16 * LAYER_TURNS) + 32)
                restart()
                gp.wait_ge(S["scored"], second)
                take_wait()
                gp.memset(r2[:, :], 0.0).then_inc(S["r2_zero"], 1)
                gp.wait_ge(S["pcol_done"], L1)
                gp.wait_ge(arrived[U_WKV], landed1)
                take_wait()
                for k in range(KT):
                    w = ring[:, U_WKV, 512 * k:512 * k + 512]
                    i = gp.tensor_scalar(w, w, pcol[:, R_MEM + k:R_MEM + k + 1], None, ALU.mult)
                i.then_inc(S["wkv_scaled"], 1)
                gp.wait_ge(g_ev["bu"], L1)
                t1 = slice(PAD, PAD + SEQ)

                def shifted(k):
                    return slice(PAD - k, PAD + SEQ - k)
                inv = v3(cc("inv"), 0, 512, 2)

                def mean_less_self(src, p0, m):
                    link(gp.tensor_tensor(src[p0:p0 + 64, m, t1], src[p0:p0 + 64, m, t1], inv[p0:p0 + 64, m, :],
                                          ALU.mult))
                    return gp.tensor_tensor(bu[p0:p0 + 64, m, t1], src[p0:p0 + 64, m, t1], bu[p0:p0 + 64, m, t1],
                                            ALU.subtract)
                link(gp.tensor_tensor(pw1[:, :, t1], bu[:, :, t1], bu[:, :, shifted(1)], ALU.add))
                link(gp.tensor_tensor(pw2[:, :, t1], pw1[:, :, t1], pw1[:, :, shifted(2)], ALU.add))
                link(mean_less_self(pw1, 0, 0))
                link(mean_less_self(pw2, 64, 0))
                link(gp.tensor_tensor(pw1[:, 1, t1], pw2[:, 1, t1], pw2[:, 1, shifted(4)], ALU.add))
                link(gp.tensor_tensor(pw2[:, 1, t1], pw1[:, 1, t1], pw1[:, 1, shifted(8)], ALU.add))
                link(mean_less_self(pw1, 0, 1))
                mean_less_self(pw2, 64, 1).then_inc(S["pool_out"], 1)
                gp.wait_ge(S["pool_out"], L1)

        @block.scalar
        def _(act):
            link, restart = chain(act, S["a_chain"])

            def norm(src, junk, n, g0):
                link(act.activation(junk, src[:, 0, :], ACT.Square, accum_out=ss[:, 0:1]))
                act.activation(junk, src[:, 1, :], ACT.Square, accum_out=ss[:, 1:2]).then_inc(S["ss_ready"], 1)
                act.wait_ge(S["ms_ready"], n)
                act.activation(rs, ms, ACT.Sqrt).then_inc(S["rstd_ready"], 1)
                act.wait_ge(S["xT_ps"], n)
                dst = memT if g0 is None else xnT
                for kt in range(KT // 2, KT):
                    i = act.activation(dst[:, kt, :], xT(kt), ACT.Copy,
                                       scale=1.0 if g0 is None else pcol[:, g0 + kt:g0 + kt + 1])
                i.then_inc(S["xT_a"], 1)

            act.wait_ge(S["loaded_mem"], 16)
            norm(xr, xnf[:, 0:1024], 1, None)
            act.wait_ge(S["bias_ps"], 1)
            link(act.activation(gla[0:HEADS, 512:896], ps[4][0:HEADS, 0:384], ACT.Copy))
            act.dma_start(rev[:, :], gla[0:HEADS, 512:896]).then_inc(S["bias_rows"], 16)
            act.wait_ge(S["bias_rows"], 16)
            act.dma_start(hank, bass.AP(rev, 0, [[1, P], [384, HEADS], [1, 256]])).then_inc(S["bias_hank"], 16)
            act.wait_ge(S["hank_ps"], 1)
            for i2 in range(2):
                i = act.activation(bias[:, 2 * i2:2 * i2 + 2, :], v3(ps[5 + i2], 0, 512, 2), ACT.Copy)
            i.then_inc(S["bias_done"], 1)
            act.wait_ge(S["loaded_h"], 16)

            with act.Fori(0, DEPTH) as layer:
                L1 = act.snap(layer + 1)
                first, second = act.snap(layer * 2 + 1), act.snap(layer * 2 + 2)
                ended = [act.snap(layer * LAYER_TURNS + (t + 2)) for t in range(2)]

                def group(name):
                    act.wait_ge(g_ps[name], ended[ENDS[name][1]] if name in ENDS else L1)
                nv = [act.snap(layer * 3 + (u + 2)) for u in range(3)]
                hv = [act.snap(layer * 3 + (u + 1)) for u in range(3)]
                restart()

                def out_of(name, dst, src, func=ACT.Copy):
                    group(name)
                    act.activation(dst, src, func).then_inc(g_ev[name], 1)

                act.wait_ge(S["pcol_ps"], L1)
                act.activation(pcol[:, :], ps[7][:, 0:N_ROWS], ACT.Copy).then_inc(S["pcol_done"], 1)
                act.wait_ge(S["pcol_done"], L1)
                act.wait_ge(S["ws_ps"], L1)
                act.activation(wsT[:, :, :], v3(ps[6], 0, 512, 4), ACT.Copy).then_inc(S["ws_done"], 1)
                act.wait_ge(S["h_upd"], hv[0])
                norm(h, r2[:, 0:1024], nv[0], R_MIX)
                group("ki")
                for q in range(4):
                    act.activation(kiT[32 * q:32 * q + 32, :], ps[5][0:32, 0:256], ACT.Copy)
                act.activation(wis[:, :, :], v3(ps[5], 256, 272, 2), ACT.Copy,
                               scale=float(IDX_HEADS ** -0.5 * IDX_DIM ** -0.5)).then_inc(g_ev["ki"], 1)
                act.wait_ge(S["dots_ps"], first)
                for b in range(4):
                    i = act.activation(rel[:, b:8:4, :], v3(ps[b], 0, 512, 2), ACT.Relu)
                i.then_inc(S["rel"], 1)
                out_of("a", gla[:, 0:512], ps[6][:, :])
                out_of("av", av[:, :, :], v3(ps[7], 0, 512, 2))
                act.wait_ge(S["dots_ps"], second)
                act.wait_ge(S["scored"], first)
                for b in range(4):
                    i = act.activation(rel[:, b:8:4, 0:P], v3(ps[b], 0, 512, 2)[:, :, 0:P], ACT.Relu)
                i.then_inc(S["rel"], 1)
                out_of("ag", sg[:, :, :], v3(ps[5], 0, 512, 2), ACT.Silu)
                act.wait_ge(S["la_ready"], L1)
                link(act.activation(eb, la, ACT.Abs))
                link(act.activation(enb, eb, ACT.Exp, scale=-1.0))
                act.activation(eb, enb, ACT.Ln, bias=1.0).then_inc(S["ls_ready"], 1)
                act.wait_ge(S["b_ready"], L1)
                act.activation(eb, bs, ACT.Exp, scale=1.0 / 16.0)
                act.activation(enb, bs, ACT.Exp, scale=-1.0 / 16.0).then_inc(S["eb_ready"], 1)
                act.wait_ge(S["qe_ready"], L1)
                act.wait_ge(S["r2_zero"], L1)
                for q in range(4):
                    i = act.activation(qbd[32 * q:32 * q + 32, :, q, :],
                                       aqT[32 * q:32 * q + 32, :].rearrange("p (t i) -> p t i", t=2), ACT.Copy)
                i.then_inc(S["qbd_done"], 1)
                out_of("k", kT[:, :, :], v3(ps[4], 0, 512, 2))
                act.wait_ge(S["kd_ps"], L1)
                act.activation(kdr, v3(ps[2], 0, 256, 2), ACT.Copy).then_inc(S["kdr_done"], 1)
                out_of("bu", bu[:, :, PAD:PAD + SEQ], v3(ps[6], 0, 512, 2))
                out_of("uv0", uvg[:, 0, :], ps[7][:, :], ACT.Gelu_apprx_tanh)
                out_of("uv1", uvg[:, 1, :], ps[4][:, :], ACT.Gelu_apprx_tanh)
                act.wait_ge(S["vms"], L1)
                act.activation(s_vr, s_vm, ACT.Sqrt).then_inc(S["vr"], 1)
                out_of("kx", kxT[:, :, :], v3(ps[5], 0, 512, 2))
                act.wait_ge(S["o_ps"], L1)
                for t in range(TT):
                    i = act.activation(osq[:, t, :], ps[t][:, 0:256], ACT.Square)
                i.then_inc(S["osq"], 1)
                act.wait_ge(S["ms_gla"], L1)
                act.activation(s_or, s_og, ACT.Sqrt).then_inc(S["r_gla"], 1)
                for t in (1, 0):
                    act.wait_ge(S["lg"], first if t else second)
                    for hh in range(HEADS):
                        k = 4 * t + hh
                        i = act.activation(prb[t][:, hh, :], lgm[t][:, hh, :], ACT.Exp, bias=s_mx[:, k:k + 1],
                                           accum_out=s_sum[:, k:k + 1])
                    i.then_inc(S["p"], 1)
                act.wait_ge(S["pt1_ps"], L1)
                act.activation(pT_mix[1][:, 4:8, :], v3(ps[1], 0, 512, 4), ACT.Copy).then_inc(S["pt1_a"], 1)
                act.wait_ge(S["mt_ps"], L1)
                act.activation(mixT[:, 6:8, :], v3(ps[6], 0, 512, 2), ACT.Copy).then_inc(S["mt_a"], 1)

                act.wait_ge(S["h_upd"], hv[1])
                norm(h, r2[:, 0:1024], nv[1], R_XA)
                out_of("xq", qT[:, :, :], v3(ps[4], 0, 512, 2))
                for t in range(TT):
                    act.wait_ge(S["xmx"], second if t else first)
                    for hh in range(HEADS):
                        k = 4 * t + hh
                        c0 = 256 * (hh // 2)
                        i = act.activation(prx[t][:, hh, :], ps[2 * t + hh % 2][:, c0:c0 + 256], ACT.Exp,
                                           bias=s_mx[:, k:k + 1], scale=float(DH ** -0.5), accum_out=s_sum[:, k:k + 1])
                    i.then_inc(S["xp"], 1)
                for t in range(TT):
                    act.wait_ge(S["xpt_ps"], second if t else first)
                    act.activation(pT_x[t][:, 4:8, :], v3(ps[5 + 2 * t], 0, 512, 4), ACT.Copy)\
                       .then_inc(S["xpt_a"], 1)

                act.wait_ge(S["h_upd"], hv[2])
                norm(h, r2[:, 0:1024], nv[2], R_FFN)
                with act.If(layer < 1):
                    for f in range(FF // P):
                        act.wait_ge(S["f_h"], f + 1)
                        act.activation(f_sil[:, f % 2, :], ps[f % 2][:, 0:256], ACT.Silu).then_inc(S["f_s"], 1)

            act.wait_ge(S["top_diff"], 1)
            act.activation(s_e, s_d, ACT.Exp).then_inc(S["top_exp"], 1)
            act.wait_ge(S["jobs_ready"], 1)
            n_jobs = act.value_load(tabi[0:1, 0:1], min_val=N_EXP, max_val=MAX_JOBS)

            def gather_hi(n):
                act.wait_ge(S["j_gps"], n)
                for b in range(2):
                    i = act.activation(xg_hi[:, 4 * b:4 * b + 4, :], v3(ps[2 + b], 0, 512, 4), ACT.Copy)
                i.then_inc(S["j_gh"], 1)

            def yrow_out(n):
                act.wait_ge(S["j_yps"], n)
                act.activation(yrow[:, 512:1024], ps[7][:, :], ACT.Copy).then_inc(S["j_ya"], 1)

            def transposed(n):
                act.wait_ge(S["j_tps"], n)
                act.activation(at_hi[:, :, :], v3(ps[4], 0, 512, 4), ACT.Copy).then_inc(S["j_th"], 1)

            gather_hi(1)
            with act.Fori(0, n_jobs) as j:
                cn = [act.snap(j * NCH + (c + 1)) for c in range(NCH)]
                j1, j2, pieces = act.snap(j + 1), act.snap(j + 2), act.snap(j * JOB_PIECES)
                landed = [act.snap(j * (16 * JOB_TURNS) + 16 * (2 * LAYER_TURNS - 3 + t + 1)) for t in range(JOB_TURNS)]
                for i in range(JOB_PIECES):
                    if i == NB - 1:
                        yrow_out(j1)
                    for c in range(NCH):
                        if i == after((1, c)):
                            act.wait_ge(S["j_h1"], cn[c])
                            act.activation(j_sil[c % 2], ps[2 * (c % 2)][:, :], ACT.Silu).then_inc(S["j_s"], 1)
                        if c < NCH - 1 and i == after((1, c + 1)) + 1:
                            transposed(cn[c])
                    if i == JOB_PIECES - 1:
                        transposed(cn[NCH - 1])
                    u, q = i // QP, i % QP
                    if q == 0:
                        act.wait_ge(arrived[u % RING], landed[u // RING])
                    act.wait_ge(S["piece_free"], pieces + (i + 1))
                    act.activation(w_hi[:, i % NB, :], ring[:, u % RING, PIECE * q:PIECE * q + PIECE], ACT.Copy)\
                       .then_inc(S["hi_ready"], 1)
                gather_hi(j2)
            yrow_out(n_jobs + 1)
            act.wait_ge(S["fin_ms"], 1)
            act.activation(rs, ms, ACT.Sqrt).then_inc(S["fin_r"], 1)

        @block.vector
        def _(dve):
            link, restart = chain(dve, S["v_chain"])
            mult, add, sub, amax, amin = ALU.mult, ALU.add, ALU.subtract, ALU.max, ALU.min

            def inverse_mean(dst, src, n):
                link(dve.tensor_scalar(dst, src, 1.0 / n, EPS, mult, add))
                return dve.reciprocal(dst, dst)

            def norm(src, n, g0):
                dve.wait_ge(S["ss_ready"], n)
                inverse_mean(ms, ss, D).then_inc(S["ms_ready"], 1)
                dve.wait_ge(S["rstd_ready"], n)
                for t in range(TT):
                    i = dve.tensor_scalar(xr[:, t, :], src[:, t, :], rs[:, t:t + 1], None, mult)
                i.then_inc(S["xr_ready"], 1)
                dve.wait_ge(S["xT_ps"], n)
                dst = memT if g0 is None else xnT
                for kt in range(KT // 2):
                    i = dve.tensor_scalar(dst[:, kt, :], xT(kt),
                                          1.0 if g0 is None else pcol[:, g0 + kt:g0 + kt + 1], None, mult)
                i.then_inc(S["xT_v"], 1)

            def add_rows(banks):
                for k, b in enumerate(banks):
                    dst = h[:, k // 2, 512 * (k % 2):512 * (k % 2) + 512]
                    i = dve.tensor_tensor(dst, dst, ps[b][:, :], add)
                return i

            dve.wait_ge(S["loaded_h"], 16)
            dve.sem_inc(S["h_upd"], 1)
            dve.wait_ge(S["loaded_mem"], 16)
            norm(xr, 1, None)

            with dve.Fori(0, DEPTH) as layer:
                L1 = dve.snap(layer + 1)
                first, second = dve.snap(layer * 2 + 1), dve.snap(layer * 2 + 2)
                ended = [dve.snap(layer * LAYER_TURNS + (t + 2)) for t in range(2)]

                def group(name):
                    dve.wait_ge(g_ps[name], ended[ENDS[name][1]] if name in ENDS else L1)
                nv = [dve.snap(layer * 3 + (u + 2)) for u in range(3)]
                par = dve.snap(layer * 272 + 272)
                restart()

                def out_of(name, dst, src):
                    group(name)
                    dve.tensor_copy(dst, src).then_inc(g_ev[name], 1)

                dve.wait_ge(S["loaded_const"], 96)
                dve.wait_ge(S["loaded_par"], par)
                for g in range(4):
                    i = dve.tensor_tensor(wsr[:, g, :], wsr[:, g, :], cc("tril"), mult)
                i.then_inc(S["wsm_done"], 1)
                dve.wait_ge(S["pcol_done"], L1)
                norm(h, nv[0], R_MIX)
                out_of("qi", qiT, v3(ps[4], 0, 512, 2))
                dve.wait_ge(g_ev["ki"], L1)

                def score_and_take(t, n):
                    sc = score[:, t, 0:n]
                    vis = cc("vis", 256 - n)
                    dve.wait_ge(S["rel"], first if t else second)
                    for hh in range(IDX_HEADS):
                        i = dve.scalar_tensor_tensor(sc, rel[:, hh, 0:n], wis[:, t, hh:hh + 1], vis if hh == 0 else sc,
                                                     mult, add)
                        if hh < IDX_HEADS - 1:
                            link(i)
                    link(i)
                    dve.memset(st[:, 95:96], 0.0).then_inc(S["scored"], 1)
                    for _ in range(TOPK // 8):
                        link(dve.max(m8[:, :], sc))
                        link(dve.match_replace(sc, m8[:, :], sc, MARK))
                    link(dve.tensor_scalar(sc, sc, HALF, -1.0e30, ALU.is_gt, mult))
                    link(dve.tensor_tensor(sc, sc, vis, add))

                score_and_take(1, 256)
                score_and_take(0, P)

                out_of("lr", lrT, ps[4][0:GLA_RANK, 0:256])
                group("logit")
                dve.tensor_scalar(la, ps[6][:, 0:256], pcol[:, R_BA:R_BA + 1], None, add).then_inc(S["la_ready"], 1)
                dve.wait_ge(S["ls_ready"], L1)
                link(dve.scalar_tensor_tensor(la, la, 0.0, eb, amin, sub))
                dve.tensor_tensor_scan(bs, cc("reset"), la, 0.0, mult, add).then_inc(S["b_ready"], 1)
                dve.wait_ge(S["eb_ready"], L1)
                dve.scalar_tensor_tensor(aqT, aqT, float(GLA_DK ** -0.5), eb, mult, mult).then_inc(S["qe_ready"], 1)
                link(dve.tensor_tensor(akT, akT, enb, mult))
                last = v3(eb, 0, 256, 4)[:, :, CHUNK - 1:CHUNK]
                dve.tensor_tensor(v3(kdT, 0, 256, 4), v3(akT, 0, 256, 4), last.broadcast_to([P, 4, CHUNK]), mult)\
                   .then_inc(S["kd_ready"], 1)
                out_of("q", qT[:, :, :], v3(ps[7], 0, 512, 2))
                out_of("cv", cv[:, :, :], v3(ps[5], 0, 512, 2))
                dve.wait_ge(S["att_ps"], L1)
                dve.wait_ge(S["r2_zero"], L1)
                dve.wait_ge(g_ev["ag"], L1)
                for t in range(TT):
                    link(dve.tensor_tensor(sg[:, t, :], sg[:, t, :], bc[:, 0, :], mult))
                for t in range(TT):
                    i = dve.copy_predicated(attT[:, t, :], gmask[:, :], ps[t][:, :])
                i.then_inc(S["att_done"], 1)
                for t in range(TT):
                    dve.wait_ge(g_ev[f"uv{t}"], L1)
                    link(dve.bn_stats(s_bn[:, 6 * t:6 * t + 6], uvg[:, t, 256:512]))
                    link(dve.bn_aggr(s_ag[:, 2 * t:2 * t + 2], s_bn[:, 6 * t:6 * t + 6]))
                inverse_mean(s_vm, s_ag[:, 1:4:2], 1).then_inc(S["vms"], 1)
                dve.wait_ge(S["kv_ps"], L1)
                kv = (ps[3][:, 0:256], ps[2][:, 256:512], ps[3][:, 256:512])
                for n in range(3):
                    link(dve.tensor_tensor(Sst[:, n, :], kv[n], cc("bd"), mult))
                for n in (1, 2):
                    e = CHUNK * (n + 1) - 1
                    i = dve.scalar_tensor_tensor(Sst[:, n, :], Sst[:, n - 1, :], eb[:, e:e + 1], Sst[:, n, :], mult, add)
                    if n == 1:
                        link(i)
                i.then_inc(S["s_ready"], 1)
                dve.wait_ge(S["vr"], L1)
                for t in range(TT):
                    link(dve.tensor_scalar(vn[:, t, :], vn[:, t, :], s_ag[:, 2 * t:2 * t + 1], s_vr[:, t:t + 1],
                                           sub, mult))
                    link(dve.tensor_tensor(vn[:, t, :], vn[:, t, :], bc[:, 1, :], mult))
                    i = dve.tensor_tensor(vn[:, t, :], vn[:, t, :], bc[:, 2, :], add)
                i.then_inc(S["vn_done"], 1)
                out_of("vx", vx[:, :, :], v3(ps[6], 0, 512, 2))
                dve.wait_ge(S["osq"], L1)
                link(dve.tensor_reduce(s_og, osq.rearrange("p t (h v) -> p (t h) v", h=HEADS), AX, add))
                inverse_mean(s_og, s_og, GLA_DV).then_inc(S["ms_gla"], 1)
                dve.wait_ge(S["r_gla"], L1)
                for t in range(TT):
                    i = dve.tensor_tensor(v3(sg[:, t, :], 0, 256, 4), v3(sg[:, t, :], 0, 256, 4),
                                          s_or[:, 4 * t:4 * t + 4].unsqueeze(2).broadcast_to([P, 4, GLA_DV]), mult)
                    link(i)
                for t in range(TT):
                    i = dve.tensor_tensor(sg[:, t, :], sg[:, t, :], ps[t][:, 0:256], mult)
                i.then_inc(S["og_done"], 1)
                dve.wait_ge(S["sg_ps"], L1)
                for t in range(TT):
                    for g in range(4):
                        dst = uvg[:, t, 64 * g:64 * g + 64]
                        i = dve.scalar_tensor_tensor(dst, ps[2 + t][:, 64 * g:64 * g + 64],
                                                     pcol[:, R_SB + g:R_SB + g + 1], dst, add, mult)
                i.then_inc(S["od_done"], 1)
                group("y")
                for m in range(2):
                    i = dve.tensor_scalar(mixT[:, 2 + m, :], ps[7][:, 256 * m:256 * m + 256],
                                          pcol[:, R_PB + m:R_PB + m + 1], pcol[:, R_PS + m:R_PS + m + 1], add, mult)
                i.then_inc(g_ev["y"], 1)
                dve.wait_ge(S["bias_done"], 1)
                for t, n in ((1, 256), (0, P)):
                    link(dve.tensor_tensor(lgm[t], bias[:, :, 256 - n:256],
                                           score[:, t, 0:n].unsqueeze(1).broadcast_to([P, HEADS, n]), add))
                    dve.wait_ge(S["lg_ps"], first if t else second)
                    for b in range(2):
                        bank = ps[4 + b if t else 6 + b]
                        link(dve.scalar_tensor_tensor(lgm[t][:, b:4:2, :], v3(bank, 0, 2 * n, 2), float(DH ** -0.5),
                                                      lgm[t][:, b:4:2, :], mult, add))
                    link(dve.tensor_reduce(s_mx[:, 4 * t:4 * t + 4], lgm[t], AX, amax))
                    dve.tensor_scalar(s_mx[:, 4 * t:4 * t + 4], s_mx[:, 4 * t:4 * t + 4], -1.0, None, mult)\
                       .then_inc(S["lg"], 1)
                dve.wait_ge(S["pt1_ps"], L1)
                dve.tensor_copy(pT_mix[1][:, 0:4, :], v3(ps[0], 0, 512, 4)).then_inc(S["pt1_v"], 1)
                dve.wait_ge(S["pt0_ps"], L1)
                dve.tensor_copy(pT_mix[0], v3(ps[2], 0, 512, 4)).then_inc(S["pt0_v"], 1)
                dve.wait_ge(S["p"], second)
                link(dve.reciprocal(s_rec, s_sum))
                dve.wait_ge(S["pv_ps"], L1)
                for t in range(TT):
                    i = dve.tensor_tensor(v3(oc[:, t, :], 0, 256, 4), v3(ps[3], 256 * t, 256 * t + 256, 4),
                                          s_rec[:, 4 * t:4 * t + 4].unsqueeze(2).broadcast_to([P, 4, DH]), mult)
                i.then_inc(S["oc_done"], 1)
                dve.wait_ge(S["mt_ps"], L1)
                dve.tensor_copy(mixT[:, 0:2, :], v3(ps[4], 0, 512, 2))
                dve.tensor_copy(mixT[:, 4:6, :], v3(ps[5], 0, 512, 2)).then_inc(S["mt_v"], 1)
                group("wout")
                add_rows((0, 1, 2, 3)).then_inc(S["h_upd"], 1)
                dve.wait_ge(S["h_upd"], nv[0])
                dve.sem_inc(S["par_free"], 1)

                norm(h, nv[1], R_XA)
                for t in range(TT):
                    dve.wait_ge(S["xlg_ps"], second if t else first)
                    for b in range(2):
                        link(dve.tensor_reduce(s_mx[:, 4 * t + b:4 * t + 4:2], v3(ps[2 * t + b], 0, 512, 2), AX, amax))
                    dve.tensor_scalar(s_mx[:, 4 * t:4 * t + 4], s_mx[:, 4 * t:4 * t + 4], -float(DH ** -0.5), None, mult)\
                       .then_inc(S["xmx"], 1)
                for t in range(TT):
                    dve.wait_ge(S["xpt_ps"], second if t else first)
                    dve.tensor_copy(pT_x[t][:, 0:4, :], v3(ps[4 + 2 * t], 0, 512, 4)).then_inc(S["xpt_v"], 1)
                dve.wait_ge(S["xp"], second)
                link(dve.reciprocal(s_rec, s_sum))
                dve.wait_ge(S["xpv_ps"], L1)
                for t in range(TT):
                    i = dve.tensor_tensor(v3(oc[:, t, :], 0, 256, 4), v3(ps[2 * t], 0, 256, 4),
                                          s_rec[:, 4 * t:4 * t + 4].unsqueeze(2).broadcast_to([P, 4, DH]), mult)
                i.then_inc(S["ox_done"], 1)
                dve.wait_ge(S["xo_ps"], L1)
                dve.tensor_copy(oxT[:, :, :], v3(ps[1], 0, 512, 2)).then_inc(S["xo_done"], 1)
                group("xout")
                add_rows((4, 5, 6, 7)).then_inc(S["h_upd"], 1)
                dve.wait_ge(S["h_upd"], nv[1])

                norm(h, nv[2], R_FFN)
                with dve.If(layer < 1):
                    for f in range(FF // P):
                        dve.wait_ge(S["f_s"], f + 1)
                        dve.tensor_tensor(f_act[:, f % 2, :], f_sil[:, f % 2, :], ps[f % 2][:, 256:512], mult)\
                           .then_inc(S["f_a"], 1)
                    dve.wait_ge(slot_free[RING - 1], LAYER_TURNS + 1)
                    add_rows((4, 5, 6, 7)).then_inc(S["h_upd"], 1)
                    dve.wait_ge(S["h_upd"], 4)

            restart()
            scf = score[:, :, :].rearrange("p a b -> p (a b)")

            def r3(i):
                return v3(scf, 16 * i, 16 * i + 16, 2)
            lg, eq, k1, lg2, k2, sel, gate, pos, tmp = (r3(i) for i in range(9))
            best = [scf[:, 160 + 2 * i:162 + 2 * i] for i in range(4)]

            def rep(v):
                return v.unsqueeze(2).broadcast_to([P, TT, N_EXP])

            def per_tile(v):
                return v.unsqueeze(1).broadcast_to([P, TT, N_EXP])
            dve.wait_ge(S["rlog_ps"], 1)
            link(dve.tensor_copy(lg, v3(ps[4], 0, 16, 2)))

            def first_best(src, top, first, hot1):
                link(dve.tensor_reduce(top, src, AX, amax))
                link(dve.tensor_tensor(eq, src, rep(top), ALU.is_equal))
                link(dve.tensor_tensor(eq, eq, per_tile(cc("erev")), mult))
                link(dve.tensor_reduce(first, eq, AX, amax))
                link(dve.tensor_tensor(hot1, eq, rep(first), ALU.is_equal))
            first_best(lg, best[0], best[1], k1)
            link(dve.scalar_tensor_tensor(lg2, k1, NEG, lg, mult, add))
            first_best(lg2, best[2], best[3], k2)
            dve.tensor_tensor(s_d, best[2], best[0], sub).then_inc(S["top_diff"], 1)
            dve.tensor_tensor(sel, k1, k2, add).then_inc(S["sel_ready"], 1)
            dve.wait_ge(S["top_exp"], 1)
            link(dve.tensor_scalar(s_g[:, 0:2], s_e, 1.0, None, add))
            link(dve.reciprocal(s_g[:, 0:2], s_g[:, 0:2]))
            link(dve.tensor_tensor(s_g[:, 2:4], s_e, s_g[:, 0:2], mult))
            link(dve.tensor_tensor(k1, k1, rep(s_g[:, 0:2]), mult))
            link(dve.tensor_tensor(k2, k2, rep(s_g[:, 2:4]), mult))
            link(dve.tensor_tensor(gate, k1, k2, add))
            dve.wait_ge(S["sel_ready"], 1)
            dve.wait_ge(S["rank_ps"], 1)
            link(dve.scalar_tensor_tensor(pos, sel, 1000.0, v3(ps[5], 0, 16, 2), mult, add))
            link(dve.tensor_scalar(pos, pos, 1000.0, None, sub))
            link(dve.memset(jobt[:, :, 0, MAX_JOBS:], -1.0))
            link(dve.memset(jobt[:, :, 1, MAX_JOBS:], 0.0))
            link(dve.tensor_copy(jobt[:, :, 0, 0:N_EXP], pos))
            link(dve.tensor_copy(jobt[:, :, 1, 0:N_EXP], gate))
            over, upto, pick, one = (scf[:, 192 + 8 * i:200 + 8 * i] for i in range(4))
            cnt = scf[:, 224:230]
            link(dve.tensor_scalar(over, ps[5][:, 16:24], float(P), None, ALU.is_gt))
            link(dve.tensor_tensor_scan(upto, cc("ones", 0, 8), over, 0.0, mult, add))
            for x in range(MAX_JOBS - N_EXP):
                link(dve.scalar_tensor_tensor(pick, upto, float(x + 1), over, ALU.is_equal, mult))
                for k, src in ((0, pos), (1, gate)):
                    link(dve.tensor_tensor(tmp, src, per_tile(pick), mult))
                    link(dve.tensor_reduce(cnt[:, 0:2], tmp, AX, add))
                    link(dve.tensor_scalar(jobt[:, :, k, N_EXP + x:N_EXP + x + 1], cnt[:, 0:2].unsqueeze(2),
                                           float(-P if k == 0 else 0), None, add))
                link(dve.tensor_tensor(one, pick, cc("eidx"), mult))
                link(dve.tensor_reduce(cnt[:, 3 + x:4 + x], one, AX, add))
            link(dve.tensor_scalar(cnt[:, 2:3], upto[:, 7:8], float(N_EXP), None, add))
            dve.tensor_copy(tabi[0:1, 0:4], cnt[0:1, 2:6]).then_inc(S["jobs_ready"], 1)
            dve.wait_ge(S["jobs_ready"], 1)
            n_jobs = dve.value_load(tabi[0:1, 0:1], min_val=N_EXP, max_val=MAX_JOBS)

            def slots_of(dst, j, gated):
                for t in range(TT):
                    i = dve.tensor_scalar(dst[:, t, :], cc("iota"), jobt[:, t, 0, bass.ds(j, 1)],
                                          jobt[:, t, 1, bass.ds(j, 1)] if gated else None,
                                          ALU.is_equal, mult if gated else ALU.bypass)
                return i

            def gather_lo(n):
                dve.wait_ge(S["j_gh"], n)
                for b in range(2):
                    i = dve.tensor_tensor(xg_lo[:, 4 * b:4 * b + 4, :], v3(ps[2 + b], 0, 512, 4),
                                          xg_hi[:, 4 * b:4 * b + 4, :], sub)
                i.then_inc(S["j_gl"], 1)

            def yrow_out(n):
                dve.wait_ge(S["j_yps"], n)
                dve.tensor_copy(yrow[:, 0:512], ps[6][:, :]).then_inc(S["j_yv"], 1)

            def transposed(n):
                dve.wait_ge(S["j_th"], n)
                dve.tensor_tensor(at_lo[:, :, :], v3(ps[4], 0, 512, 4), at_hi[:, :, :], sub).then_inc(S["j_t"], 1)

            def combined(n):
                dve.wait_ge(S["j_c1"], n)
                add_rows((4, 5, 6, 7)).then_inc(S["j_cv"], 1)

            dve.wait_ge(S["loaded_nffn"], 16)
            for t in range(TT):
                dve.tensor_tensor(xr[:, t, :], xr[:, t, :], yrow, mult)
            slots_of(hot, 0, False).then_inc(S["j_g"], 1)
            dve.memset(hotgT, 0.0).then_inc(S["j_gt"], 1)
            gather_lo(1)
            with dve.Fori(0, n_jobs) as j:
                cn = [dve.snap(j * NCH + (c + 1)) for c in range(NCH)]
                j1, j2, pieces = dve.snap(j + 1), dve.snap(j + 2), dve.snap(j * JOB_PIECES)
                for i in range(JOB_PIECES):
                    if i == NB - 1:
                        yrow_out(j1)
                    for c in range(NCH):
                        if i == after((3, c)):
                            dve.wait_ge(S["j_s"], cn[c])
                            dve.wait_ge(S["j_h3"], cn[c])
                            dve.tensor_tensor(j_act, j_sil[c % 2], ps[2 * (c % 2) + 1][:, :], mult).then_inc(S["j_a"], 1)
                        if c < NCH - 1 and i == after((1, c + 1)) + 1:
                            transposed(cn[c])
                    if i == after((3, 0)):
                        combined(j1)
                        slots_of(hotg, j, True)
                        slots_of(hot, j1, False).then_inc(S["j_g"], 1)
                    if i == JOB_PIECES - 1:
                        transposed(cn[NCH - 1])
                    u, q = i // QP, i % QP
                    dve.wait_ge(S["hi_ready"], pieces + (i + 1))
                    dve.tensor_tensor(w_lo[:, i % NB, :], ring[:, u % RING, PIECE * q:PIECE * q + PIECE],
                                      w_hi[:, i % NB, :], sub).then_inc(S["lo_ready"], 1)
                gather_lo(j2)
                dve.wait_ge(S["j_gtps"], j1)
                dve.tensor_copy(hotgT, v3(ps[5], 0, 256, 2)).then_inc(S["j_gt"], 1)
            yrow_out(n_jobs + 1)
            combined(n_jobs + 1)
            dve.wait_ge(S["j_cv"], n_jobs + 1)
            dve.memset(st[:, 95:96], 0.0)

            restart()
            for t in range(TT):
                link(dve.tensor_tensor_reduce(out=xr[:, t, :], in0=h[:, t, :], in1=h[:, t, :], scale=1.0, scalar=0.0,
                                              op0=mult, op1=add, accum_out=ss[:, t:t + 1]))
            inverse_mean(ms, ss, D).then_inc(S["fin_ms"], 1)
            dve.wait_ge(S["fin_r"], 1)
            dve.wait_ge(S["loaded_fnorm"], 16)
            for t in range(TT):
                i = dve.scalar_tensor_tensor(xr[:, t, :], h[:, t, :], rs[:, t:t + 1], fnorm, mult, mult)
            i.then_inc(S["fin"], 1)

        @block.tensor
        def _(pe):
            mm = pe.matmul

            def transposes(n):
                pe.wait_ge(S["xr_ready"], n)
                for kt in range(KT):
                    for t in range(TT):
                        c0 = 256 * (kt % 2) + P * t
                        i = pe.transpose(ps[kt // 2][:, c0:c0 + P], xr[:, t, P * kt:P * kt + P], ident)
                i.then_inc(S["xT_ps"], 1)
                pe.wait_ge(S["xT_v"], n)
                pe.wait_ge(S["xT_a"], n)

            def on_features(dst, w, src=xnT):
                for k in range(KT):
                    i = mm(dst, w[:, k, :], src[:, k, :], start=k == 0, stop=k == KT - 1)
                return i

            def on_tokens(dst, w, t, src=xnT):
                for k in range(KT):
                    i = mm(dst, src[:, k, P * t:P * t + P], w[:, k, :], start=k == 0, stop=k == KT - 1)
                return i

            pe.wait_ge(S["loaded_const"], 96)
            for s in range(RING):
                pe.sem_inc(slot_free[s], 1)
            transposes(1)
            mm(ps[4][0:HEADS, 0:384], kdec[0:BUCKETS, 0:HEADS], gla[0:BUCKETS, 0:384], start=True, stop=True)\
                .then_inc(S["bias_ps"], 1)
            pe.wait_ge(S["bias_hank"], 16)
            for i2 in range(2):
                i = mm(ps[5 + i2][:, :], glab[:, 0:P], hank[:, 2 * i2:2 * i2 + 2, :], start=True, stop=True)
            i.then_inc(S["hank_ps"], 1)
            pe.wait_ge(S["bias_done"], 1)

            with pe.Fori(0, DEPTH) as layer:
                L1 = pe.snap(layer + 1)
                first, second = pe.snap(layer * 2 + 1), pe.snap(layer * 2 + 2)
                nv = [pe.snap(layer * 3 + (u + 2)) for u in range(3)]
                par = pe.snap(layer * 272 + 272)
                landed = [pe.snap(layer * (16 * LAYER_TURNS) + 16 * (t + 1)) for t in range(LAYER_TURNS)]

                def w_in(u):
                    lo, hi = IN_UNITS[u]
                    return v3(ring[:, u, :], 0, KT * (hi - lo), KT)

                pe.wait_ge(S["loaded_par"], par)
                pe.wait_ge(S["wsm_done"], L1)
                for g in range(4):
                    i = pe.transpose(ps[6][:, P * g:P * g + P], wsr[:, g, :], ident)
                i.then_inc(S["ws_ps"], 1)
                pe.transpose(ps[7][:, 0:N_ROWS], prow[:, :], ident[0:N_ROWS, 0:N_ROWS]).then_inc(S["pcol_ps"], 1)
                transposes(nv[0])

                pe.wait_ge(S["pcol_done"], L1)
                pe.wait_ge(arrived[U_QI], landed[0])
                w = w_in(U_QI)
                for m in range(2):
                    i = on_features(ps[4][:, 256 * m:256 * m + 256], w[:, :, P * m:P * m + P])
                i.then_inc(g_ps["qi"], 1)
                on_features(ps[5][0:32, 0:256], w[:, :, 256:288])
                for t in range(TT):
                    i = on_tokens(ps[5][:, 256 + 8 * t:264 + 8 * t], w[:, :, 288:296], t)
                i.then_inc(g_ps["ki"], 1)

                def dots(t, n):
                    for hh in range(IDX_HEADS):
                        r0 = 32 * (hh % 4)
                        c0 = 256 * (hh // 4)
                        i = mm(ps[hh % 4][:, c0:c0 + n], qiT[r0:r0 + 32, hh // 4, P * t:P * t + P],
                               kiT[r0:r0 + 32, 0:n], start=True, stop=True, tile_position=(r0, 0))
                    return i
                pe.wait_ge(g_ev["qi"], L1)
                pe.wait_ge(g_ev["ki"], L1)
                dots(1, 256).then_inc(S["dots_ps"], 1)

                pe.wait_ge(arrived[U_A], landed[0])
                pe.wait_ge(S["ws_done"], L1)
                w = w_in(U_A)
                for m in range(2):
                    i = on_features(ps[6][:, 256 * m:256 * m + 256], w[:, :, P * m:P * m + P])
                i.then_inc(g_ps["a"], 1)
                for t in range(TT):
                    i = on_tokens(ps[7][:, 256 * t:256 * t + 256], w[:, :, 256:512], t)
                i.then_inc(g_ps["av"], 1)
                pe.wait_ge(S["rel"], first)
                dots(0, P).then_inc(S["dots_ps"], 1)
                pe.wait_ge(arrived[U_AG], landed[0])
                w = w_in(U_AG)
                on_features(ps[4][0:GLA_RANK, 0:256], w[:, :, 256:272]).then_inc(g_ps["lr"], 1)
                for t in range(TT):
                    i = on_tokens(ps[5][:, 256 * t:256 * t + 256], w[:, :, 0:256], t)
                i.then_inc(g_ps["ag"], 1)
                pe.wait_ge(g_ev["a"], L1)
                pe.wait_ge(g_ev["lr"], L1)
                mm(ps[6][:, 0:256], wa2[:, :], lrT, start=True, stop=True).then_inc(g_ps["logit"], 1)

                pe.wait_ge(arrived[U_CQ], landed[0])
                pe.wait_ge(g_ev["av"], L1)
                w = w_in(U_CQ)
                for m in range(2):
                    i = on_features(ps[7][:, 256 * m:256 * m + 256], w[:, :, P * m:P * m + P])
                i.then_inc(g_ps["q"], 1)
                for m in range(2):
                    i = on_features(ps[4][:, 256 * m:256 * m + 256], w[:, :, 256 + P * m:384 + P * m])
                i.then_inc(g_ps["k"], 1)
                pe.wait_ge(arrived[U_CV], landed[0])
                pe.wait_ge(g_ev["ag"], L1)
                for t in range(TT):
                    i = on_tokens(ps[5][:, 256 * t:256 * t + 256], w_in(U_CV), t)
                i.then_inc(g_ps["cv"], 1)

                pe.wait_ge(S["qbd_done"], L1)
                pe.wait_ge(S["kd_ready"], L1)
                pe.wait_ge(S["rel"], second)
                for t in range(TT):
                    i = mm(ps[t][:, :], akT[:, P * t:P * t + P], qbd[:, t, :, :], start=True, stop=True)
                i.then_inc(S["att_ps"], 1)
                for t in range(TT):
                    i = pe.transpose(ps[2][:, P * t:P * t + P], kdT[:, P * t:P * t + P], ident)
                i.then_inc(S["kd_ps"], 1)

                pe.wait_ge(arrived[U_BU], landed[0])
                pe.wait_ge(S["la_ready"], L1)
                w = w_in(U_BU)
                for m in range(2):
                    i = on_features(ps[6][:, 256 * m:256 * m + 256], w[:, :, P * m:P * m + P])
                i.then_inc(g_ps["bu"], 1)
                pe.wait_ge(arrived[U_UV], landed[0])
                pe.wait_ge(g_ev["q"], L1)
                on_tokens(ps[7][:, :], w_in(U_UV), 0).then_inc(g_ps["uv0"], 1)
                pe.wait_ge(g_ev["k"], L1)
                on_tokens(ps[4][:, :], w_in(U_UV), 1).then_inc(g_ps["uv1"], 1)

                pe.wait_ge(S["kdr_done"], L1)
                mm(ps[3][:, 0:256], kdr[0:64, 0, :], av[0:64, 0, :], start=True, stop=True)
                mm(ps[3][:, 256:512], kdr[0:64, 1, :], av[0:64, 1, :], start=True, stop=True)
                mm(ps[2][:, 256:512], kdr[64:128, 0, :], av[64:128, 0, :], start=True, stop=True)\
                    .then_inc(S["kv_ps"], 1)

                pe.wait_ge(arrived[U_WKV], landed[1])
                pe.wait_ge(g_ev["cv"], L1)
                pe.wait_ge(g_ev["bu"], L1)
                pe.wait_ge(S["wkv_scaled"], L1)
                w = v3(ring[:, U_WKV, :], 0, 4096, KT)
                for m in range(2):
                    i = on_features(ps[5][:, 256 * m:256 * m + 256], w[:, :, P * m:P * m + P], memT)
                i.then_inc(g_ps["kx"], 1)
                for t in range(2):
                    i = on_tokens(ps[6][:, 256 * t:256 * t + 256], w[:, :, 256:512], t, memT)
                i.then_inc(g_ps["vx"], 1)

                pe.wait_ge(S["att_done"], L1)
                pe.wait_ge(S["zeroed"], 1)
                pe.wait_ge(S["s_ready"], L1)
                for t in range(TT):
                    for half in range(2):
                        n = 2 * t + half
                        state = zeros[:, :] if n == 0 else Sst[:, n - 1, :]
                        mm(ps[t][64 * half:64 * half + 64, 0:256], aqT[:, CHUNK * n:CHUNK * n + CHUNK], state,
                           start=True, stop=False, skip_group_check=True)
                    for hh in range(HEADS):
                        i = mm(ps[t][:, 64 * hh:64 * hh + 64], attT[:, t, P * hh:P * hh + P],
                               av[:, t, 64 * hh:64 * hh + 64], start=False, stop=True, skip_group_check=True)
                i.then_inc(S["o_ps"], 1)

                pe.wait_ge(S["vn_done"], L1)
                for t in range(TT):
                    for g in range(4):
                        i = mm(ps[2 + t][:, 64 * g:64 * g + 64], wsT[:, g, :], vn[:, t, 64 * g:64 * g + 64],
                               start=True, stop=True)
                i.then_inc(S["sg_ps"], 1)

                pe.wait_ge(S["pool_out"], L1)
                pe.wait_ge(g_ev["uv0"], L1)
                for m in range(2):
                    i = mm(ps[7][:, 256 * m:256 * m + 256], pwbd[:, m, :], bu[:, m, PAD:PAD + SEQ], start=True, stop=True)
                i.then_inc(g_ps["y"], 1)

                def attend(t, n, keys, banks, name):
                    for hh in range(HEADS):
                        r0 = 64 * (hh % 2)
                        c0 = n * (hh // 2)
                        i = mm(ps[banks + hh % 2][:, c0:c0 + n], qT[r0:r0 + 64, hh // 2, P * t:P * t + P],
                               keys[r0:r0 + 64, hh // 2, 0:n], start=True, stop=True)
                    i.then_inc(S[name], 1)

                def values(dst, pT, vals, t, tiles):
                    for hh in range(HEADS):
                        for k in range(tiles):
                            i = mm(dst[:, 64 * hh:64 * hh + 64], pT[:, tiles * hh + k, :],
                                   vals[:, k, 64 * hh:64 * hh + 64], start=k == 0, stop=k == tiles - 1)
                    return i

                pe.wait_ge(g_ev["uv1"], L1)
                pe.wait_ge(g_ev["kx"], L1)
                attend(1, 256, kT, 4, "lg_ps")
                pe.wait_ge(g_ev["vx"], L1)
                pe.wait_ge(g_ev["y"], L1)
                attend(0, P, kT, 6, "lg_ps")
                pe.wait_ge(S["og_done"], L1)
                pe.wait_ge(S["p"], first)
                for hh in range(HEADS):
                    for k in range(2):
                        x = 2 * hh + k
                        i = pe.transpose(ps[x // 4][:, P * (x % 4):P * (x % 4) + P],
                                         prb[1][:, hh, P * k:P * k + P], ident)
                i.then_inc(S["pt1_ps"], 1)
                pe.wait_ge(S["od_done"], L1)
                pe.wait_ge(S["p"], second)
                for hh in range(HEADS):
                    i = pe.transpose(ps[2][:, P * hh:P * hh + P], prb[0][:, hh, :], ident)
                i.then_inc(S["pt0_ps"], 1)

                def transpose_rows(bank, src):
                    for k in range(2):
                        for t in range(TT):
                            c0 = 256 * k + P * t
                            i = pe.transpose(ps[bank][:, c0:c0 + P], src[:, t, P * k:P * k + P], ident)
                    return i
                pe.wait_ge(S["lg"], second)
                transpose_rows(4, sg)
                transpose_rows(6, uvg)
                pe.wait_ge(S["pt1_v"], L1)
                pe.wait_ge(S["pt1_a"], L1)
                values(ps[3][:, 256:512], pT_mix[1], cv, 1, 2)
                pe.wait_ge(S["pt0_v"], L1)
                values(ps[3][:, 0:256], pT_mix[0], cv, 0, 1).then_inc(S["pv_ps"], 1)
                pe.wait_ge(S["oc_done"], L1)
                transpose_rows(5, oc).then_inc(S["mt_ps"], 1)

                pe.wait_ge(S["mt_v"], L1)
                pe.wait_ge(S["mt_a"], L1)
                for i4, m in enumerate(WOUT_ORDER):
                    s = U_WOUT + i4
                    pe.wait_ge(arrived[s], landed[1])
                    w = v3(ring[:, s, :], 0, 2048, 2)
                    for k in range(2):
                        for t in range(TT):
                            for half in range(2):
                                i = mm(ps[2 * t + half][:, :], mixT[:, 2 * m + k, P * t:P * t + P],
                                       w[:, k, 512 * half:512 * half + 512],
                                       start=i4 == 0 and k == 0, stop=i4 == 3 and k == 1)
                    i.then_inc(slot_free[s], 1)

                transposes(nv[1])
                pe.wait_ge(arrived[U_WQ], landed[1])
                w = v3(ring[:, U_WQ, :], 0, 2048, KT)
                for m in range(2):
                    i = on_features(ps[4][:, 256 * m:256 * m + 256], w[:, :, P * m:P * m + P])
                i.then_inc(g_ps["xq"], 1)
                pe.wait_ge(g_ev["xq"], L1)
                for t in range(TT):
                    attend(t, MEM, kxT, 2 * t, "xlg_ps")
                for t in range(TT):
                    pe.wait_ge(S["xp"], second if t else first)
                    for x in range(8):
                        i = pe.transpose(ps[4 + 2 * t + x // 4][:, P * (x % 4):P * (x % 4) + P],
                                         prx[t][:, x // 2, P * (x % 2):P * (x % 2) + P], ident)
                    i.then_inc(S["xpt_ps"], 1)
                for t in range(TT):
                    pe.wait_ge(S["xpt_v"], second if t else first)
                    pe.wait_ge(S["xpt_a"], second if t else first)
                    i = values(ps[2 * t][:, 0:256], pT_x[t], vx, t, 2)
                i.then_inc(S["xpv_ps"], 1)
                pe.wait_ge(S["ox_done"], L1)
                transpose_rows(1, oc).then_inc(S["xo_ps"], 1)
                pe.wait_ge(S["xo_done"], L1)
                pe.wait_ge(arrived[U_WO], landed[1])
                w = v3(ring[:, U_WO, :], 0, 2048, 2)
                for t in range(TT):
                    for half in range(2):
                        for k in range(2):
                            i = mm(ps[4 + 2 * t + half][:, :], oxT[:, k, P * t:P * t + P],
                                   w[:, k, 512 * half:512 * half + 512], start=k == 0, stop=k == 1)
                i.then_inc(g_ps["xout"], 1)

                transposes(nv[2])
                with pe.If(layer < 1):
                    def down(f, slot, k, frees):
                        pe.wait_ge(S["f_a"], f + 1)
                        w2 = ring[:, slot, k * D:k * D + D]
                        for q in range(4):
                            i = mm(ps[4 + q][:, :], f_act[:, f % 2, P * (q // 2):P * (q // 2) + P],
                                   w2[:, 512 * (q % 2):512 * (q % 2) + 512], start=f == 0, stop=f == FF // P - 1)
                            if q < len(frees):
                                i.then_inc(slot_free[frees[q]], 1)
                        return i

                    f = 0
                    before = None
                    for c, n in enumerate(FFN_TILES):
                        u1, u3, u2 = 3 * c, 3 * c + 1, 3 * c + 2
                        for k in range(n):
                            for w, u in enumerate((u1, u3)):
                                if k == 0:
                                    pe.wait_ge(arrived[u % RING], landed[2 + u // RING])
                                wt = v3(ring[:, u % RING, :], 0, KT * n * P, KT)
                                i = on_features(ps[f % 2][:, 256 * w:256 * w + 256], wt[:, :, P * k:P * k + P])
                            i.then_inc(S["f_h"], 1)
                            frees = (u1 % RING, u3 % RING) if k == n - 1 else ()
                            if before is not None:
                                bf, bslot, bk, blast = before
                                i = down(bf, bslot, bk, frees)
                                if blast:
                                    i.then_inc(slot_free[bslot], 1)
                            if k == 0:
                                pe.wait_ge(arrived[u2 % RING], landed[2 + u2 // RING])
                            before = (f, u2 % RING, k, k == n - 1)
                            f += 1
                    down(before[0], before[1], before[2], ()).then_inc(slot_free[before[1]], 1)

            for t in range(TT):
                i = on_tokens(ps[4][:, 8 * t:8 * t + 8], routw, t)
            i.then_inc(S["rlog_ps"], 1)
            pe.wait_ge(S["sel_ready"], 1)
            sel = score[:, :, :].rearrange("p a b -> p (a b)")[:, 80:96]
            before_, ones = cc("before"), cc("ones")
            mm(ps[5][:, 0:8], before_, sel[:, 0:8], start=True, stop=True)
            mm(ps[5][:, 8:16], before_, sel[:, 8:16], start=True, stop=False)
            mm(ps[5][:, 8:16], ones, sel[:, 0:8], start=False, stop=True)
            mm(ps[5][:, 16:24], ones, sel[:, 0:8], start=True, stop=False)
            mm(ps[5][:, 16:24], ones, sel[:, 8:16], start=False, stop=True).then_inc(S["rank_ps"], 1)
            pe.wait_ge(S["jobs_ready"], 1)
            n_jobs = pe.value_load(tabi[0:1, 0:1], min_val=N_EXP, max_val=MAX_JOBS)

            def gather(n):
                pe.wait_ge(S["j_g"], n)
                for kt in range(KT):
                    for t in range(TT):
                        i = mm(ps[2 + kt // 4][:, P * (kt % 4):P * (kt % 4) + P], xr[:, t, P * kt:P * kt + P],
                               hot[:, t, :], start=t == 0, stop=t == TT - 1)
                i.then_inc(S["j_gps"], 1)

            gather(1)
            for half in range(2):
                for q in range(2):
                    i = mm(ps[6 + half][:, 256 * q:256 * q + 256], zeros[:, 0:P], zeros[:, :], start=True, stop=True)
            i.then_inc(S["j_yps"], 1)

            def combine(n):
                pe.wait_ge(S["j_gt"], n)
                for half, ready in ((0, "j_yv"), (1, "j_ya")):
                    pe.wait_ge(S[ready], n)
                    for t in range(TT):
                        i = mm(ps[4 + 2 * t + half][:, :], hotgT[:, t, :], yrow[:, 512 * half:512 * half + 512],
                               start=True, stop=True)
                i.then_inc(S["j_c1"], 1)

            for _ in range(NB - 1):
                pe.sem_inc(S["piece_free"], 1)
            with pe.Fori(0, n_jobs) as j:
                cn = [pe.snap(j * NCH + (c + 1)) for c in range(NCH)]
                j1, j2, pieces = pe.snap(j + 1), pe.snap(j + 2), pe.snap(j * JOB_PIECES)

                def products(w, c):
                    u = UNIT_OF[w, c]
                    for q in range(QP):
                        i = QP * u + q
                        pe.wait_ge(S["lo_ready"], pieces + (i + 1))
                        hi, lo = w_hi[:, i % NB, :], w_lo[:, i % NB, :]
                        steps = []
                        for part in range(2):
                            if w == 2:
                                dst, xh, xl = ps[6 + part], at_hi[:, q, :], at_lo[:, q, :]
                                opens, closes = c == 0 and q == 0, c == NCH - 1 and q == QP - 1
                            else:
                                k = 2 * q + part
                                dst, xh, xl = ps[2 * (c % 2) + (w == 3)], xg_hi[:, k, :], xg_lo[:, k, :]
                                opens, closes = k == 0, k == KT - 1
                            wh, wl = hi[:, FC * part:FC * part + FC], lo[:, FC * part:FC * part + FC]
                            steps += [(dst, xh, wh, opens, False), (dst, xl, wh, False, False), (dst, xh, wl, False, closes)]
                        for n, (dst, x, y, opens, closes) in enumerate(steps):
                            ins = mm(dst[:, :], x, y, start=opens, stop=closes)
                            if n == 0:
                                ins.then_inc(S["piece_free"], 1)
                            elif n == 1 and q == QP - 1:
                                ins.then_inc(slot_free[u % RING], 1)
                    return ins

                def transpose_act(c):
                    pe.wait_ge(S["j_a"], cn[c])
                    for f in range(4):
                        i = pe.transpose(ps[4][:, P * f:P * f + P], j_act[:, P * f:P * f + P], ident)
                    i.then_inc(S["j_tps"], 1)

                pe.wait_ge(S["j_gl"], j1)
                products(1, 0).then_inc(S["j_h1"], 1)
                products(3, 0).then_inc(S["j_h3"], 1)
                combine(j1)
                for c in range(1, NCH):
                    products(1, c).then_inc(S["j_h1"], 1)
                    if c == 1:
                        pe.wait_ge(S["j_cv"], j1)
                    transpose_act(c - 1)
                    products(3, c).then_inc(S["j_h3"], 1)
                    pe.wait_ge(S["j_t"], cn[c - 1])
                    products(2, c - 1)
                transpose_act(NCH - 1)
                for t in range(TT):
                    i = pe.transpose(ps[5][:, P * t:P * t + P], hotg[:, t, :], ident)
                i.then_inc(S["j_gtps"], 1)
                gather(j2)
                pe.wait_ge(S["j_t"], cn[NCH - 1])
                products(2, NCH - 1).then_inc(S["j_yps"], 1)
            combine(n_jobs + 1)


INPUTS = ("x", "mem", "rel_bias", "final_norm", "norm_mix", "w_in", "gla_wa2", "gla_ba", "gla_norm", "pool_w", "pool_b",
          "pool_scale", "sgu_ln_g", "sgu_ln_b", "sgu_w", "sgu_b", "w_out", "norm_xa", "norm_mem", "xa_wq", "xa_wkv",
          "xa_wo", "norm_ffn", "ffn_w1", "ffn_w3", "ffn_w2", "router", "moe_w1", "moe_w3", "moe_w2")


def kernel(**inputs):
    import numpy as _np
    import concourse.bacc as _bacc
    from concourse import mybir as _mybir
    from concourse.bass_utils import run_bass_kernel_spmd as _run

    nc = _bacc.Bacc("TRN2", target_bir_lowering=False, num_devices=1)
    arrays = {name: _np.ascontiguousarray(inputs[name]) for name in INPUTS}
    for name, value in zip(("consts", "glam", "onehot", "flip"), shape_constants()):
        arrays[name] = value
    aps = {name: nc.dram_tensor(f"in_{name}", a.shape, _mybir.dt.from_np(a.dtype), kind="ExternalInput").ap()
           for name, a in arrays.items()}
    out = nc.dram_tensor("out", arrays["x"].shape, _mybir.dt.from_np(arrays["x"].dtype), kind="ExternalOutput").ap()
    build(nc, aps, out)
    r = _run(nc, [{f"in_{name}": a for name, a in arrays.items()}], core_ids=[0])
    return r.results[0]["out"]
```

```python
import math
from contextlib import ExitStack

import numpy as np

import concourse.bass as bass
from concourse import mybir

P = 128
F32 = mybir.dt.float32
F32R = mybir.dt.float32r
I32 = mybir.dt.int32
U8 = mybir.dt.uint8
ALU = mybir.AluOpType
ACT = mybir.ActivationFunctionType
AX = mybir.AxisListType.X

SEQ, D, DEPTH, MEM = 256, 1024, 2, 256
TT = SEQ // P
KT = D // P
GW = 256
EPS = 1e-6
HEADS = 4
GLA_DK, GLA_DV, GLA_RANK, CHUNK = 32, 64, 16, 64
IDX_HEADS, IDX_DIM, TOPK = 8, 32, 64
DH = 64
WINDOWS = (2, 4, 8, 16)
PAD = 16
N_EXP, FE, FF = 8, 3584, 2816
BUCKETS, MAX_DIST = 32, 128
IN_W = 2616
RING = 7
LAYER_TURNS = 5
JOB_TURNS = 3
FC = 512
NCH = FE // FC
MAX_JOBS = N_EXP + 3
PIECE, NB = 1024, 4
QP = 4096 // PIECE
JOB_UNITS = [(1, 0), (3, 0)] + [x for c in range(1, NCH) for x in ((1, c), (3, c), (2, c - 1))] + [(2, NCH - 1)]
UNIT_OF = {x: u for u, x in enumerate(JOB_UNITS)}
JOB_PIECES = QP * len(JOB_UNITS)
FFN_TILES = (4, 3, 3, 3, 3, 3, 3)
FFN_PIECES = [x for f in range(FF // P) for x in ((1, f), (3, f), (2, f - 1)) if x[1] >= 0] + [(2, FF // P - 1)]
FFN_EARLY = 2
FFN_WHERE = [(c, k, n) for c, n in enumerate(FFN_TILES) for k in range(n)]


def after(unit):
    return QP * UNIT_OF[unit] + QP - 1 + NB


NEG, MARK, HALF = -3.0e38, -3.4e38, -3.2e38

C_AQ, C_AV, C_AG, C_LR, C_BU = 0, 256, 512, 768, 784
C_CQ, C_CK, C_CV, C_QI, C_KI, C_WI, C_UV = 1040, 1296, 1552, 1808, 2064, 2096, 2104
IN_UNITS = ((C_QI, C_UV), (0, 512), (C_AG, C_BU), (C_CQ, C_CV), (C_CV, C_QI), (C_BU, C_CQ), (C_UV, IN_W))
U_QI, U_A, U_AG, U_CQ, U_CV, U_BU, U_UV = range(7)
U_WKV, U_WOUT, U_WQ, U_WO = 0, 1, 5, 6
WOUT_ORDER = (1, 0, 3, 2)

R_MIX, R_XA, R_MEM, R_FFN, R_BA, R_PB, R_PS, R_SB, N_ROWS = 0, 8, 16, 24, 32, 33, 35, 37, 41

CONST = {}
_at = 0
for _name, _w in (("ident", P), ("vis", 256), ("reset", 256), ("bd", 256), ("tril", P), ("inv", 512),
                  ("before", P), ("ones", P), ("iota", P), ("eidx", 8), ("erev", 8)):
    CONST[_name] = (_at, _at + _w)
    _at += _w
CONST_W = _at


def shape_constants():
    c = np.zeros((P, CONST_W), np.float32)
    r = np.arange(P)
    s = np.arange(256)

    def put(name, v):
        c[:, CONST[name][0]:CONST[name][1]] = v

    put("ident", np.eye(P))
    put("vis", np.where(s[None, :] <= P + r[:, None], 0.0, NEG))
    put("reset", np.where(s % CHUNK == 0, 0.0, 1.0)[None, :])
    put("bd", (r[:, None] // GLA_DK == s[None, :] // GLA_DV))
    put("tril", r[None, :] <= r[:, None])
    inv = np.zeros((P, 2, 256), np.float32)
    for g, w in enumerate(WINDOWS):
        inv[64 * (g % 2):64 * (g % 2) + 64, g // 2, :] = 1.0 / np.minimum(s + 1, w).astype(np.float32)
    put("inv", inv.reshape(P, 512))
    put("before", r[:, None] < r[None, :])
    put("ones", 1.0)
    put("iota", r[None, :])
    put("eidx", np.arange(8)[None, :])
    put("erev", 8 - np.arange(8)[None, :])
    gla = ((r[:, None] <= r[None, :]) & (r[:, None] // CHUNK == r[None, :] // CHUNK)).astype(np.int32)
    gla = np.ascontiguousarray(np.tile(gla[:, None, :], (1, HEADS, 1)).reshape(P, HEADS * P)).astype(np.float32)
    n = np.maximum(255 - np.arange(384), 0)
    exact = BUCKETS // 2
    nf = np.maximum(n, 1).astype(np.float32)
    large = exact + (np.log(nf / np.float32(exact)) / np.float32(math.log(MAX_DIST / exact))
                     * np.float32(BUCKETS - exact)).astype(np.int32)
    bucket = np.where(n < exact, n, np.minimum(large, BUCKETS - 1))
    onehot = (np.arange(BUCKETS)[:, None] == bucket[None, :]).astype(np.float32)
    flip = np.ascontiguousarray(np.eye(P, dtype=np.float32)[::-1])
    return c, gla, onehot, flip


def build(nc, A, out):
    ctx = ExitStack()
    with ctx:
        def sb(name, shape, dt=F32):
            return ctx.enter_context(nc.sbuf_tensor(name, shape, dt))

        def sem(name):
            return ctx.enter_context(nc.semaphore(name))

        ring = sb("ring", [P, RING, 4096])
        cst = sb("cst", [P, CONST_W])
        gmask = sb("gmask", [P, HEADS * P], U8)
        h = sb("h", [P, TT, D])
        base = nc.sbuf_base
        xnT = sb("xnT", [P, KT, SEQ])
        mixT = xnT
        qidx = sb("qidx", [P, 1024])
        qT = sb("qT", [P, 2, SEQ])
        kT = sb("kT", [P, 2, SEQ])
        cv = sb("cv", [P, TT, GW])
        av = sb("av", [P, TT, GW])
        sg = sb("sg", [P, TT, GW])
        gla = sb("gla", [P, 1024])
        glab = sb("glab", [P, 512])
        kdec = sb("kdec", [P, 512])
        Sst = sb("Sst", [P, 3, GW])
        kxT = sb("kxT", [P, 2, MEM])
        vx = sb("vx", [P, 2, GW])
        bu = sb("bu", [P, 2, PAD + SEQ])
        pw1 = sb("pw1", [P, 2, PAD + SEQ])
        pw2 = sb("pw2", [P, 2, PAD + SEQ])
        to_mem = nc.sbuf_base - base
        memT = sb("memT", [P, KT, MEM])
        stretch = nc.sbuf_base - base

        def over(name, shape):
            n = 4 * int(np.prod(shape[1:]))
            assert over.at + n <= over.end
            t = nc.alloc_sbuf_tensor_at(name, shape, F32R, offset=base + over.at, align_bytes=32)
            over.at += n
            return t
        over.at, over.end = 0, stretch
        w_hi, w_lo = over("w_hi", [P, NB, PIECE]), over("w_lo", [P, NB, PIECE])
        xg_hi, xg_lo = over("xg_hi", [P, KT, P]), over("xg_lo", [P, KT, P])
        at_hi, at_lo = over("at_hi", [P, 4, P]), over("at_lo", [P, 4, P])
        y_lo1, hotT = over("y_lo1", [P, FC]), over("hotT", [P, TT, P])
        assert over.at <= stretch - 4096
        over.at, over.end = 8 * NB * PIECE, to_mem
        x_lo, fa_hi = over("x_lo", [P, KT, SEQ]), over("fa_hi", [P, 2, SEQ])

        uvg_at = nc.sbuf_base
        uvg = sb("uvg", [P, TT, 512])
        bias = sb("bias", [P, HEADS, 256])
        r2_at = nc.sbuf_base
        r2 = sb("r2", [P, 2048])
        bc = sb("bc", [P, 3, GW])
        wsT = sb("wsT", [P, 4, P])
        pwbd = sb("pwbd", [P, 2, P])
        wa2 = sb("wa2", [GLA_RANK, P])
        prow = sb("prow", [N_ROWS, P])
        pcol = sb("pcol", [P, N_ROWS])
        routw = sb("routw", [P, KT, N_EXP])
        wis = sb("wis", [P, TT, IDX_HEADS])
        score_at = nc.sbuf_base
        score = sb("score", [P, 2, 256])
        m8 = sb("m8", [P, 8])
        tick = sb("tick", [P, 2])
        eps = sb("eps", [P, 1])
        diag = sb("diag", [P, TT, P])
        zeros = sb("zeros", [P, GW])
        st = sb("st", [P, 96])
        tabi = sb("tabi", [1, 16], I32)
        jobt = sb("jobt", [P, TT, 2, MAX_JOBS + 1])

        x_hi = nc.alloc_sbuf_tensor_at("x_hi", [P, KT, SEQ], F32R, offset=r2_at, align_bytes=32)
        y_hi = nc.alloc_sbuf_tensor_at("y_hi", [P, 2, FC], F32R, offset=uvg_at, align_bytes=32)
        y_lo0 = nc.alloc_sbuf_tensor_at("y_lo0", [P, FC], F32R, offset=score_at, align_bytes=32)
        y_lo = [y_lo0, y_lo1]
        fa_lo = nc.alloc_sbuf_tensor_at("fa_lo", [P, 2, SEQ], F32R, offset=score_at, align_bytes=32)

        def cc(name, a=0, b=None):
            lo, hi = CONST[name]
            return cst[:, lo + a:hi if b is None else lo + b]

        ident = cc("ident")
        ps = [ctx.enter_context(nc.psum_tensor(f"bank{i}", [P, 512], F32)) for i in range(8)]

        def v3(t, a, b, x):
            return t[:, a:b].rearrange("p (x y) -> p x y", x=x)

        def xT(kt, bank0=0):
            return ps[bank0 + kt // 2][:, 256 * (kt % 2):256 * (kt % 2) + 256]

        def norm_no(layer, u):
            return (4, 1) if u == 0 else (3, 2 + u)

        def count(layer, no, each, off):
            if isinstance(no, int):
                return each * (no - 1) + off
            return layer * (each * no[0]) + (each * (no[1] - 1) + off)
        memr = memT[:, :, :].rearrange("p k m -> p (k m)").rearrange("p (t d) -> p t d", t=2)

        xr = v3(r2, 0, 2048, 2)
        rel = v3(r2, 0, 2048, 8)
        qbd = r2[:, 0:1024].rearrange("p (t h i) -> p t h i", t=2, h=4)
        attT = r2[:, 1024:2048].rearrange("p (t n) -> p t n", t=2)
        qiT = v3(qidx, 0, 512, 2)
        kiT = qidx[:, 512:768]
        lrT = qidx[0:GLA_RANK, 768:1024]
        aqT, akT, eb, enb = (gla[:, 256 * i:256 * i + 256] for i in range(4))
        la, bs = glab[:, 0:256], glab[:, 256:512]
        kdT, kdr = kdec[:, 0:256], v3(kdec, 256, 512, 2)
        lgm = [v3(r2, 1024, 1536, 4), v3(gla, 0, 1024, 4)]
        prb = [v3(r2, 1536, 2048, 4), v3(r2, 0, 1024, 4)]
        pT_mix = [v3(glab, 0, 512, 4), v3(qidx, 0, 1024, 8)]
        prx = [v3(r2, 0, 1024, 4), v3(r2, 1024, 2048, 4)]
        pT_x = [v3(qidx, 0, 1024, 8), v3(gla, 0, 1024, 8)]
        oc = v3(Sst[:, :, :].rearrange("p a b -> p (a b)"), 0, 512, 2)
        wsr = uvg[:, 0, :].rearrange("p (g s) -> p g s", g=4)
        osq = v3(kdec, 0, 512, 2)
        vn = uvg[:, :, 256:512]
        oxT = kT
        f_sil = v3(uvg[:, 1, :], 0, 512, 2)
        xnf = xnT[:, :, :].rearrange("p k m -> p (k m)")
        j_sil = [memT[:, 4 + 2 * i:6 + 2 * i, :].rearrange("p a b -> p (a b)") for i in range(2)]
        j_act = wsT[:, :, :].rearrange("p a b -> p (a b)")
        nffn = uvg[:, :, :].rearrange("p a b -> p (a b)")
        hot, hot_now = (bc[:, i, :].rearrange("p (t s) -> p t s", t=2) for i in range(2))
        fnorm = bias[:, :, :].rearrange("p h x -> p (h x)")
        hank = [kxT, vx]

        ss, rms, rs = st[:, 0:2], st[:, 2:4], st[:, 4:6]
        s_mx, s_sum, s_rec = st[:, 8:16], st[:, 16:24], st[:, 24:32]
        s_bn, s_ag, s_vm, s_vr = st[:, 32:44], st[:, 44:48], st[:, 48:50], st[:, 50:52]
        s_og, s_or = st[:, 52:60], st[:, 60:68]
        s_d, s_e, s_g = st[:, 68:70], st[:, 70:72], st[:, 72:76]
        j_gate = st[:, 76:78]

        names = """loaded_h loaded_mem loaded_cst loaded_const loaded_prow loaded_par loaded_fnorm bias_row bias_rows
            bias_hank stored v_chain a_chain
            g_chain bias_ps hank_ps bias_done h_upd rms_ready diag_ready rows0_ps xT_ps xT_v xT_a
            par_free zeroed wkv_scaled pcol_ps pcol_done wsm_done ws_ps ws_done la_ready ls_ready b_ready
            eb_ready qe_ready r2_zero qbd_done kd_ready att_ps att_done kd_ps kdr_done kv_ps s_ready o_ps osq
            ms_gla r_gla og_done pool_out vms vr vn_done sg_ps od_done pt1_ps pt0_ps pt1_v pt1_a pt0_v pv_ps
            oc_done mt_ps mt_v mt_a xpv_ps ox_done xo_ps xo_done f_y f_x f_xh f_h f_s f_a  rlog_ps top_diff top_exp
            sel_ready rank_ps jobs_ready j_h1 j_h3 j_s j_a j_tps j_th j_t j_yps j_yv j_ya j_g j_gps j_gtps j_gh j_gl
            j_gt j_c1 j_cv loaded_nffn hi_ready lo_ready piece_free fin scored dots_ps rel lg p xmx xp xpt_ps xpt_a lg_ps xlg_ps xpt_v""".split()
        S = {n: sem(n) for n in names}
        arrived = [sem(f"arrived{i}") for i in range(RING)]
        slot_free = [sem(f"slot_free{i}") for i in range(RING)]
        GROUPS = ("qi", "ki", "a", "av", "lr", "ag", "logit", "q", "k", "cv", "bu", "uv0", "uv1", "kx", "vx", "y", "xq", "wout", "xout")
        ENDS = {"ki": (U_QI, 0), "av": (U_A, 0), "ag": (U_AG, 0), "k": (U_CQ, 0), "cv": (U_CV, 0), "bu": (U_BU, 0),
                "uv1": (U_UV, 0), "vx": (U_WKV, 1), "xq": (U_WQ, 1), "wout": (U_WOUT + 3, 1), "xout": (U_WO, 1)}
        g_ps = {n: slot_free[ENDS[n][0]] if n in ENDS else sem(f"ps_{n}") for n in GROUPS}
        g_ev = {n: sem(f"ev_{n}") for n in GROUPS if n not in ("logit", "wout", "xout")}

        consts, glam, onehot, flip = A["consts"], A["glam"], A["onehot"], A["flip"]
        rev = nc.dram_tensor("bias_scratch", (HEADS, 384), F32, kind="Internal")
        block = ctx.enter_context(nc.Block())

        def chain(eng, s):
            n = [0]

            def link(ins):
                n[0] += 1
                ins.then_inc(s, 1)
                eng.wait_ge(s, n[0])

            def restart():
                n[0] = 0
                eng.sem_clear(s)
            return link, restart

        def rows(ap, n):
            return ap.rearrange("(r c) -> r c", c=P)

        def ffn_piece(i):
            w, f = FFN_PIECES[i]
            c, k, n = FFN_WHERE[f]
            u = 3 * c + (0, 2, 1)[w - 1]
            slot = ring[:, u % RING, :]
            weights = slot[:, k * D:k * D + D] if w == 2 else v3(slot, 0, KT * n * P, KT)[:, :, P * k:P * k + P]
            return u, k == 0, k == n - 1, weights

        def ffn_buf(bufs, i):
            return bufs[:, (i + NB - FFN_EARLY) % NB, :]

        def as_piece(w, buf):
            return buf if w == 2 else v3(buf, 0, PIECE, KT)

        @block.sync
        def _(sp):
            sp.dma_start(h[:, 0, :], A["x"][0, 0:P, :]).then_inc(S["loaded_h"], 16)
            sp.dma_start(h[:, 1, :], A["x"][0, P:SEQ, :]).then_inc(S["loaded_h"], 16)
            sp.dma_start(cst[:, :], consts).then_inc(S["loaded_cst"], 16)

            with sp.Fori(0, DEPTH) as layer:
                lay = bass.ds(layer, 1)
                L1 = sp.snap(layer + 1)
                turn = [sp.snap(layer * LAYER_TURNS + (t + 1)) for t in range(LAYER_TURNS)]
                sp.wait_ge(S["par_free"], 1)
                sp.wait_ge(S["par_free"], L1)
                for name, row, n in (("norm_mix", R_MIX, 8), ("norm_xa", R_XA, 8), ("norm_mem", R_MEM, 8),
                                     ("norm_ffn", R_FFN, 8), ("gla_ba", R_BA, 1), ("pool_scale", R_PS, 2)):
                    sp.dma_start(prow[row:row + n, :], A[name][lay].rearrange("e (r c) -> (e r) c", c=P))\
                      .then_inc(S["loaded_prow"], 16)
                sp.dma_start(prow[R_PB:R_PB + 2, :], A["pool_b"][lay].rearrange("e (r a) c -> (e r) (a c)", a=2))\
                  .then_inc(S["loaded_prow"], 16)
                sp.dma_start(prow[R_SB:R_SB + 4, :], A["sgu_b"][lay].rearrange("e g t -> (e g) t"))\
                  .then_inc(S["loaded_prow"], 16)
                def unit(t, s, dst, src):
                    sp.wait_ge(slot_free[s], 1)
                    sp.wait_ge(slot_free[s], turn[t])
                    sp.dma_start(dst, src).then_inc(arrived[s], 16)

                for s, (lo, hi) in enumerate(IN_UNITS):
                    unit(0, s, ring[:, s, 0:KT * (hi - lo)].rearrange("p (k c) -> p k c", k=KT),
                         A["w_in"][lay, :, lo:hi].rearrange("e (k p) c -> p (e k) c", p=P))
                    if s == 0:
                        for i, name in enumerate(("gla_norm", "sgu_ln_g", "sgu_ln_b")):
                            sp.dma_start(bc[:, i, :], A[name][lay].broadcast_to([P, GW])).then_inc(S["loaded_par"], 16)
                        sp.dma_start(wa2[:, :], A["gla_wa2"][lay].rearrange("e r c -> (e r) c")).then_inc(S["loaded_par"], 16)
                        sp.dma_start(wsr, A["sgu_w"][lay].rearrange("e g t s -> t (e g) s")).then_inc(S["loaded_par"], 16)
                        for g in range(4):
                            r0 = 64 * (g % 2)
                            sp.dma_start(pwbd[r0:r0 + 64, g // 2, r0:r0 + 64],
                                         A["pool_w"][lay, g].rearrange("e c d -> (e c) d")).then_inc(S["loaded_par"], 16)
                        with sp.If(layer < 1):
                            sp.dma_start(gla[0:BUCKETS, 0:384], onehot).then_inc(S["loaded_const"], 16)
                            sp.dma_start(kdec[0:BUCKETS, 0:HEADS], A["rel_bias"]).then_inc(S["loaded_const"], 16)
                            sp.dma_start(glab[:, 0:P], flip).then_inc(S["loaded_const"], 16)
                            sp.dma_start(memr, A["mem"][0].rearrange("(t p) d -> p t d", p=P))\
                              .then_inc(S["loaded_mem"], 16)
                            sp.dma_start(uvg[:, 1, :], glam).then_inc(S["loaded_mem"], 16)
                            sp.dma_start(routw[:, :, :], A["router"][0].rearrange("(k p) e -> p k e", p=P))\
                              .then_inc(S["loaded_mem"], 16)
                unit(1, U_WKV, v3(ring[:, U_WKV, :], 0, 4096, KT),
                     A["xa_wkv"][lay].rearrange("e (k p) c -> p (e k) c", p=P))
                for i, m in enumerate(WOUT_ORDER):
                    unit(1, U_WOUT + i, v3(ring[:, U_WOUT + i, :], 0, 2048, 2),
                         A["w_out"][lay, 256 * m:256 * m + 256, :].rearrange("e (k p) c -> p (e k) c", p=P))
                unit(1, U_WQ, v3(ring[:, U_WQ, :], 0, 2048, KT),
                     A["xa_wq"][lay].rearrange("e (k p) c -> p (e k) c", p=P))
                unit(1, U_WO, v3(ring[:, U_WO, :], 0, 2048, 2),
                     A["xa_wo"][lay].rearrange("e (k p) c -> p (e k) c", p=P))
                with sp.If(layer < 1):
                    f0 = 0
                    for c, n in enumerate(FFN_TILES):
                        for w, name in enumerate(("ffn_w1", "ffn_w3")):
                            u = 3 * c + w
                            unit(2 + u // RING, u % RING, v3(ring[:, u % RING, :], 0, KT * n * P, KT),
                                 A[name][0, :, P * f0:P * (f0 + n)].rearrange("(k p) c -> p k c", p=P))
                        u = 3 * c + 2
                        unit(2 + u // RING, u % RING, v3(ring[:, u % RING, :], 0, n * D, n),
                             A["ffn_w2"][0, P * f0:P * (f0 + n), :].rearrange("(k p) c -> p k c", p=P))
                        f0 += n

            def job_loads(j, e):
                turns = [sp.snap(j * JOB_TURNS + (2 * LAYER_TURNS - 3 + t + 1)) for t in range(JOB_TURNS)]
                ex = bass.ds(e, 1)
                for u, (w, c) in enumerate(JOB_UNITS):
                    slot = ring[:, u % RING, :]
                    sp.wait_ge(slot_free[u % RING], 1)
                    sp.wait_ge(slot_free[u % RING], turns[u // RING])
                    if w == 2:
                        dst, src = v3(slot, 0, 4096, 4), A["moe_w2"][0, ex, FC * c:FC * c + FC, :]
                    else:
                        dst, src = v3(slot, 0, 4096, KT), A[f"moe_w{w}"][0, ex, :, FC * c:FC * c + FC]
                    sp.dma_start(dst, src.rearrange("e (k p) c -> p (e k) c", p=P)).then_inc(arrived[u % RING], 16)

            sp.wait_ge(S["par_free"], DEPTH + 1)
            sp.dma_start(fnorm, A["final_norm"].rearrange("(e d) -> e d", e=1).broadcast_to([P, D]))\
              .then_inc(S["loaded_fnorm"], 16)
            sp.dma_start(nffn, A["norm_ffn"][DEPTH - 1:DEPTH, :].broadcast_to([P, D])).then_inc(S["loaded_nffn"], 16)
            with sp.Fori(0, N_EXP) as j:
                job_loads(j, j)
            sp.wait_ge(S["jobs_ready"], 1)
            n_jobs = sp.value_load(tabi[0:1, 0:1], min_val=N_EXP, max_val=MAX_JOBS)
            with sp.If(n_jobs > N_EXP):
                with sp.Fori(N_EXP, n_jobs) as j:
                    e = sp.value_load(tabi[0:1, bass.ds(j - (N_EXP - 1), 1)], min_val=0, max_val=N_EXP - 1)
                    job_loads(j, e)
            for t in range(TT):
                sp.wait_ge(S["fin"], t + 1)
                sp.dma_start(out[0, P * t:P * t + P, :], xr[:, t, :]).then_inc(S["stored"], 16)
            sp.wait_ge(S["stored"], 32)

        @block.gpsimd
        def _(gp):
            link, restart = chain(gp, S["g_chain"])

            def take_wait():
                link(gp.tensor_tensor(tick[:, 0:1], tick[:, 1:2], tick[:, 1:2], ALU.add))
            link(gp.memset(tick[:, :], 0.0))
            link(gp.memset(eps[:, :], EPS))
            gp.memset(zeros[:, :], 0.0).then_inc(S["zeroed"], 1)
            gp.memset(pwbd[:, :, :], 0.0).then_inc(S["par_free"], 1)
            gp.wait_ge(S["zeroed"], 1)
            gp.wait_ge(S["bias_row"], 1)
            gp.dma_start(rev[:, :], gla[0:HEADS, 512:896]).then_inc(S["bias_rows"], 16)
            gp.wait_ge(S["bias_rows"], 16)
            for i2 in range(2):
                gp.dma_start(hank[i2][:, :, :], bass.AP(rev, 2 * i2 * 384, [[1, P], [384, 2], [1, 256]]))\
                  .then_inc(S["bias_hank"], 16)
            gp.wait_ge(S["loaded_mem"], 48)
            link(gp.tensor_copy(gmask[:, :], uvg[:, 1, :]))
            with gp.Fori(0, DEPTH) as layer:
                L1 = gp.snap(layer + 1)
                first, second = gp.snap(layer * 2 + 1), gp.snap(layer * 2 + 2)
                landed1 = gp.snap(layer * (16 * LAYER_TURNS) + 32)
                restart()
                gp.wait_ge(S["scored"], second)
                take_wait()
                gp.memset(r2[:, :], 0.0).then_inc(S["r2_zero"], 1)
                for t in (bu, pw1, pw2):
                    link(gp.memset(t[:, :, 0:PAD], 0.0))
                gp.wait_ge(S["pcol_done"], L1)
                gp.wait_ge(arrived[U_WKV], landed1)
                take_wait()
                for k in range(KT):
                    w = ring[:, U_WKV, 512 * k:512 * k + 512]
                    i = gp.tensor_scalar(w, w, pcol[:, R_MEM + k:R_MEM + k + 1], None, ALU.mult)
                i.then_inc(S["wkv_scaled"], 1)
                gp.wait_ge(g_ev["bu"], L1)
                t1 = slice(PAD, PAD + SEQ)

                def shifted(k):
                    return slice(PAD - k, PAD + SEQ - k)
                inv = v3(cc("inv"), 0, 512, 2)

                def mean_less_self(src, p0, m):
                    link(gp.tensor_tensor(src[p0:p0 + 64, m, t1], src[p0:p0 + 64, m, t1], inv[p0:p0 + 64, m, :],
                                          ALU.mult))
                    return gp.tensor_tensor(bu[p0:p0 + 64, m, t1], src[p0:p0 + 64, m, t1], bu[p0:p0 + 64, m, t1],
                                            ALU.subtract)
                link(gp.tensor_tensor(pw1[:, :, t1], bu[:, :, t1], bu[:, :, shifted(1)], ALU.add))
                link(gp.tensor_tensor(pw2[:, :, t1], pw1[:, :, t1], pw1[:, :, shifted(2)], ALU.add))
                link(mean_less_self(pw1, 0, 0))
                link(mean_less_self(pw2, 64, 0))
                link(gp.tensor_tensor(pw1[:, 1, t1], pw2[:, 1, t1], pw2[:, 1, shifted(4)], ALU.add))
                link(gp.tensor_tensor(pw2[:, 1, t1], pw1[:, 1, t1], pw1[:, 1, shifted(8)], ALU.add))
                link(mean_less_self(pw1, 0, 1))
                mean_less_self(pw2, 64, 1).then_inc(S["pool_out"], 1)
                gp.wait_ge(S["pool_out"], L1)

        @block.scalar
        def _(act):
            link, restart = chain(act, S["a_chain"])

            def root_mean(src, junk, t):
                link(act.activation(junk, src[:, t, :], ACT.Square, accum_out=ss[:, t:t + 1]))
                act.activation(rms[:, t:t + 1], ss[:, t:t + 1], ACT.Sqrt, bias=eps[:, :], scale=1.0 / D)\
                   .then_inc(S["rms_ready"], 1)

            def normed_out(layer, no, dst, g0, bank0=0):
                for b in (1, 3):
                    act.wait_ge(S["xT_ps"], count(layer, no, 4, 4 if g0 is None else b + 1))
                    for kt in (2 * b, 2 * b + 1):
                        i = act.activation(dst[:, kt, :], xT(kt, bank0), ACT.Copy,
                                           scale=1.0 if g0 is None else pcol[:, g0 + kt:g0 + kt + 1])
                i.then_inc(S["xT_a"], 1)

            act.wait_ge(S["zeroed"], 1)

            with act.Fori(0, DEPTH) as layer:
                L1 = act.snap(layer + 1)
                first, second = act.snap(layer * 2 + 1), act.snap(layer * 2 + 2)
                ended = [act.snap(layer * LAYER_TURNS + (t + 2)) for t in range(2)]

                def group(name):
                    act.wait_ge(g_ps[name], ended[ENDS[name][1]] if name in ENDS else L1)

                def norm(u, g0, between=None):
                    for t in range(TT):
                        act.wait_ge(S["h_upd"], layer * 6 + (2 * u + t + 1))
                        root_mean(h, r2[:, 0:1024], t)
                    if between is not None:
                        between()
                    normed_out(layer, norm_no(layer, u), xnT, g0)
                restart()

                def out_of(name, dst, src, func=ACT.Copy):
                    group(name)
                    act.activation(dst, src, func).then_inc(g_ev[name], 1)

                def parameters():
                    act.wait_ge(S["pcol_ps"], L1)
                    act.activation(pcol[:, :], ps[3][:, 0:N_ROWS], ACT.Copy).then_inc(S["pcol_done"], 1)
                    act.wait_ge(S["pcol_done"], L1)
                norm(0, R_MIX, parameters)
                with act.If(layer < 1):
                    act.wait_ge(S["bias_ps"], 1)
                    act.activation(gla[0:HEADS, 512:896], ps[7][0:HEADS, 0:384], ACT.Copy).then_inc(S["bias_row"], 1)
                group("ki")
                for q in range(4):
                    act.activation(kiT[32 * q:32 * q + 32, :], ps[5][0:32, 0:256], ACT.Copy)
                act.activation(wis[:, :, :], v3(ps[5], 256, 272, 2), ACT.Copy,
                               scale=float(IDX_HEADS ** -0.5 * IDX_DIM ** -0.5)).then_inc(g_ev["ki"], 1)
                with act.If(layer < 1):
                    act.wait_ge(S["loaded_mem"], 48)
                    for t in range(TT):
                        root_mean(memr, bias[:, :, :].rearrange("p h x -> p (h x)"), t)
                restart()
                act.wait_ge(S["dots_ps"], first)
                for b in range(4):
                    i = act.activation(rel[:, b:8:4, :], v3(ps[b], 0, 512, 2), ACT.Relu)
                i.then_inc(S["rel"], 1)
                with act.If(layer < 1):
                    normed_out(layer, 2, memT, None, 4)
                act.wait_ge(S["ws_ps"], L1)
                act.activation(wsT[:, :, :], v3(ps[4], 0, 512, 4), ACT.Copy).then_inc(S["ws_done"], 1)
                out_of("a", gla[:, 0:512], ps[6][:, :])
                out_of("av", av[:, :, :], v3(ps[7], 0, 512, 2))
                with act.If(layer < 1):
                    act.wait_ge(S["hank_ps"], 1)
                    for i2 in range(2):
                        i = act.activation(bias[:, 2 * i2:2 * i2 + 2, :], v3(ps[4 + i2], 0, 512, 2), ACT.Copy)
                    i.then_inc(S["bias_done"], 1)
                act.wait_ge(S["dots_ps"], second)
                act.wait_ge(S["scored"], first)
                for b in range(4):
                    i = act.activation(rel[:, b:8:4, 0:P], v3(ps[b], 0, 512, 2)[:, :, 0:P], ACT.Relu)
                i.then_inc(S["rel"], 1)
                out_of("ag", sg[:, :, :], v3(ps[5], 0, 512, 2), ACT.Silu)
                act.wait_ge(S["la_ready"], L1)
                link(act.activation(eb, la, ACT.Abs))
                link(act.activation(enb, eb, ACT.Exp, scale=-1.0))
                act.activation(eb, enb, ACT.Ln, bias=1.0).then_inc(S["ls_ready"], 1)
                act.wait_ge(S["b_ready"], L1)
                act.activation(eb, bs, ACT.Exp, scale=1.0 / 16.0)
                act.activation(enb, bs, ACT.Exp, scale=-1.0 / 16.0).then_inc(S["eb_ready"], 1)
                act.wait_ge(S["qe_ready"], L1)
                act.wait_ge(S["r2_zero"], L1)
                for q in range(4):
                    i = act.activation(qbd[32 * q:32 * q + 32, :, q, :],
                                       aqT[32 * q:32 * q + 32, :].rearrange("p (t i) -> p t i", t=2), ACT.Copy)
                i.then_inc(S["qbd_done"], 1)
                out_of("k", kT[:, :, :], v3(ps[4], 0, 512, 2))
                act.wait_ge(S["kd_ps"], L1)
                act.activation(kdr, v3(ps[2], 0, 256, 2), ACT.Copy).then_inc(S["kdr_done"], 1)
                out_of("bu", bu[:, :, PAD:PAD + SEQ], v3(ps[6], 0, 512, 2))
                out_of("uv0", uvg[:, 0, :], ps[7][:, :], ACT.Gelu_apprx_tanh)
                out_of("uv1", uvg[:, 1, :], ps[4][:, :], ACT.Gelu_apprx_tanh)
                act.wait_ge(S["vms"], L1)
                act.activation(s_vr, s_vm, ACT.Sqrt).then_inc(S["vr"], 1)
                out_of("kx", kxT[:, :, :], v3(ps[5], 0, 512, 2))
                act.wait_ge(S["o_ps"], L1)
                for t in range(TT):
                    i = act.activation(osq[:, t, :], ps[t][:, 0:256], ACT.Square)
                i.then_inc(S["osq"], 1)
                act.wait_ge(S["ms_gla"], L1)
                act.activation(s_or, s_og, ACT.Sqrt).then_inc(S["r_gla"], 1)
                for t in (1, 0):
                    act.wait_ge(S["lg"], first if t else second)
                    for hh in range(HEADS):
                        k = 4 * t + hh
                        i = act.activation(prb[t][:, hh, :], lgm[t][:, hh, :], ACT.Exp, bias=s_mx[:, k:k + 1],
                                           accum_out=s_sum[:, k:k + 1])
                    i.then_inc(S["p"], 1)
                act.wait_ge(S["pt1_ps"], L1)
                act.activation(pT_mix[1][:, 4:8, :], v3(ps[1], 0, 512, 4), ACT.Copy).then_inc(S["pt1_a"], 1)
                act.wait_ge(S["mt_ps"], L1)
                act.activation(mixT[:, 6:8, :], v3(ps[6], 0, 512, 2), ACT.Copy).then_inc(S["mt_a"], 1)

                norm(1, R_XA)
                out_of("xq", qT[:, :, :], v3(ps[4], 0, 512, 2))
                for t in range(TT):
                    act.wait_ge(S["xmx"], second if t else first)
                    for hh in range(HEADS):
                        k = 4 * t + hh
                        c0 = 256 * (hh // 2)
                        i = act.activation(prx[t][:, hh, :], ps[2 * t + hh % 2][:, c0:c0 + 256], ACT.Exp,
                                           bias=s_mx[:, k:k + 1], scale=float(DH ** -0.5), accum_out=s_sum[:, k:k + 1])
                    i.then_inc(S["xp"], 1)
                for t in range(TT):
                    act.wait_ge(S["xpt_ps"], second if t else first)
                    act.activation(pT_x[t][:, 4:8, :], v3(ps[5 + 2 * t], 0, 512, 4), ACT.Copy)\
                       .then_inc(S["xpt_a"], 1)


                def split(i):
                    w = FFN_PIECES[i][0]
                    u, begins, _, weights = ffn_piece(i)
                    if begins:
                        act.wait_ge(arrived[u % RING], 16 * (3 + u // RING))
                    act.wait_ge(S["piece_free"], i + 1)
                    act.activation(as_piece(w, ffn_buf(w_hi, i)), weights, ACT.Copy).then_inc(S["hi_ready"], 1)

                def early():
                    with act.If(layer < 1):
                        act.wait_ge(g_ps["xout"], ENDS["xout"][1] + 2)
                        for i in range(FFN_EARLY):
                            split(i)
                norm(2, R_FFN, early)
                with act.If(layer < 1):
                    act.wait_ge(S["xT_v"], 4)
                    act.wait_ge(S["xT_a"], 4)
                    for k2 in range(2):
                        act.activation(x_hi[:, 4 * k2:4 * k2 + 4, :], xnT[:, 4 * k2:4 * k2 + 4, :], ACT.Copy)\
                           .then_inc(S["f_xh"], 1)
                    act.wait_ge(S["f_x"], 2)

                    def silu(f):
                        act.wait_ge(S["f_h"], f + 1)
                        act.activation(f_sil[:, f % 2, :], ps[f % 2][:, 0:256], ACT.Silu).then_inc(S["f_s"], 1)

                    for i in range(FFN_EARLY, len(FFN_PIECES)):
                        if i >= NB and FFN_PIECES[i - NB][0] == 3:
                            silu(FFN_PIECES[i - NB][1])
                        split(i)
                    silu(FF // P - 1)

            act.wait_ge(S["top_diff"], 1)
            act.activation(s_e, s_d, ACT.Exp).then_inc(S["top_exp"], 1)
            def gather_hi(n):
                act.wait_ge(S["j_gps"], n)
                for b in range(2):
                    i = act.activation(xg_hi[:, 4 * b:4 * b + 4, :], v3(ps[2 + b], 0, 512, 4), ACT.Copy)
                i.then_inc(S["j_gh"], 1)

            def yrow_out(j, half):
                act.wait_ge(S["j_yps"], j + 1)
                act.activation(y_hi[:, half, :], ps[6 + half][:, :], ACT.Copy).then_inc(S["j_ya"], 1)

            def transposed(n):
                act.wait_ge(S["j_tps"], n)
                act.activation(at_hi[:, :, :], v3(ps[4], 0, 512, 4), ACT.Copy).then_inc(S["j_th"], 1)

            gather_hi(1)
            act.wait_ge(S["jobs_ready"], 1)
            n_jobs = act.value_load(tabi[0:1, 0:1], min_val=N_EXP, max_val=MAX_JOBS)
            with act.Fori(0, n_jobs) as j:
                cn = [act.snap(j * NCH + (c + 1)) for c in range(NCH)]
                j1, j2, pieces = act.snap(j + 1), act.snap(j + 2), act.snap(j * JOB_PIECES + len(FFN_PIECES))
                landed = [act.snap(j * (16 * JOB_TURNS) + 16 * (2 * LAYER_TURNS - 3 + t + 1)) for t in range(JOB_TURNS)]
                for i in range(JOB_PIECES):
                    if i in (NB - 1, NB):
                        yrow_out(j, i - (NB - 1))
                    for c in range(NCH):
                        if i == after((1, c)):
                            act.wait_ge(S["j_h1"], cn[c])
                            act.activation(j_sil[c % 2], ps[2 * (c % 2)][:, :], ACT.Silu).then_inc(S["j_s"], 1)
                        if c < NCH - 1 and i == after((1, c + 1)) + 1:
                            transposed(cn[c])
                    if i == JOB_PIECES - 1:
                        transposed(cn[NCH - 1])
                    u, q = i // QP, i % QP
                    if q == 0:
                        act.wait_ge(arrived[u % RING], landed[u // RING])
                    act.wait_ge(S["piece_free"], pieces + (i + 1))
                    act.activation(w_hi[:, i % NB, :], ring[:, u % RING, PIECE * q:PIECE * q + PIECE], ACT.Copy)\
                       .then_inc(S["hi_ready"], 1)
                gather_hi(j2)
            for half in range(2):
                yrow_out(n_jobs, half)
            act.wait_ge(S["j_cv"], n_jobs * 2 + 1)
            act.activation(st[:, 92:93], eps[:, :], ACT.Copy)
            restart()
            for t in range(TT):
                if t:
                    act.wait_ge(S["j_cv"], n_jobs * 2 + 2)
                root_mean(h, xr[:, t, :], t)

        @block.vector
        def _(dve):
            link, restart = chain(dve, S["v_chain"])
            mult, add, sub, amax, amin = ALU.mult, ALU.add, ALU.subtract, ALU.max, ALU.min

            def inverse_mean(dst, src, n):
                link(dve.tensor_scalar(dst, src, 1.0 / n, EPS, mult, add))
                return dve.reciprocal(dst, dst)

            def factors(layer, no):
                for t in range(TT):
                    dve.wait_ge(S["rms_ready"], count(layer, no, 2, t + 1))
                    link(dve.reciprocal(rs[:, t:t + 1], rms[:, t:t + 1]))
                    dve.tensor_scalar(diag[:, t, :], ident, rs[:, t:t + 1], None, mult)\
                       .then_inc(S["diag_ready"], 1)

            def normed_out(layer, no, dst, g0, bank0=0):
                for b in (0, 2):
                    dve.wait_ge(S["xT_ps"], count(layer, no, 4, 4 if g0 is None else b + 1))
                    for kt in (2 * b, 2 * b + 1):
                        i = dve.tensor_scalar(dst[:, kt, :], xT(kt, bank0),
                                              1.0 if g0 is None else pcol[:, g0 + kt:g0 + kt + 1], None, mult)
                i.then_inc(S["xT_v"], 1)

            def add_rows(banks, t0=0):
                for k, b in enumerate(banks):
                    dst = h[:, t0 + k // 2, 512 * (k % 2):512 * (k % 2) + 512]
                    i = dve.tensor_tensor(dst, dst, ps[b][:, :], add)
                return i

            dve.wait_ge(S["loaded_h"], 32)
            for t in range(TT):
                dve.sem_inc(S["h_upd"], 1)
            dve.wait_ge(S["loaded_cst"], 16)

            with dve.Fori(0, DEPTH) as layer:
                L1 = dve.snap(layer + 1)
                first, second = dve.snap(layer * 2 + 1), dve.snap(layer * 2 + 2)
                ended = [dve.snap(layer * LAYER_TURNS + (t + 2)) for t in range(2)]

                def group(name):
                    dve.wait_ge(g_ps[name], ended[ENDS[name][1]] if name in ENDS else L1)
                par = dve.snap(layer * 144 + 144)

                def norm(u, g0, between=None):
                    factors(layer, norm_no(layer, u))
                    if between is not None:
                        between()
                    normed_out(layer, norm_no(layer, u), xnT, g0)

                def update(u, banks, ready):
                    dve.wait_ge(S["rows0_ps"], layer * 3 + (u + 1))
                    for t in range(TT):
                        if t:
                            ready()
                        add_rows(banks[2 * t:2 * t + 2], t).then_inc(S["h_upd"], 1)
                    dve.wait_ge(S["h_upd"], 8 if u == 2 else layer * 6 + (2 * u + 4))
                restart()

                def out_of(name, dst, src):
                    group(name)
                    dve.tensor_copy(dst, src).then_inc(g_ev[name], 1)

                factors(layer, norm_no(layer, 0))
                dve.wait_ge(S["pcol_done"], L1)
                normed_out(layer, norm_no(layer, 0), xnT, R_MIX)
                dve.wait_ge(S["loaded_par"], par)
                for g in range(4):
                    i = dve.tensor_tensor(wsr[:, g, :], wsr[:, g, :], cc("tril"), mult)
                i.then_inc(S["wsm_done"], 1)
                out_of("qi", qiT, v3(ps[4], 0, 512, 2))
                with dve.If(layer < 1):
                    factors(layer, 2)
                    normed_out(layer, 2, memT, None, 4)
                restart()
                dve.wait_ge(g_ev["ki"], L1)

                def score_and_take(t, n):
                    sc = score[:, t, 0:n]
                    vis = cc("vis", 256 - n)
                    dve.wait_ge(S["rel"], first if t else second)
                    for hh in range(IDX_HEADS):
                        i = dve.scalar_tensor_tensor(sc, rel[:, hh, 0:n], wis[:, t, hh:hh + 1], vis if hh == 0 else sc,
                                                     mult, add)
                        if hh < IDX_HEADS - 1:
                            link(i)
                    link(i)
                    dve.memset(st[:, 95:96], 0.0).then_inc(S["scored"], 1)
                    for _ in range(TOPK // 8):
                        link(dve.max(m8[:, :], sc))
                        link(dve.match_replace(sc, m8[:, :], sc, MARK))
                    link(dve.tensor_scalar(sc, sc, HALF, -1.0e30, ALU.is_gt, mult))
                    link(dve.tensor_tensor(sc, sc, vis, add))

                score_and_take(1, 256)
                score_and_take(0, P)

                out_of("lr", lrT, ps[4][0:GLA_RANK, 0:256])
                group("logit")
                dve.tensor_scalar(la, ps[6][:, 0:256], pcol[:, R_BA:R_BA + 1], None, add).then_inc(S["la_ready"], 1)
                dve.wait_ge(S["ls_ready"], L1)
                link(dve.scalar_tensor_tensor(la, la, 0.0, eb, amin, sub))
                dve.tensor_tensor_scan(bs, cc("reset"), la, 0.0, mult, add).then_inc(S["b_ready"], 1)
                dve.wait_ge(S["eb_ready"], L1)
                dve.scalar_tensor_tensor(aqT, aqT, float(GLA_DK ** -0.5), eb, mult, mult).then_inc(S["qe_ready"], 1)
                link(dve.tensor_tensor(akT, akT, enb, mult))
                last = v3(eb, 0, 256, 4)[:, :, CHUNK - 1:CHUNK]
                dve.tensor_tensor(v3(kdT, 0, 256, 4), v3(akT, 0, 256, 4), last.broadcast_to([P, 4, CHUNK]), mult)\
                   .then_inc(S["kd_ready"], 1)
                out_of("q", qT[:, :, :], v3(ps[7], 0, 512, 2))
                out_of("cv", cv[:, :, :], v3(ps[5], 0, 512, 2))
                dve.wait_ge(S["att_ps"], L1)
                dve.wait_ge(S["r2_zero"], L1)
                dve.wait_ge(g_ev["ag"], L1)
                for t in range(TT):
                    link(dve.tensor_tensor(sg[:, t, :], sg[:, t, :], bc[:, 0, :], mult))
                for t in range(TT):
                    i = dve.copy_predicated(attT[:, t, :], gmask[:, :], ps[t][:, :])
                i.then_inc(S["att_done"], 1)
                for t in range(TT):
                    dve.wait_ge(g_ev[f"uv{t}"], L1)
                    link(dve.bn_stats(s_bn[:, 6 * t:6 * t + 6], uvg[:, t, 256:512]))
                    link(dve.bn_aggr(s_ag[:, 2 * t:2 * t + 2], s_bn[:, 6 * t:6 * t + 6]))
                inverse_mean(s_vm, s_ag[:, 1:4:2], 1).then_inc(S["vms"], 1)
                dve.wait_ge(S["kv_ps"], L1)
                kv = (ps[3][:, 0:256], ps[2][:, 256:512], ps[3][:, 256:512])
                for n in range(3):
                    link(dve.tensor_tensor(Sst[:, n, :], kv[n], cc("bd"), mult))
                for n in (1, 2):
                    e = CHUNK * (n + 1) - 1
                    i = dve.scalar_tensor_tensor(Sst[:, n, :], Sst[:, n - 1, :], eb[:, e:e + 1], Sst[:, n, :], mult, add)
                    if n == 1:
                        link(i)
                i.then_inc(S["s_ready"], 1)
                dve.wait_ge(S["vr"], L1)
                for t in range(TT):
                    link(dve.tensor_scalar(vn[:, t, :], vn[:, t, :], s_ag[:, 2 * t:2 * t + 1], s_vr[:, t:t + 1],
                                           sub, mult))
                    link(dve.tensor_tensor(vn[:, t, :], vn[:, t, :], bc[:, 1, :], mult))
                    i = dve.tensor_tensor(vn[:, t, :], vn[:, t, :], bc[:, 2, :], add)
                i.then_inc(S["vn_done"], 1)
                out_of("vx", vx[:, :, :], v3(ps[6], 0, 512, 2))
                dve.wait_ge(S["osq"], L1)
                link(dve.tensor_reduce(s_og, osq.rearrange("p t (h v) -> p (t h) v", h=HEADS), AX, add))
                inverse_mean(s_og, s_og, GLA_DV).then_inc(S["ms_gla"], 1)
                dve.wait_ge(S["r_gla"], L1)
                for t in range(TT):
                    i = dve.tensor_tensor(v3(sg[:, t, :], 0, 256, 4), v3(sg[:, t, :], 0, 256, 4),
                                          s_or[:, 4 * t:4 * t + 4].unsqueeze(2).broadcast_to([P, 4, GLA_DV]), mult)
                    link(i)
                for t in range(TT):
                    i = dve.tensor_tensor(sg[:, t, :], sg[:, t, :], ps[t][:, 0:256], mult)
                i.then_inc(S["og_done"], 1)
                dve.wait_ge(S["sg_ps"], L1)
                for t in range(TT):
                    for g in range(4):
                        dst = uvg[:, t, 64 * g:64 * g + 64]
                        i = dve.scalar_tensor_tensor(dst, ps[2 + t][:, 64 * g:64 * g + 64],
                                                     pcol[:, R_SB + g:R_SB + g + 1], dst, add, mult)
                i.then_inc(S["od_done"], 1)
                group("y")
                for m in range(2):
                    i = dve.tensor_scalar(mixT[:, 2 + m, :], ps[7][:, 256 * m:256 * m + 256],
                                          pcol[:, R_PB + m:R_PB + m + 1], pcol[:, R_PS + m:R_PS + m + 1], add, mult)
                i.then_inc(g_ev["y"], 1)
                dve.wait_ge(S["bias_done"], 1)
                for t, n in ((1, 256), (0, P)):
                    link(dve.tensor_tensor(lgm[t], bias[:, :, 256 - n:256],
                                           score[:, t, 0:n].unsqueeze(1).broadcast_to([P, HEADS, n]), add))
                    dve.wait_ge(S["lg_ps"], first if t else second)
                    for b in range(2):
                        bank = ps[4 + b if t else 6 + b]
                        link(dve.scalar_tensor_tensor(lgm[t][:, b:4:2, :], v3(bank, 0, 2 * n, 2), float(DH ** -0.5),
                                                      lgm[t][:, b:4:2, :], mult, add))
                    link(dve.tensor_reduce(s_mx[:, 4 * t:4 * t + 4], lgm[t], AX, amax))
                    dve.tensor_scalar(s_mx[:, 4 * t:4 * t + 4], s_mx[:, 4 * t:4 * t + 4], -1.0, None, mult)\
                       .then_inc(S["lg"], 1)
                dve.wait_ge(S["pt1_ps"], L1)
                dve.tensor_copy(pT_mix[1][:, 0:4, :], v3(ps[0], 0, 512, 4)).then_inc(S["pt1_v"], 1)
                dve.wait_ge(S["pt0_ps"], L1)
                dve.tensor_copy(pT_mix[0], v3(ps[2], 0, 512, 4)).then_inc(S["pt0_v"], 1)
                dve.wait_ge(S["p"], second)
                link(dve.reciprocal(s_rec, s_sum))
                dve.wait_ge(S["pv_ps"], L1)
                for t in range(TT):
                    i = dve.tensor_tensor(v3(oc[:, t, :], 0, 256, 4), v3(ps[3], 256 * t, 256 * t + 256, 4),
                                          s_rec[:, 4 * t:4 * t + 4].unsqueeze(2).broadcast_to([P, 4, DH]), mult)
                i.then_inc(S["oc_done"], 1)
                dve.wait_ge(S["mt_ps"], L1)
                dve.tensor_copy(mixT[:, 0:2, :], v3(ps[4], 0, 512, 2))
                dve.tensor_copy(mixT[:, 4:6, :], v3(ps[5], 0, 512, 2)).then_inc(S["mt_v"], 1)
                update(0, (0, 1, 2, 3), lambda: group("wout"))
                dve.sem_inc(S["par_free"], 1)

                norm(1, R_XA)
                for t in range(TT):
                    dve.wait_ge(S["xlg_ps"], second if t else first)
                    for b in range(2):
                        link(dve.tensor_reduce(s_mx[:, 4 * t + b:4 * t + 4:2], v3(ps[2 * t + b], 0, 512, 2), AX, amax))
                    dve.tensor_scalar(s_mx[:, 4 * t:4 * t + 4], s_mx[:, 4 * t:4 * t + 4], -float(DH ** -0.5), None, mult)\
                       .then_inc(S["xmx"], 1)
                for t in range(TT):
                    dve.wait_ge(S["xpt_ps"], second if t else first)
                    dve.tensor_copy(pT_x[t][:, 0:4, :], v3(ps[4 + 2 * t], 0, 512, 4)).then_inc(S["xpt_v"], 1)
                dve.wait_ge(S["xp"], second)
                link(dve.reciprocal(s_rec, s_sum))
                dve.wait_ge(S["xpv_ps"], L1)
                for t in range(TT):
                    i = dve.tensor_tensor(v3(oc[:, t, :], 0, 256, 4), v3(ps[2 * t], 0, 256, 4),
                                          s_rec[:, 4 * t:4 * t + 4].unsqueeze(2).broadcast_to([P, 4, DH]), mult)
                i.then_inc(S["ox_done"], 1)
                dve.wait_ge(S["xo_ps"], L1)
                dve.tensor_copy(oxT[:, :, :], v3(ps[1], 0, 512, 2)).then_inc(S["xo_done"], 1)
                update(1, (4, 5, 6, 7), lambda: group("xout"))


                def split(i):
                    w = FFN_PIECES[i][0]
                    _, _, _, weights = ffn_piece(i)
                    dve.wait_ge(S["hi_ready"], i + 1)
                    dve.tensor_tensor(as_piece(w, ffn_buf(w_lo, i)), weights, as_piece(w, ffn_buf(w_hi, i)), sub)\
                       .then_inc(S["lo_ready"], 1)

                def early():
                    with dve.If(layer < 1):
                        for i in range(FFN_EARLY):
                            split(i)
                norm(2, R_FFN, early)
                with dve.If(layer < 1):
                    dve.wait_ge(S["xT_v"], 4)
                    for k2 in range(2):
                        ks = slice(4 * k2, 4 * k2 + 4)
                        dve.wait_ge(S["f_xh"], k2 + 1)
                        dve.tensor_tensor(x_lo[:, ks, :], xnT[:, ks, :], x_hi[:, ks, :], sub).then_inc(S["f_x"], 1)

                    def hidden(f):
                        dve.wait_ge(S["f_s"], f + 1)
                        link(dve.tensor_tensor(f_sil[:, f % 2, :], f_sil[:, f % 2, :], ps[f % 2][:, 256:512], mult))
                        link(dve.tensor_copy(fa_hi[:, f % 2, :], f_sil[:, f % 2, :]))
                        dve.tensor_tensor(fa_lo[:, f % 2, :], f_sil[:, f % 2, :], fa_hi[:, f % 2, :], sub)                           .then_inc(S["f_a"], 1)

                    for i in range(FFN_EARLY, len(FFN_PIECES)):
                        if i >= NB and FFN_PIECES[i - NB][0] == 3:
                            hidden(FFN_PIECES[i - NB][1])
                        split(i)
                    hidden(FF // P - 1)
                    update(2, (4, 5, 6, 7), lambda: dve.wait_ge(S["f_y"], 1))

            def slots_of(dst, j):
                for t in range(TT):
                    i = dve.tensor_scalar(dst[:, t, :], cc("iota"), jobt[:, t, 0, bass.ds(j, 1)], None, ALU.is_equal)
                return i

            def gather_lo(n):
                dve.wait_ge(S["j_gh"], n)
                for b in range(2):
                    i = dve.tensor_tensor(xg_lo[:, 4 * b:4 * b + 4, :], v3(ps[2 + b], 0, 512, 4),
                                          xg_hi[:, 4 * b:4 * b + 4, :], sub)
                i.then_inc(S["j_gl"], 1)

            def yrow_out(j, half):
                dve.wait_ge(S["j_ya"], j * 2 + (half + 1))
                dve.tensor_tensor(y_lo[half][:, :], ps[6 + half][:, :], y_hi[:, half, :], sub).then_inc(S["j_yv"], 1)

            def transposed(n):
                dve.wait_ge(S["j_th"], n)
                dve.tensor_tensor(at_lo[:, :, :], v3(ps[4], 0, 512, 4), at_hi[:, :, :], sub).then_inc(S["j_t"], 1)

            def combined(j, t):
                dve.wait_ge(S["j_c1"], j * 2 + (t + 1))
                for half in range(2):
                    dst = h[:, t, 512 * half:512 * half + 512]
                    i = dve.scalar_tensor_tensor(dst, ps[4 + 2 * t + half][:, :], j_gate[:, t:t + 1], dst, mult, add)
                i.then_inc(S["j_cv"], 1)

            restart()
            scf = score[:, :, :].rearrange("p a b -> p (a b)")

            def r3(i):
                return v3(scf, 16 * i, 16 * i + 16, 2)
            lg, eq, k1, lg2, k2, sel, gate, pos, tmp = (r3(i) for i in range(9))
            best = [scf[:, 160 + 2 * i:162 + 2 * i] for i in range(4)]

            def rep(v):
                return v.unsqueeze(2).broadcast_to([P, TT, N_EXP])

            def per_tile(v):
                return v.unsqueeze(1).broadcast_to([P, TT, N_EXP])
            dve.wait_ge(S["loaded_nffn"], 16)
            for t in range(TT):
                dve.scalar_tensor_tensor(xr[:, t, :], h[:, t, :], rs[:, t:t + 1], nffn, mult, mult)
            dve.wait_ge(S["rlog_ps"], 1)
            link(dve.tensor_copy(lg, v3(ps[4], 0, 16, 2)))

            def first_best(src, top, first, hot1):
                link(dve.tensor_reduce(top, src, AX, amax))
                link(dve.tensor_tensor(eq, src, rep(top), ALU.is_equal))
                link(dve.tensor_tensor(eq, eq, per_tile(cc("erev")), mult))
                link(dve.tensor_reduce(first, eq, AX, amax))
                link(dve.tensor_tensor(hot1, eq, rep(first), ALU.is_equal))
            first_best(lg, best[0], best[1], k1)
            link(dve.scalar_tensor_tensor(lg2, k1, NEG, lg, mult, add))
            first_best(lg2, best[2], best[3], k2)
            dve.tensor_tensor(s_d, best[2], best[0], sub).then_inc(S["top_diff"], 1)
            dve.tensor_tensor(sel, k1, k2, add).then_inc(S["sel_ready"], 1)
            dve.wait_ge(S["top_exp"], 1)
            link(dve.tensor_scalar(s_g[:, 0:2], s_e, 1.0, None, add))
            link(dve.reciprocal(s_g[:, 0:2], s_g[:, 0:2]))
            link(dve.tensor_tensor(s_g[:, 2:4], s_e, s_g[:, 0:2], mult))
            link(dve.tensor_tensor(k1, k1, rep(s_g[:, 0:2]), mult))
            link(dve.tensor_tensor(k2, k2, rep(s_g[:, 2:4]), mult))
            link(dve.tensor_tensor(gate, k1, k2, add))
            dve.wait_ge(S["sel_ready"], 1)
            dve.wait_ge(S["rank_ps"], 1)
            link(dve.scalar_tensor_tensor(pos, sel, 1000.0, v3(ps[5], 0, 16, 2), mult, add))
            link(dve.tensor_scalar(pos, pos, 1000.0, None, sub))
            link(dve.memset(jobt[:, :, 0, MAX_JOBS:], -1.0))
            link(dve.memset(jobt[:, :, 1, MAX_JOBS:], 0.0))
            link(dve.tensor_copy(jobt[:, :, 0, 0:N_EXP], pos))
            link(dve.tensor_copy(jobt[:, :, 1, 0:N_EXP], gate))
            slots_of(hot, 0).then_inc(S["j_g"], 1)
            over, upto, pick, one = (scf[:, 192 + 8 * i:200 + 8 * i] for i in range(4))
            cnt = scf[:, 224:230]
            link(dve.tensor_scalar(over, ps[5][:, 16:24], float(P), None, ALU.is_gt))
            link(dve.tensor_tensor_scan(upto, cc("ones", 0, 8), over, 0.0, mult, add))
            for x in range(MAX_JOBS - N_EXP):
                link(dve.scalar_tensor_tensor(pick, upto, float(x + 1), over, ALU.is_equal, mult))
                for k, src in ((0, pos), (1, gate)):
                    link(dve.tensor_tensor(tmp, src, per_tile(pick), mult))
                    link(dve.tensor_reduce(cnt[:, 0:2], tmp, AX, add))
                    link(dve.tensor_scalar(jobt[:, :, k, N_EXP + x:N_EXP + x + 1], cnt[:, 0:2].unsqueeze(2),
                                           float(-P if k == 0 else 0), None, add))
                link(dve.tensor_tensor(one, pick, cc("eidx"), mult))
                link(dve.tensor_reduce(cnt[:, 3 + x:4 + x], one, AX, add))
            link(dve.tensor_scalar(cnt[:, 2:3], upto[:, 7:8], float(N_EXP), None, add))
            dve.tensor_copy(tabi[0:1, 0:4], cnt[0:1, 2:6]).then_inc(S["jobs_ready"], 1)
            gather_lo(1)
            dve.wait_ge(S["jobs_ready"], 1)
            n_jobs = dve.value_load(tabi[0:1, 0:1], min_val=N_EXP, max_val=MAX_JOBS)

            link(dve.memset(j_gate, 0.0))
            dve.tensor_copy(hotT[:, :, :], v3(zeros, 0, 256, 2)).then_inc(S["j_gt"], 1)
            with dve.Fori(0, n_jobs) as j:
                cn = [dve.snap(j * NCH + (c + 1)) for c in range(NCH)]
                j1, j2, pieces = dve.snap(j + 1), dve.snap(j + 2), dve.snap(j * JOB_PIECES + len(FFN_PIECES))
                for i in range(JOB_PIECES):
                    if i in (NB - 1, NB):
                        yrow_out(j, i - (NB - 1))
                    for c in range(NCH):
                        if i == after((3, c)):
                            dve.wait_ge(S["j_s"], cn[c])
                            dve.wait_ge(S["j_h3"], cn[c])
                            dve.tensor_tensor(j_act, j_sil[c % 2], ps[2 * (c % 2) + 1][:, :], mult).then_inc(S["j_a"], 1)
                        if c < NCH - 1 and i == after((1, c + 1)) + 1:
                            transposed(cn[c])
                    for t in range(TT):
                        if i == after((3, 0)) + t:
                            combined(j, t)
                    if i == after((3, 0)) + TT:
                        dve.wait_ge(S["j_cv"], j * 2 + 2)
                        dve.tensor_copy(j_gate.unsqueeze(2), jobt[:, :, 1, bass.ds(j, 1)])
                        slots_of(hot_now, j)
                    if i == after((3, 0)) + TT + 1:
                        slots_of(hot, j1).then_inc(S["j_g"], 1)
                    if i == JOB_PIECES - 1:
                        transposed(cn[NCH - 1])
                    u, q = i // QP, i % QP
                    dve.wait_ge(S["hi_ready"], pieces + (i + 1))
                    dve.tensor_tensor(w_lo[:, i % NB, :], ring[:, u % RING, PIECE * q:PIECE * q + PIECE],
                                      w_hi[:, i % NB, :], sub).then_inc(S["lo_ready"], 1)
                gather_lo(j2)
                dve.wait_ge(S["j_gtps"], j1)
                dve.tensor_copy(hotT[:, :, :], v3(ps[5], 0, 256, 2)).then_inc(S["j_gt"], 1)
            for half in range(2):
                yrow_out(n_jobs, half)
            for t in range(TT):
                combined(n_jobs, t)
            dve.wait_ge(S["j_cv"], n_jobs * 2 + 2)
            dve.memset(st[:, 95:96], 0.0)

            restart()
            dve.wait_ge(S["loaded_fnorm"], 16)
            for t in range(TT):
                dve.wait_ge(S["rms_ready"], 14 + t + 1)
                link(dve.reciprocal(rs[:, t:t + 1], rms[:, t:t + 1]))
                dve.scalar_tensor_tensor(xr[:, t, :], h[:, t, :], rs[:, t:t + 1], fnorm, mult, mult)\
                   .then_inc(S["fin"], 1)

        @block.tensor
        def _(pe):
            mm = pe.matmul

            def transposes(layer, no, src, bank0=0):
                for t in range(TT):
                    pe.wait_ge(S["diag_ready"], count(layer, no, 2, t + 1))
                    for kt in range(KT):
                        if not isinstance(no, int) and t == 0 and kt == KT - 2:
                            pe.wait_ge(S["pcol_done"], layer + 1)
                        i = mm(xT(kt, bank0)[:, P * t:P * t + P], src[:, t, P * kt:P * kt + P], diag[:, t, :],
                               start=True, stop=True)
                        if t and kt % 2:
                            i.then_inc(S["xT_ps"], 1)
                pe.wait_ge(S["xT_v"], count(layer, no, 1, 1))
                pe.wait_ge(S["xT_a"], count(layer, no, 1, 1))

            def on_features(dst, w, src=xnT):
                for k in range(KT):
                    i = mm(dst, w[:, k, :], src[:, k, :], start=k == 0, stop=k == KT - 1)
                return i

            def on_tokens(dst, w, t, src=xnT):
                for k in range(KT):
                    i = mm(dst, src[:, k, P * t:P * t + P], w[:, k, :], start=k == 0, stop=k == KT - 1)
                return i

            pe.wait_ge(S["loaded_cst"], 16)
            pe.wait_ge(S["loaded_h"], 32)
            for s in range(RING):
                pe.sem_inc(slot_free[s], 1)
            for _ in range(NB - 1):
                pe.sem_inc(S["piece_free"], 1)

            def split_products(i, steps, ends, rows0=False):
                n = 0
                for dst, xh, xl, wh, wl, opens, closes in steps:
                    for x, y in ((xh, wh), (xl, wh), (xh, wl)):
                        ins = mm(dst, x, y, start=opens and n % 3 == 0, stop=closes and n % 3 == 2)
                        if n == 0:
                            ins.then_inc(S["piece_free"], 1)
                        elif n == 1 and ends is not None:
                            ins.then_inc(slot_free[ends], 1)
                        elif n == 5 and rows0:
                            ins.then_inc(S["rows0_ps"], 1)
                        n += 1
                return ins
            with pe.Fori(0, DEPTH) as layer:
                L1 = pe.snap(layer + 1)
                first, second = pe.snap(layer * 2 + 1), pe.snap(layer * 2 + 2)
                prow_in, par = pe.snap(layer * 128 + 128), pe.snap(layer * 144 + 144)
                landed = [pe.snap(layer * (16 * LAYER_TURNS) + 16 * (t + 1)) for t in range(LAYER_TURNS)]

                def w_in(u):
                    lo, hi = IN_UNITS[u]
                    return v3(ring[:, u, :], 0, KT * (hi - lo), KT)

                pe.wait_ge(S["loaded_prow"], prow_in)
                mm(ps[3][:, 64:65], ident, ident[:, 0:1], start=True, stop=True)
                pe.transpose(ps[3][:, 0:N_ROWS], prow[:, :], ident[0:N_ROWS, 0:N_ROWS]).then_inc(S["pcol_ps"], 1)
                transposes(layer, norm_no(layer, 0), h)
                pe.wait_ge(S["loaded_par"], par)
                with pe.If(layer < 1):
                    pe.wait_ge(S["loaded_const"], 48)
                    mm(ps[7][0:HEADS, 0:384], kdec[0:BUCKETS, 0:HEADS], gla[0:BUCKETS, 0:384], start=True, stop=True)\
                        .then_inc(S["bias_ps"], 1)

                pe.wait_ge(arrived[U_QI], landed[0])
                w = w_in(U_QI)
                for m in range(2):
                    i = on_features(ps[4][:, 256 * m:256 * m + 256], w[:, :, P * m:P * m + P])
                i.then_inc(g_ps["qi"], 1)
                on_features(ps[5][0:32, 0:256], w[:, :, 256:288])
                for t in range(TT):
                    i = on_tokens(ps[5][:, 256 + 8 * t:264 + 8 * t], w[:, :, 288:296], t)
                i.then_inc(g_ps["ki"], 1)

                def dots(t, n):
                    for hh in range(IDX_HEADS):
                        r0 = 32 * (hh % 4)
                        c0 = 256 * (hh // 4)
                        i = mm(ps[hh % 4][:, c0:c0 + n], qiT[r0:r0 + 32, hh // 4, P * t:P * t + P],
                               kiT[r0:r0 + 32, 0:n], start=True, stop=True, tile_position=(r0, 0))
                    return i
                pe.wait_ge(g_ev["qi"], L1)
                pe.wait_ge(g_ev["ki"], L1)
                dots(1, 256).then_inc(S["dots_ps"], 1)
                with pe.If(layer < 1):
                    pe.wait_ge(S["bias_row"], 1)
                    transposes(layer, 2, memr, 4)
                pe.wait_ge(S["wsm_done"], L1)
                for g in range(4):
                    i = pe.transpose(ps[4][:, P * g:P * g + P], wsr[:, g, :], ident)
                i.then_inc(S["ws_ps"], 1)

                pe.wait_ge(arrived[U_A], landed[0])
                w = w_in(U_A)
                for m in range(2):
                    i = on_features(ps[6][:, 256 * m:256 * m + 256], w[:, :, P * m:P * m + P])
                i.then_inc(g_ps["a"], 1)
                for t in range(TT):
                    i = on_tokens(ps[7][:, 256 * t:256 * t + 256], w[:, :, 256:512], t)
                i.then_inc(g_ps["av"], 1)
                with pe.If(layer < 1):
                    pe.wait_ge(S["bias_hank"], 32)
                    pe.wait_ge(S["ws_done"], 1)
                    for i2 in range(2):
                        i = mm(ps[4 + i2][:, :], glab[:, 0:P], hank[i2][:, :, :], start=True, stop=True)
                    i.then_inc(S["hank_ps"], 1)
                pe.wait_ge(S["rel"], first)
                dots(0, P).then_inc(S["dots_ps"], 1)
                pe.wait_ge(arrived[U_AG], landed[0])
                pe.wait_ge(S["ws_done"], L1)
                pe.wait_ge(S["bias_done"], 1)
                w = w_in(U_AG)
                on_features(ps[4][0:GLA_RANK, 0:256], w[:, :, 256:272]).then_inc(g_ps["lr"], 1)
                for t in range(TT):
                    i = on_tokens(ps[5][:, 256 * t:256 * t + 256], w[:, :, 0:256], t)
                i.then_inc(g_ps["ag"], 1)
                pe.wait_ge(g_ev["a"], L1)
                pe.wait_ge(g_ev["lr"], L1)
                mm(ps[6][:, 0:256], wa2[:, :], lrT, start=True, stop=True).then_inc(g_ps["logit"], 1)

                pe.wait_ge(arrived[U_CQ], landed[0])
                pe.wait_ge(g_ev["av"], L1)
                w = w_in(U_CQ)
                for m in range(2):
                    i = on_features(ps[7][:, 256 * m:256 * m + 256], w[:, :, P * m:P * m + P])
                i.then_inc(g_ps["q"], 1)
                for m in range(2):
                    i = on_features(ps[4][:, 256 * m:256 * m + 256], w[:, :, 256 + P * m:384 + P * m])
                i.then_inc(g_ps["k"], 1)
                pe.wait_ge(arrived[U_CV], landed[0])
                pe.wait_ge(g_ev["ag"], L1)
                for t in range(TT):
                    i = on_tokens(ps[5][:, 256 * t:256 * t + 256], w_in(U_CV), t)
                i.then_inc(g_ps["cv"], 1)

                pe.wait_ge(S["qbd_done"], L1)
                pe.wait_ge(S["kd_ready"], L1)
                pe.wait_ge(S["rel"], second)
                for t in range(TT):
                    i = mm(ps[t][:, :], akT[:, P * t:P * t + P], qbd[:, t, :, :], start=True, stop=True)
                i.then_inc(S["att_ps"], 1)
                for t in range(TT):
                    i = pe.transpose(ps[2][:, P * t:P * t + P], kdT[:, P * t:P * t + P], ident)
                i.then_inc(S["kd_ps"], 1)

                pe.wait_ge(arrived[U_BU], landed[0])
                pe.wait_ge(S["la_ready"], L1)
                w = w_in(U_BU)
                for m in range(2):
                    i = on_features(ps[6][:, 256 * m:256 * m + 256], w[:, :, P * m:P * m + P])
                i.then_inc(g_ps["bu"], 1)
                pe.wait_ge(arrived[U_UV], landed[0])
                pe.wait_ge(g_ev["q"], L1)
                on_tokens(ps[7][:, :], w_in(U_UV), 0).then_inc(g_ps["uv0"], 1)
                pe.wait_ge(g_ev["k"], L1)
                on_tokens(ps[4][:, :], w_in(U_UV), 1).then_inc(g_ps["uv1"], 1)

                pe.wait_ge(S["kdr_done"], L1)
                mm(ps[3][:, 0:256], kdr[0:64, 0, :], av[0:64, 0, :], start=True, stop=True)
                mm(ps[3][:, 256:512], kdr[0:64, 1, :], av[0:64, 1, :], start=True, stop=True)
                mm(ps[2][:, 256:512], kdr[64:128, 0, :], av[64:128, 0, :], start=True, stop=True)\
                    .then_inc(S["kv_ps"], 1)

                pe.wait_ge(arrived[U_WKV], landed[1])
                pe.wait_ge(g_ev["cv"], L1)
                pe.wait_ge(g_ev["bu"], L1)
                pe.wait_ge(S["wkv_scaled"], L1)
                w = v3(ring[:, U_WKV, :], 0, 4096, KT)
                for m in range(2):
                    i = on_features(ps[5][:, 256 * m:256 * m + 256], w[:, :, P * m:P * m + P], memT)
                i.then_inc(g_ps["kx"], 1)
                for t in range(2):
                    i = on_tokens(ps[6][:, 256 * t:256 * t + 256], w[:, :, 256:512], t, memT)
                i.then_inc(g_ps["vx"], 1)

                pe.wait_ge(S["att_done"], L1)
                pe.wait_ge(S["zeroed"], 1)
                pe.wait_ge(S["s_ready"], L1)
                for t in range(TT):
                    for half in range(2):
                        n = 2 * t + half
                        state = zeros[:, :] if n == 0 else Sst[:, n - 1, :]
                        mm(ps[t][64 * half:64 * half + 64, 0:256], aqT[:, CHUNK * n:CHUNK * n + CHUNK], state,
                           start=True, stop=False, skip_group_check=True)
                    for hh in range(HEADS):
                        i = mm(ps[t][:, 64 * hh:64 * hh + 64], attT[:, t, P * hh:P * hh + P],
                               av[:, t, 64 * hh:64 * hh + 64], start=False, stop=True, skip_group_check=True)
                i.then_inc(S["o_ps"], 1)

                pe.wait_ge(S["vn_done"], L1)
                for t in range(TT):
                    for g in range(4):
                        i = mm(ps[2 + t][:, 64 * g:64 * g + 64], wsT[:, g, :], vn[:, t, 64 * g:64 * g + 64],
                               start=True, stop=True)
                i.then_inc(S["sg_ps"], 1)

                pe.wait_ge(S["pool_out"], L1)
                pe.wait_ge(g_ev["uv0"], L1)
                for m in range(2):
                    i = mm(ps[7][:, 256 * m:256 * m + 256], pwbd[:, m, :], bu[:, m, PAD:PAD + SEQ], start=True, stop=True)
                i.then_inc(g_ps["y"], 1)

                def attend(t, n, keys, banks, name):
                    for hh in range(HEADS):
                        r0 = 64 * (hh % 2)
                        c0 = n * (hh // 2)
                        i = mm(ps[banks + hh % 2][:, c0:c0 + n], qT[r0:r0 + 64, hh // 2, P * t:P * t + P],
                               keys[r0:r0 + 64, hh // 2, 0:n], start=True, stop=True)
                    i.then_inc(S[name], 1)

                def values(dst, pT, vals, t, tiles):
                    for hh in range(HEADS):
                        for k in range(tiles):
                            i = mm(dst[:, 64 * hh:64 * hh + 64], pT[:, tiles * hh + k, :],
                                   vals[:, k, 64 * hh:64 * hh + 64], start=k == 0, stop=k == tiles - 1)
                    return i

                pe.wait_ge(g_ev["uv1"], L1)
                pe.wait_ge(g_ev["kx"], L1)
                attend(1, 256, kT, 4, "lg_ps")
                pe.wait_ge(g_ev["vx"], L1)
                pe.wait_ge(g_ev["y"], L1)
                attend(0, P, kT, 6, "lg_ps")
                pe.wait_ge(S["og_done"], L1)
                pe.wait_ge(S["p"], first)
                for hh in range(HEADS):
                    for k in range(2):
                        x = 2 * hh + k
                        i = pe.transpose(ps[x // 4][:, P * (x % 4):P * (x % 4) + P],
                                         prb[1][:, hh, P * k:P * k + P], ident)
                i.then_inc(S["pt1_ps"], 1)
                pe.wait_ge(S["od_done"], L1)
                pe.wait_ge(S["p"], second)
                for hh in range(HEADS):
                    i = pe.transpose(ps[2][:, P * hh:P * hh + P], prb[0][:, hh, :], ident)
                i.then_inc(S["pt0_ps"], 1)

                def transpose_rows(bank, src):
                    for k in range(2):
                        for t in range(TT):
                            c0 = 256 * k + P * t
                            i = pe.transpose(ps[bank][:, c0:c0 + P], src[:, t, P * k:P * k + P], ident)
                    return i
                pe.wait_ge(S["lg"], second)
                transpose_rows(4, sg)
                transpose_rows(6, uvg)
                pe.wait_ge(S["pt1_v"], L1)
                pe.wait_ge(S["pt1_a"], L1)
                values(ps[3][:, 256:512], pT_mix[1], cv, 1, 2)
                pe.wait_ge(S["pt0_v"], L1)
                values(ps[3][:, 0:256], pT_mix[0], cv, 0, 1).then_inc(S["pv_ps"], 1)
                pe.wait_ge(S["oc_done"], L1)
                transpose_rows(5, oc).then_inc(S["mt_ps"], 1)

                pe.wait_ge(S["mt_v"], L1)
                pe.wait_ge(S["mt_a"], L1)
                for i4, m in enumerate(WOUT_ORDER):
                    s = U_WOUT + i4
                    pe.wait_ge(arrived[s], landed[1])
                    w = v3(ring[:, s, :], 0, 2048, 2)
                    for t in range(TT):
                        for k in range(2):
                            for half in range(2):
                                i = mm(ps[2 * t + half][:, :], mixT[:, 2 * m + k, P * t:P * t + P],
                                       w[:, k, 512 * half:512 * half + 512],
                                       start=i4 == 0 and k == 0, stop=i4 == 3 and k == 1)
                        if i4 == 3 and t == 0:
                            i.then_inc(S["rows0_ps"], 1)
                    i.then_inc(slot_free[s], 1)

                transposes(layer, norm_no(layer, 1), h)
                pe.wait_ge(arrived[U_WQ], landed[1])
                w = v3(ring[:, U_WQ, :], 0, 2048, KT)
                for m in range(2):
                    i = on_features(ps[4][:, 256 * m:256 * m + 256], w[:, :, P * m:P * m + P])
                i.then_inc(g_ps["xq"], 1)
                pe.wait_ge(g_ev["xq"], L1)
                for t in range(TT):
                    attend(t, MEM, kxT, 2 * t, "xlg_ps")
                for t in range(TT):
                    pe.wait_ge(S["xp"], second if t else first)
                    for x in range(8):
                        i = pe.transpose(ps[4 + 2 * t + x // 4][:, P * (x % 4):P * (x % 4) + P],
                                         prx[t][:, x // 2, P * (x % 2):P * (x % 2) + P], ident)
                    i.then_inc(S["xpt_ps"], 1)
                for t in range(TT):
                    pe.wait_ge(S["xpt_v"], second if t else first)
                    pe.wait_ge(S["xpt_a"], second if t else first)
                    i = values(ps[2 * t][:, 0:256], pT_x[t], vx, t, 2)
                i.then_inc(S["xpv_ps"], 1)
                pe.wait_ge(S["ox_done"], L1)
                transpose_rows(1, oc).then_inc(S["xo_ps"], 1)
                pe.wait_ge(S["xo_done"], L1)
                pe.wait_ge(arrived[U_WO], landed[1])
                w = v3(ring[:, U_WO, :], 0, 2048, 2)
                for t in range(TT):
                    for half in range(2):
                        for k in range(2):
                            i = mm(ps[4 + 2 * t + half][:, :], oxT[:, k, P * t:P * t + P],
                                   w[:, k, 512 * half:512 * half + 512], start=k == 0, stop=k == 1)
                    if t == 0:
                        i.then_inc(S["rows0_ps"], 1)
                i.then_inc(g_ps["xout"], 1)

                transposes(layer, norm_no(layer, 2), h)
                with pe.If(layer < 1):
                    for i, (w, f) in enumerate(FFN_PIECES):
                        u, _, ends, _ = ffn_piece(i)
                        if w == 2:
                            pe.wait_ge(S["f_a"], f + 1)
                        pe.wait_ge(S["lo_ready"], i + 1)
                        wh, wl = as_piece(w, ffn_buf(w_hi, i)), as_piece(w, ffn_buf(w_lo, i))
                        steps = []
                        if w == 2:
                            for q in range(4):
                                tok, col = slice(P * (q // 2), P * (q // 2) + P), slice(512 * (q % 2), 512 * (q % 2) + 512)
                                steps.append((ps[4 + q][:, :], fa_hi[:, f % 2, tok], fa_lo[:, f % 2, tok],
                                              wh[:, col], wl[:, col], f == 0, f == FF // P - 1))
                        else:
                            dst = ps[f % 2][:, 0:256] if w == 1 else ps[f % 2][:, 256:512]
                            for k in range(KT):
                                steps.append((dst, wh[:, k, :], wl[:, k, :], x_hi[:, k, :], x_lo[:, k, :],
                                              k == 0, k == KT - 1))
                        if i == 0:
                            pe.wait_ge(S["f_x"], 2)
                        ins = split_products(i, steps, u % RING if ends else None, (w, f) == FFN_PIECES[-1])
                        if w == 3:
                            ins.then_inc(S["f_h"], 1)
                    ins.then_inc(S["f_y"], 1)

            for t in range(TT):
                i = on_tokens(ps[4][:, 8 * t:8 * t + 8], routw, t)
            i.then_inc(S["rlog_ps"], 1)
            pe.wait_ge(S["sel_ready"], 1)
            sel = score[:, :, :].rearrange("p a b -> p (a b)")[:, 80:96]
            before_, ones = cc("before"), cc("ones")
            mm(ps[5][:, 0:8], before_, sel[:, 0:8], start=True, stop=True)
            mm(ps[5][:, 8:16], before_, sel[:, 8:16], start=True, stop=False)
            mm(ps[5][:, 8:16], ones, sel[:, 0:8], start=False, stop=True)
            mm(ps[5][:, 16:24], ones, sel[:, 0:8], start=True, stop=False)
            mm(ps[5][:, 16:24], ones, sel[:, 8:16], start=False, stop=True).then_inc(S["rank_ps"], 1)
            def gather(n):
                pe.wait_ge(S["j_g"], n)
                for kt in range(KT):
                    for t in range(TT):
                        i = mm(ps[2 + kt // 4][:, P * (kt % 4):P * (kt % 4) + P], xr[:, t, P * kt:P * kt + P],
                               hot[:, t, :], start=t == 0, stop=t == TT - 1)
                i.then_inc(S["j_gps"], 1)

            gather(1)
            for half in range(2):
                for q in range(2):
                    i = mm(ps[6 + half][:, 256 * q:256 * q + 256], zeros[:, 0:P], zeros[:, :], start=True, stop=True)
            i.then_inc(S["j_yps"], 1)

            def combine(j):
                pe.wait_ge(S["j_gt"], j + 1)
                pe.wait_ge(S["j_yv"], j * 2 + 2)
                for t in range(TT):
                    for half in range(2):
                        mm(ps[4 + 2 * t + half][:, :], hotT[:, t, :], y_hi[:, half, :], start=True, stop=False)
                        i = mm(ps[4 + 2 * t + half][:, :], hotT[:, t, :], y_lo[half][:, :], start=False, stop=True)
                    i.then_inc(S["j_c1"], 1)

            pe.wait_ge(S["jobs_ready"], 1)
            n_jobs = pe.value_load(tabi[0:1, 0:1], min_val=N_EXP, max_val=MAX_JOBS)
            with pe.Fori(0, n_jobs) as j:
                cn = [pe.snap(j * NCH + (c + 1)) for c in range(NCH)]
                j1, j2, pieces = pe.snap(j + 1), pe.snap(j + 2), pe.snap(j * JOB_PIECES + len(FFN_PIECES))

                def products(w, c):
                    u = UNIT_OF[w, c]
                    for q in range(QP):
                        i = QP * u + q
                        pe.wait_ge(S["lo_ready"], pieces + (i + 1))
                        hi, lo = w_hi[:, i % NB, :], w_lo[:, i % NB, :]
                        steps = []
                        for part in range(2):
                            if w == 2:
                                dst, xh, xl = ps[6 + part], at_hi[:, q, :], at_lo[:, q, :]
                                opens, closes = c == 0 and q == 0, c == NCH - 1 and q == QP - 1
                            else:
                                k = 2 * q + part
                                dst, xh, xl = ps[2 * (c % 2) + (w == 3)], xg_hi[:, k, :], xg_lo[:, k, :]
                                opens, closes = k == 0, k == KT - 1
                            cols = slice(FC * part, FC * part + FC)
                            steps.append((dst[:, :], xh, xl, hi[:, cols], lo[:, cols], opens, closes))
                        ins = split_products(i, steps, u % RING if q == QP - 1 else None)
                    return ins

                def transpose_act(c):
                    pe.wait_ge(S["j_a"], cn[c])
                    for f in range(4):
                        i = pe.transpose(ps[4][:, P * f:P * f + P], j_act[:, P * f:P * f + P], ident)
                    i.then_inc(S["j_tps"], 1)

                pe.wait_ge(S["j_gl"], j1)
                products(1, 0).then_inc(S["j_h1"], 1)
                products(3, 0).then_inc(S["j_h3"], 1)
                combine(j)
                for c in range(1, NCH):
                    products(1, c).then_inc(S["j_h1"], 1)
                    if c == 1:
                        pe.wait_ge(S["j_cv"], j * 2 + 1)
                    transpose_act(c - 1)
                    products(3, c).then_inc(S["j_h3"], 1)
                    pe.wait_ge(S["j_t"], cn[c - 1])
                    if c == 1:
                        pe.wait_ge(S["j_cv"], j * 2 + 2)
                    products(2, c - 1)
                transpose_act(NCH - 1)
                for t in range(TT):
                    i = pe.transpose(ps[5][:, P * t:P * t + P], hot_now[:, t, :], ident)
                i.then_inc(S["j_gtps"], 1)
                gather(j2)
                pe.wait_ge(S["j_t"], cn[NCH - 1])
                products(2, NCH - 1).then_inc(S["j_yps"], 1)
            combine(n_jobs)


INPUTS = ("x", "mem", "rel_bias", "final_norm", "norm_mix", "w_in", "gla_wa2", "gla_ba", "gla_norm", "pool_w", "pool_b",
          "pool_scale", "sgu_ln_g", "sgu_ln_b", "sgu_w", "sgu_b", "w_out", "norm_xa", "norm_mem", "xa_wq", "xa_wkv",
          "xa_wo", "norm_ffn", "ffn_w1", "ffn_w3", "ffn_w2", "router", "moe_w1", "moe_w3", "moe_w2")


def kernel(**inputs):
    import numpy as _np
    import concourse.bacc as _bacc
    from concourse import mybir as _mybir
    from concourse.bass_utils import run_bass_kernel_spmd as _run

    nc = _bacc.Bacc("TRN2", target_bir_lowering=False, num_devices=1)
    arrays = {name: _np.ascontiguousarray(inputs[name]) for name in INPUTS}
    for name, value in zip(("consts", "glam", "onehot", "flip"), shape_constants()):
        arrays[name] = value
    aps = {name: nc.dram_tensor(f"in_{name}", a.shape, _mybir.dt.from_np(a.dtype), kind="ExternalInput").ap()
           for name, a in arrays.items()}
    out = nc.dram_tensor("out", arrays["x"].shape, _mybir.dt.from_np(arrays["x"].dtype), kind="ExternalOutput").ap()
    build(nc, aps, out)
    r = _run(nc, [{f"in_{name}": a for name, a in arrays.items()}], core_ids=[0])
    return r.results[0]["out"]
```
